# Optimizing a Trainium2 kernel written in Bass

```python
import math
import jax, jax.numpy as jnp
from jax import lax
import numpy as np

D_MODEL = 1024
BATCH = 1
SEQ = 128
DEPTH = 2
DEC_BATCH = 1
DEC_SEQ = 512
PAST_LEN = 128

GRID_W = 64
HY_W = D_MODEL // 2
HY_BANDS = 16
HY_FEAT = 1 + 2 * HY_BANDS
HY_HIDDEN = 64
SHORT_CONV = 3
SSM_W = D_MODEL // 2
SSM_HEAD_DIM = 64
SSM_HEADS = SSM_W // SSM_HEAD_DIM
SSM_GROUPS = 2
SSM_STATE = 64
SSM_CHUNK = 128
XBC_W = SSM_W + 2 * SSM_GROUPS * SSM_STATE
N_HEADS = 8
KV_HEADS = 2
HEAD_DIM = 64
Q_PER_KV = N_HEADS // KV_HEADS
ATT_W = N_HEADS * HEAD_DIM
KV_W = KV_HEADS * HEAD_DIM
WINDOW = 128
ATT_BLOCK = 128
BAND = ATT_BLOCK + 2 * WINDOW
ROPE_BASE = 10000.0
N_BRANCH = 3
FFN_HIDDEN = ((8 * D_MODEL + 3 * 256 - 1) // (3 * 256)) * 256
SPLIT_SIZES = (3 * HY_W, SSM_W, XBC_W, 2 * SSM_HEADS, ATT_W, KV_W, KV_W, N_BRANCH * D_MODEL)
SPLIT_IDX = tuple(int(s) for s in np.cumsum(SPLIT_SIZES)[:-1])
N_IN = sum(SPLIT_SIZES)
EPS = 1e-6

kernel_name = 'hybrid_dit_prefix_hyena_ssd_swa_step'

F32 = jnp.float32

def rmsnorm(x, g):
    xf = x.astype(F32)
    y = xf * lax.rsqrt(jnp.mean(xf * xf, axis=-1, keepdims=True) + EPS)
    return (y * g.astype(F32)).astype(x.dtype)

def dwconv(x, w, b):
    C = x.shape[-1]
    pad = SHORT_CONV // 2
    y = lax.conv_general_dilated(x, w[:, None, :].astype(x.dtype), window_strides=(1,),
                                 padding=((pad, pad),), dimension_numbers=('NWC', 'WIO', 'NWC'),
                                 feature_group_count=C)
    return y + b.astype(x.dtype)

def adaln(cond, w, b):
    mod = jax.nn.silu(cond) @ w + b
    return mod.reshape(cond.shape[0], 6, D_MODEL)

def hyena_filters(L, p):
    t = jnp.arange(L, dtype=F32) / L
    ang = 2.0 * jnp.pi * t[:, None] * jnp.arange(1, HY_BANDS + 1, dtype=F32)[None]
    feat = jnp.concatenate([t[:, None], jnp.cos(ang), jnp.sin(ang)], axis=-1)
    h = jnp.sin(p['hy_freq1'].astype(F32) * (feat @ p['hy_w1'].astype(F32) + p['hy_b1'].astype(F32)))
    h = jnp.sin(p['hy_freq2'].astype(F32) * (h @ p['hy_w2'].astype(F32) + p['hy_b2'].astype(F32)))
    h = (h @ p['hy_w3'].astype(F32)) * jnp.exp(-t[:, None] * p['hy_decay'].astype(F32)[None])
    return h.reshape(L, 2, 2, HY_W)

def long_conv(u, hf, hb, bias):
    L, C = hf.shape
    k = jnp.concatenate([hf, jnp.zeros((1, C), F32), hb[:0:-1]], axis=0)
    uf = u.astype(F32)
    spec = jnp.fft.rfft(uf, n=2 * L, axis=1) * jnp.fft.rfft(k, axis=0)[None]
    y = jnp.fft.irfft(spec, n=2 * L, axis=1)[:, :L]
    return (y + uf * bias.astype(F32)).astype(u.dtype)

def hyena_branch(hy_in, p):
    L = hy_in.shape[1]
    hc = dwconv(hy_in, p['hy_conv_w'], p['hy_conv_b'])
    v, x1, x2 = jnp.split(hc, 3, axis=-1)
    filt = hyena_filters(L, p)
    z = x1 * long_conv(v, filt[:, 0, 0], filt[:, 0, 1], p['hy_bias'][0])
    return x2 * long_conv(z, filt[:, 1, 0], filt[:, 1, 1], p['hy_bias'][1])

def ssd(x, dt, a, bm, cm, h0):
    b, L, H, P = x.shape
    nc = L // SSM_CHUNK
    rep = H // bm.shape[2]
    bm = jnp.repeat(bm, rep, axis=2).reshape(b, nc, SSM_CHUNK, H, SSM_STATE)
    cm = jnp.repeat(cm, rep, axis=2).reshape(b, nc, SSM_CHUNK, H, SSM_STATE)
    x = x.reshape(b, nc, SSM_CHUNK, H, P)
    dt = dt.reshape(b, nc, SSM_CHUNK, H)
    acum = jnp.cumsum(dt * a, axis=2)
    xdt = x * dt[..., None]
    tri = jnp.tril(jnp.ones((SSM_CHUNK, SSM_CHUNK), bool))[None, None, :, :, None]
    diff = acum[:, :, :, None, :] - acum[:, :, None, :, :]
    lmat = jnp.exp(jnp.where(tri, diff, -jnp.inf))
    scores = jnp.einsum('bcihn,bcjhn->bcijh', cm, bm) * lmat
    y_diag = jnp.einsum('bcijh,bcjhp->bcihp', scores, xdt)
    decay_end = jnp.exp(acum[:, :, -1:, :] - acum)
    chunk_states = jnp.einsum('bcjhn,bcjh,bcjhp->bchpn', bm, decay_end, xdt)
    chunk_decay = jnp.exp(acum[:, :, -1, :])

    def step(h, inp):
        s, d = inp
        return d[:, :, None, None] * h + s, h

    h_final, h_starts = lax.scan(step, h0.astype(F32),
                                 (jnp.moveaxis(chunk_states, 1, 0), jnp.moveaxis(chunk_decay, 1, 0)))
    h_starts = jnp.moveaxis(h_starts, 0, 1)
    y_off = jnp.einsum('bcihn,bchpn->bcihp', cm, h_starts) * jnp.exp(acum)[..., None]
    return (y_diag + y_off).reshape(b, L, H, P), h_final

def ssm_branch(s_z, s_xbc, s_dt, p, h0):
    B_, L, _ = s_xbc.shape
    xbc = jax.nn.silu(dwconv(s_xbc, p['ssm_conv_w'], p['ssm_conv_b']))
    xs, bm, cm = jnp.split(xbc, (SSM_W, SSM_W + SSM_GROUPS * SSM_STATE), axis=-1)
    xs = xs.astype(F32).reshape(B_, L, SSM_HEADS, SSM_HEAD_DIM)
    bm = bm.astype(F32).reshape(B_, L, SSM_GROUPS, SSM_STATE)
    cm = cm.astype(F32).reshape(B_, L, SSM_GROUPS, SSM_STATE)
    dt = jax.nn.softplus(s_dt.astype(F32).reshape(B_, L, 2, SSM_HEADS) + p['ssm_dt_bias'].astype(F32))
    a = -jnp.exp(p['ssm_a_log'].astype(F32))
    dskip = p['ssm_d'].astype(F32)
    y_f, h_f = ssd(xs, dt[:, :, 0], a[0], bm, cm, h0[:, 0])
    y_b, h_b = ssd(xs[:, ::-1], dt[:, ::-1, 1], a[1], bm[:, ::-1], cm[:, ::-1], h0[:, 1])
    y = y_f + y_b[:, ::-1] + (dskip[0] + dskip[1])[:, None] * xs
    y = y.reshape(B_, L, SSM_W).astype(s_z.dtype)
    y = rmsnorm(y * jax.nn.silu(s_z), p['ssm_norm'])
    return y, jnp.stack([h_f, h_b], axis=1)

def axial_rope_tables(L):
    rows = L // GRID_W
    row = jnp.repeat(jnp.arange(rows), GRID_W)
    col = jnp.tile(jnp.arange(GRID_W), rows)
    pos = jnp.stack([row, col], axis=-1).astype(F32)
    nq = HEAD_DIM // 4
    inv = ROPE_BASE ** (-jnp.arange(nq, dtype=F32) / nq)
    ang = pos[:, :, None] * inv
    return jnp.cos(ang), jnp.sin(ang)

def apply_rope(x, cos, sin):
    B, L, H, _ = x.shape
    xf = x.astype(F32).reshape(B, L, H, 2, 2, HEAD_DIM // 4)
    x1, x2 = xf[..., 0, :], xf[..., 1, :]
    c = cos[None, :, None]
    s = sin[None, :, None]
    out = jnp.stack([x1 * c - x2 * s, x2 * c + x1 * s], axis=-2)
    return out.reshape(B, L, H, HEAD_DIM).astype(x.dtype)

def attend(q, k, v, mask, sink):
    s = jnp.einsum('bqkgd,bskd->bkgqs', q.astype(F32), k.astype(F32)) * (HEAD_DIM ** -0.5)
    if mask is not None:
        s = jnp.where(mask, s, -jnp.inf)
    sk = sink.astype(F32)[None, :, :, None, None]
    m = jnp.maximum(jnp.max(s, axis=-1, keepdims=True), sk)
    e = jnp.exp(s - m)
    prob = e / (jnp.sum(e, axis=-1, keepdims=True) + jnp.exp(sk - m))
    o = jnp.einsum('bkgqs,bskd->bqkgd', prob, v.astype(F32))
    return o.astype(q.dtype)

def ctx_attention(q, k, v, sink):
    B, L = q.shape[:2]
    nb = L // ATT_BLOCK
    qb = q.reshape(B, nb, ATT_BLOCK, KV_HEADS, Q_PER_KV, HEAD_DIM).swapaxes(0, 1)
    out = lax.map(lambda qq: attend(qq, k, v, None, sink), qb)
    return out.swapaxes(0, 1).reshape(B, L, ATT_W)

def latent_attention(q, k, v, ck, cv, sink):
    B, L = q.shape[:2]
    Lc = ck.shape[1]
    nb = L // ATT_BLOCK
    qb = q.reshape(B, nb, ATT_BLOCK, KV_HEADS, Q_PER_KV, HEAD_DIM).swapaxes(0, 1)
    kp = jnp.pad(k, ((0, 0), (WINDOW, WINDOW), (0, 0), (0, 0)))
    vp = jnp.pad(v, ((0, 0), (WINDOW, WINDOW), (0, 0), (0, 0)))
    ctx_ok = jnp.ones((ATT_BLOCK, Lc), bool)

    def blk(args):
        qq, i = args
        start = i * ATT_BLOCK
        kb = lax.dynamic_slice_in_dim(kp, start, BAND, axis=1)
        vb = lax.dynamic_slice_in_dim(vp, start, BAND, axis=1)
        kpos = start - WINDOW + jnp.arange(BAND)
        qpos = start + jnp.arange(ATT_BLOCK)
        band_ok = (jnp.abs(qpos[:, None] - kpos[None]) <= WINDOW) & (kpos >= 0)[None] & (kpos < L)[None]
        mask = jnp.concatenate([ctx_ok, band_ok], axis=1)
        keys = jnp.concatenate([ck.astype(kb.dtype), kb], axis=1)
        vals = jnp.concatenate([cv.astype(vb.dtype), vb], axis=1)
        return attend(qq, keys, vals, mask, sink)

    out = lax.map(blk, (qb, jnp.arange(nb)))
    return out.swapaxes(0, 1).reshape(B, L, ATT_W)

def mixer(u, p, ctx):
    B, L, _ = u.shape
    proj = u @ p['w_in']
    hy_in, s_z, s_xbc, s_dt, a_q, a_k, a_v, g = jnp.split(proj, SPLIT_IDX, axis=-1)
    hy_y = hyena_branch(hy_in, p)
    if ctx is None:
        h0 = jnp.zeros((B, 2, SSM_HEADS, SSM_HEAD_DIM, SSM_STATE), F32)
    else:
        h0 = ctx[2]
    ssm_y, ssm_state = ssm_branch(s_z, s_xbc, s_dt, p, h0)
    q = a_q.reshape(B, L, N_HEADS, HEAD_DIM)
    k = a_k.reshape(B, L, KV_HEADS, HEAD_DIM)
    v = a_v.reshape(B, L, KV_HEADS, HEAD_DIM)
    sink = p['attn_sink'].reshape(KV_HEADS, Q_PER_KV)
    if ctx is None:
        att = ctx_attention(q.reshape(B, L, KV_HEADS, Q_PER_KV, HEAD_DIM), k, v, sink)
        side = (k, v, ssm_state)
    else:
        cos, sin = axial_rope_tables(L)
        q = apply_rope(q, cos, sin)
        k = apply_rope(k, cos, sin)
        att = latent_attention(q.reshape(B, L, KV_HEADS, Q_PER_KV, HEAD_DIM), k, v, ctx[0], ctx[1], sink)
        side = None
    gate = jax.nn.sigmoid(g).reshape(B, L, N_BRANCH, D_MODEL)
    merged = (gate[:, :, 0] * (hy_y @ p['hy_proj'])
              + gate[:, :, 1] * (ssm_y @ p['ssm_proj'])
              + gate[:, :, 2] * (att @ p['attn_proj']))
    return merged @ p['w_out'], side

def ffn(h, p):
    return (jax.nn.silu(h @ p['ffn_w_gate']) * (h @ p['ffn_w_up'])) @ p['ffn_w_down']

def layer(x, mod, p, ctx):
    m = mod[:, None]
    h = rmsnorm(x, p['norm_mix_pre']) * (1.0 + m[:, :, 1]) + m[:, :, 0]
    mix, side = mixer(h, p, ctx)
    x = x + m[:, :, 2] * rmsnorm(mix, p['norm_mix_post'])
    h = rmsnorm(x, p['norm_ffn_pre']) * (1.0 + m[:, :, 4]) + m[:, :, 3]
    x = x + m[:, :, 5] * rmsnorm(ffn(h, p), p['norm_ffn_post'])
    return x, side

def setup_inputs(seed: int = 0) -> dict:
    key = jax.random.key(seed)
    ks = iter(jax.random.split(key, 64))

    def nrm(shape, scale=1.0):
        return scale * jax.random.normal(next(ks), shape, F32)

    def unif(shape, lo, hi):
        return jax.random.uniform(next(ks), shape, F32, lo, hi)

    dt0 = jnp.exp(unif((DEPTH, 2, SSM_HEADS), math.log(1e-3), math.log(1e-1)))
    dt_bias = dt0 + jnp.log(-jnp.expm1(-dt0))
    return {
        'x_prompt': nrm((BATCH, SEQ, D_MODEL)),
        'x_sample': nrm((DEC_BATCH, DEC_SEQ, D_MODEL)),
        'c': nrm((DEC_BATCH, D_MODEL)),
        'cache_k': nrm((DEC_BATCH, DEPTH, PAST_LEN, KV_HEADS, HEAD_DIM)),
        'cache_v': nrm((DEC_BATCH, DEPTH, PAST_LEN, KV_HEADS, HEAD_DIM)),
        'state_ssm': nrm((DEC_BATCH, DEPTH, 2, SSM_HEADS, SSM_HEAD_DIM, SSM_STATE), 0.3),
        'c_ctx': nrm((D_MODEL,)),
        'ada_w': nrm((DEPTH, D_MODEL, 6 * D_MODEL), D_MODEL ** -0.5),
        'ada_b': nrm((DEPTH, 6 * D_MODEL), 0.02),
        'norm_mix_pre': 1.0 + nrm((DEPTH, D_MODEL), 0.05),
        'norm_mix_post': 1.0 + nrm((DEPTH, D_MODEL), 0.05),
        'norm_ffn_pre': 1.0 + nrm((DEPTH, D_MODEL), 0.05),
        'norm_ffn_post': 1.0 + nrm((DEPTH, D_MODEL), 0.05),
        'w_in': nrm((DEPTH, D_MODEL, N_IN), D_MODEL ** -0.5),
        'hy_conv_w': nrm((DEPTH, SHORT_CONV, 3 * HY_W), SHORT_CONV ** -0.5),
        'hy_conv_b': nrm((DEPTH, 3 * HY_W), 0.02),
        'hy_w1': nrm((DEPTH, HY_FEAT, HY_HIDDEN), HY_FEAT ** -0.5),
        'hy_b1': nrm((DEPTH, HY_HIDDEN), 0.1),
        'hy_freq1': 1.0 + nrm((DEPTH, HY_HIDDEN), 0.1),
        'hy_w2': nrm((DEPTH, HY_HIDDEN, HY_HIDDEN), HY_HIDDEN ** -0.5),
        'hy_b2': nrm((DEPTH, HY_HIDDEN), 0.1),
        'hy_freq2': 1.0 + nrm((DEPTH, HY_HIDDEN), 0.1),
        'hy_w3': nrm((DEPTH, HY_HIDDEN, 4 * HY_W), 0.1 * HY_HIDDEN ** -0.5),
        'hy_decay': jnp.exp(unif((DEPTH, 4 * HY_W), math.log(3.0), math.log(15.0))),
        'hy_bias': nrm((DEPTH, 2, HY_W), 0.5),
        'ssm_conv_w': nrm((DEPTH, SHORT_CONV, XBC_W), SHORT_CONV ** -0.5),
        'ssm_conv_b': nrm((DEPTH, XBC_W), 0.02),
        'ssm_a_log': jnp.log(unif((DEPTH, 2, SSM_HEADS), 1.0, 16.0)),
        'ssm_dt_bias': dt_bias,
        'ssm_d': 1.0 + nrm((DEPTH, 2, SSM_HEADS), 0.1),
        'ssm_norm': 1.0 + nrm((DEPTH, SSM_W), 0.05),
        'attn_sink': nrm((DEPTH, N_HEADS), 0.5),
        'hy_proj': nrm((DEPTH, HY_W, D_MODEL), HY_W ** -0.5),
        'ssm_proj': nrm((DEPTH, SSM_W, D_MODEL), SSM_W ** -0.5),
        'attn_proj': nrm((DEPTH, ATT_W, D_MODEL), ATT_W ** -0.5),
        'w_out': nrm((DEPTH, D_MODEL, D_MODEL), D_MODEL ** -0.5),
        'ffn_w_gate': nrm((DEPTH, D_MODEL, FFN_HIDDEN), D_MODEL ** -0.5),
        'ffn_w_up': nrm((DEPTH, D_MODEL, FFN_HIDDEN), D_MODEL ** -0.5),
        'ffn_w_down': nrm((DEPTH, FFN_HIDDEN, D_MODEL), FFN_HIDDEN ** -0.5),
    }

def reference(x_prompt, x_sample, c, cache_k, cache_v, state_ssm, c_ctx, ada_w, ada_b,
              norm_mix_pre, norm_mix_post, norm_ffn_pre, norm_ffn_post, w_in,
              hy_conv_w, hy_conv_b, hy_w1, hy_b1, hy_freq1, hy_w2, hy_b2, hy_freq2, hy_w3,
              hy_decay, hy_bias, ssm_conv_w, ssm_conv_b, ssm_a_log, ssm_dt_bias, ssm_d, ssm_norm,
              attn_sink, hy_proj, ssm_proj, attn_proj, w_out, ffn_w_gate, ffn_w_up, ffn_w_down):
    stacked = {
        'ada_w': ada_w, 'ada_b': ada_b,
        'norm_mix_pre': norm_mix_pre, 'norm_mix_post': norm_mix_post,
        'norm_ffn_pre': norm_ffn_pre, 'norm_ffn_post': norm_ffn_post,
        'w_in': w_in, 'hy_conv_w': hy_conv_w, 'hy_conv_b': hy_conv_b,
        'hy_w1': hy_w1, 'hy_b1': hy_b1, 'hy_freq1': hy_freq1,
        'hy_w2': hy_w2, 'hy_b2': hy_b2, 'hy_freq2': hy_freq2,
        'hy_w3': hy_w3, 'hy_decay': hy_decay, 'hy_bias': hy_bias,
        'ssm_conv_w': ssm_conv_w, 'ssm_conv_b': ssm_conv_b, 'ssm_a_log': ssm_a_log,
        'ssm_dt_bias': ssm_dt_bias, 'ssm_d': ssm_d, 'ssm_norm': ssm_norm,
        'attn_sink': attn_sink, 'hy_proj': hy_proj, 'ssm_proj': ssm_proj, 'attn_proj': attn_proj,
        'w_out': w_out, 'ffn_w_gate': ffn_w_gate, 'ffn_w_up': ffn_w_up, 'ffn_w_down': ffn_w_down,
    }
    y_prompt = x_prompt
    y_sample = x_sample
    ks, vs, ss = [], [], []
    for l in range(DEPTH):
        p = {name: arr[l] for name, arr in stacked.items()}
        mod_ctx = adaln(c_ctx[None], p['ada_w'], p['ada_b'])
        y_prompt, (k_l, v_l, s_l) = layer(y_prompt, mod_ctx, p, None)
        ks.append(k_l)
        vs.append(v_l)
        ss.append(s_l)
        mod_lat = adaln(c, p['ada_w'], p['ada_b'])
        y_sample, _ = layer(y_sample, mod_lat, p, (cache_k[:, l], cache_v[:, l], state_ssm[:, l]))
    new_k = jnp.stack(ks, axis=1)
    new_v = jnp.stack(vs, axis=1)
    new_ssm = jnp.stack(ss, axis=1)
    return (y_prompt, y_sample, new_k, new_v, new_ssm)


_drawn_inputs = setup_inputs


def setup_inputs(seed=0):
    import zlib

    import numpy as np

    out = dict(_drawn_inputs(seed))
    spreads = {}
    factors = {'cache_k': 2.907, 'cache_v': 2.727, 'ssm_d': 2.855, 'attn_sink': 8.0, 'hy_conv_b': 2.921}
    for name, (base, spread) in spreads.items():
        noise = np.random.default_rng([zlib.crc32(name.encode()), seed]).standard_normal(out[name].shape)
        drawn = base * np.exp(spread * noise) if base else spread * noise
        out[name] = __import__('jax').numpy.asarray(drawn.astype(out[name].dtype))
    for name, factor in factors.items():
        out[name] = (out[name] * factor).astype(out[name].dtype)
    return out
```

```python
from contextlib import ExitStack
import numpy as np
import concourse.bass as bass
from concourse import mybir

ALU = mybir.AluOpType
ACT = mybir.ActivationFunctionType
F32 = mybir.dt.float32

P = 128
D = 1024
DEPTH = 2
LP, LS = 128, 512
T = LP + LS
NT = T // P
KD = D // P
GRID_W = 64
HY_W = 512
BANDS = 16
FEAT = 1 + 2 * BANDS
HID = 64
HEADS, HD = 8, 64
KV = 2
WINDOW = 128
FF = 2816
KF = FF // P
EPS = 1e-6
NEG = -1.0e30
IN_HY, IN_Z, IN_XBC, IN_DT, IN_Q, IN_K, IN_V, IN_G = 0, 1536, 2048, 2816, 2832, 3344, 3472, 3600
N_IN = 6672
RING = 3
WB = 4096
TWO_PI = 2.0 * np.pi

CONST = {}
_at = 0
for _n, _w in (("ident", P), ("ones", P), ("t_le_i", P), ("t_ge_i", P), ("t_gt_j", P), ("t_lt_j", P), ("rotate", P),
               ("cos", LS), ("sin", LS), ("mask", 512), ("mask_first", 384), ("dft_c_p", P), ("dft_s_p", P),
               ("idft_s_p", P), ("spec_w", 2), ("neg_t", NT), ("eps", 1),
               ("dft_c", 4 * LS), ("dft_s", 4 * LS), ("idft_s", 4 * LS)):
    CONST[_n] = (_at, _w)
    _at += _w
N_CONST = _at


def constant_tables():
    c = np.zeros((P, N_CONST), np.float64)

    def put(name, a):
        at, w = CONST[name]
        c[:a.shape[0], at:at + w] = a.reshape(a.shape[0], -1)

    p, f = np.arange(P)[:, None], np.arange(P)[None]
    put("ident", (p == f) * 1.0)
    put("ones", np.ones((P, P)))
    put("t_le_i", (p <= f) * 1.0)
    put("t_ge_i", (p >= f) * 1.0)
    put("t_gt_j", (p > f) * 1.0)
    put("t_lt_j", (p < f) * 1.0)
    rot = np.zeros((P, P))
    for m in range(P):
        if m % 32 < 16:
            rot[m + 16, m] = -1.0
        else:
            rot[m - 16, m] = 1.0
    put("rotate", rot)
    nq = HD // 4
    inv = 10000.0 ** (-np.arange(nq) / nq)
    tok = np.arange(LS)
    pos = np.stack([tok // GRID_W, tok % GRID_W])
    ang = np.zeros((P, LS))
    for m in range(P):
        ang[m] = pos[(m % HD) // 32] * np.float32(inv[m % 16])
    put("cos", np.cos(ang))
    put("sin", np.sin(ang))
    before = np.where(f >= p, 0.0, NEG)
    after = np.where(f <= p, 0.0, NEG)
    zero = np.zeros((P, P))
    put("mask", np.concatenate([zero, before, zero, after], 1))
    put("mask_first", np.concatenate([zero, zero, after], 1))
    for tail, n in (("_p", LP), ("", LS)):
        i = np.arange(n)
        cosine = np.cos(np.pi * np.outer(i, i) / n)
        sine = np.sin(np.pi * np.outer(i, i) / n)
        forward, inverse = sine.copy(), sine.copy()
        forward[:, 0] = (-1.0) ** i
        inverse[0, :] = (-1.0) ** i
        lay = lambda a: a.reshape(n // P, P, n).transpose(1, 0, 2)
        put("dft_c" + tail, lay(cosine))
        put("dft_s" + tail, lay(forward))
        put("idft_s" + tail, lay(inverse))
    w = np.stack([np.full(P, 1.0 / LP), np.full(P, 1.0 / LS)], 1)
    w[0] *= 0.5
    put("spec_w", w)
    t = np.concatenate([np.arange(LP) / LP, np.arange(LS) / LS])
    put("neg_t", -t.reshape(NT, P).T)
    put("eps", np.full((P, 1), EPS))
    return c.astype(np.float32)


def filter_features():
    t = np.concatenate([np.arange(LP) / LP, np.arange(LS) / LS])
    ang = 2.0 * np.pi * t[None] * np.arange(1, BANDS + 1)[:, None]
    return np.concatenate([t[None], np.cos(ang), np.sin(ang)]).astype(np.float32)


ROWS = {}
_at = 0
for _n, _w in (("mix_pre", 8), ("mix_post", 8), ("ffn_pre", 8), ("ffn_post", 8), ("hy_w", 36), ("hy_b", 12),
               ("ssm_w", 18), ("ssm_b", 6), ("ssm_norm", 4)):
    ROWS[_n] = (_at, _w)
    _at += _w
N_ROWS = _at


class Steps:

    def __init__(self, known):
        self.known, self.named, self.count = known, {}, 0

    def __call__(self, instruction, *name):
        self.count += 1
        if name:
            self.named[name] = self.count
        return instruction

    def __getitem__(self, name):
        return self.known.get(name if isinstance(name, tuple) else (name,), 1)


def build(nc, A, O, known):
    tiles = ExitStack()
    with tiles:
        def sb(name, cols, rows=P):
            return tiles.enter_context(nc.sbuf_tensor(name, [rows, cols], F32))

        def sem(name):
            return tiles.enter_context(nc.semaphore(name))

        const = sb("const", N_CONST)

        def K(name, a=0, b=None, rows=P):
            at, w = CONST[name]
            return const[0:rows, at + a:at + (w if b is None else b)]

        def tiled(t, base, n, w=T):
            return t[:, base:base + n * w].rearrange("p (n w) -> p n w", n=n)

        xT = tiled(sb("residual", KD * T), 0, KD)
        hT = tiled(sb("normed", KD * T), 0, KD)
        ring = sb("weights", RING * WB)
        pcol = sb("param_cols", N_ROWS)
        bcol = sb("bias_cols", 52)
        modT = sb("modulation", 96)[:, :].rearrange("p (n c) -> p n c", c=2)
        scale_pre = sb("scale_pre", 32)[:, :].rearrange("p (s n c) -> p s n c", s=2, c=2)
        gain_post = sb("gain_post", 32)[:, :].rearrange("p (s n c) -> p s n c", s=2, c=2)
        condT = sb("cond", 16)
        dt_bias = sb("dt_bias", 16)
        neg_a = sb("neg_a", 16)
        dskip2 = sb("dskip2", 16)
        dskip = sb("dskip", 4)
        sinks = sb("sinks", 8)
        hy_bias = sb("hy_bias", 1, 1)
        arena_size = 20760
        arena = sb("arena", arena_size)
        ps = tiles.enter_context(nc.psum_tensor("ps", [P, 4 * 1024], F32))

        tensor_done, vector_done = sem("tensor_done"), sem("vector_done")
        scalar_done, pool_done = sem("scalar_done"), sem("pool_done")
        weights_in = [sem(f"weights_in{i}") for i in range(RING)]
        const_in, x_in, y_out = sem("const_in"), sem("x_in"), sem("y_out")
        cond_in, rows_in, rowvec_in, filt_in = sem("cond_in"), sem("rows_in"), sem("rowvec_in"), sem("filt_in")
        decay_in, w3_in, state_in, cache_in = sem("decay_in"), sem("w3_in"), sem("state_in"), sem("cache_in")
        state_out, kv_out, hidden_in = sem("state_out"), sem("kv_out"), sem("hidden_in")
        layer_sems = [tensor_done, vector_done, scalar_done, pool_done, *weights_in, cond_in, rows_in,
                      rowvec_in, filt_in, decay_in, w3_in, state_in, cache_in, state_out, kv_out, hidden_in]

        def new_steps():
            return [Steps(known.get(e, {})) for e in "TVSG"]

        def slot(s):
            return ps[:, 1024 * s:1024 * s + 1024]

        def tokens(s):
            return ps[:, 1024 * s + 384:1024 * s + 1024]

        xrows = arena[:, 0:NT * D].rearrange("p (n d) -> p n d", d=D)
        with nc.Block() as block:
            Tn, Vc, Sc, Gp = new_steps()

            @block.sync
            def _(sp):
                sp.dma_start(const[:, :], A["consts"]).then_inc(const_in, 16)
                sp.dma_start(xrows[:, 0, :], A["x_prompt"][0]).then_inc(x_in, 16)
                sp.dma_start(xrows[:, 1:NT, :], A["x_sample"][0].rearrange("(n p) d -> p n d", p=P)).then_inc(x_in, 16)

            @block.tensor
            def _(pe):
                pe.wait_ge(const_in, 16)
                pe.wait_ge(x_in, 32)
                for k in range(KD):
                    if k >= 4:
                        pe.wait_ge(vector_done, k - 3)
                    for n in range(NT):
                        t = pe.transpose(tokens(k % 4)[:, n * P:(n + 1) * P], xrows[:, n, k * P:(k + 1) * P], K("ident"))
                    t.then_inc(tensor_done, 1)

            @block.vector
            def _(dve):
                for k in range(KD):
                    dve.wait_ge(tensor_done, k + 1)
                    dve.tensor_copy(xT[:, k, :], tokens(k % 4)).then_inc(vector_done, 1)

        nc.sync.sem_clear(tensor_done)
        nc.sync.sem_clear(vector_done)
        nc.all_engine_barrier()

        with nc.Fori(0, DEPTH) as layer:
            named = layer_body(nc, A, O, known, layer, locals())
            for s in layer_sems:
                nc.sync.sem_clear(s)
            nc.all_engine_barrier()

        with nc.Block() as block:
            @block.tensor
            def _(pe):
                for n in range(NT):
                    if n >= 4:
                        pe.wait_ge(vector_done, n - 3)
                    for k in range(KD):
                        t = pe.transpose(slot(n % 4)[:, k * P:(k + 1) * P], xT[:, k, n * P:(n + 1) * P], K("ident"))
                    t.then_inc(tensor_done, 1)

            @block.vector
            def _(dve):
                for n in range(NT):
                    dve.wait_ge(tensor_done, n + 1)
                    dve.tensor_copy(xrows[:, n, :], slot(n % 4)).then_inc(vector_done, 1)

            @block.sync
            def _(sp):
                for n in range(NT):
                    sp.wait_ge(vector_done, n + 1)
                    dst = O["y_prompt"][0] if n == 0 else O["y_sample"][0, (n - 1) * P:n * P, :]
                    sp.dma_start(dst, xrows[:, n, :]).then_inc(y_out, 16)
                sp.wait_ge(y_out, 16 * NT)
    return named


def layer_body(nc, A, O, known, layer, env):
    K, tiled, xT, hT, ring, pcol, bcol, modT = (env[n] for n in ("K", "tiled", "xT", "hT", "ring", "pcol", "bcol", "modT"))
    scale_pre, gain_post, condT, dt_bias, neg_a = (env[n] for n in ("scale_pre", "gain_post", "condT", "dt_bias", "neg_a"))
    dskip2, dskip, sinks, arena, slot, tokens = (env[n] for n in ("dskip2", "dskip", "sinks", "arena", "slot", "tokens"))
    tensor_done, vector_done, scalar_done, pool_done = (env[n] for n in ("tensor_done", "vector_done", "scalar_done", "pool_done"))
    weights_in, hidden_in = env["weights_in"], env["hidden_in"]
    cond_in, rows_in, rowvec_in, filt_in, decay_in = (env[n] for n in ("cond_in", "rows_in", "rowvec_in", "filt_in", "decay_in"))
    w3_in, state_in, cache_in, state_out, kv_out = (env[n] for n in ("w3_in", "state_in", "cache_in", "state_out", "kv_out"))
    Tn, Vc, Sc, Gp = (Steps(known.get(e, {})) for e in "TVSG")

    def row(name, k, rows=1):
        return pcol[:, ROWS[name][0] + k:ROWS[name][0] + k + rows]

    prow = arena[:, 0:P]
    brow = arena[:, P:2 * P]
    crow = arena[:, 2 * P:3 * P]
    hrow = arena[0:4, 6600:6600 + HID]
    mrow = arena[0:2, 3 * P:3 * P + 6 * D]
    squares = [arena[:, 7000 + T * i:7000 + T * (i + 1)] for i in range(3)]
    rstd = arena[:, 7000 + 3 * T:7000 + 4 * T]
    lnvar = arena[:, 7000 + 4 * T:7000 + 5 * T]
    zg = tiled(arena, 0, 4)
    xbc = tiled(arena, 2560, 6)
    BT, CT = xbc[:, 4, :], xbc[:, 5, :]
    x_tok = arena[:, 6400:6400 + NT * 512].rearrange("p (c n) -> p c n", c=NT)
    B_tok = arena[:, 8960:8960 + T].rearrange("p (c n) -> p c n", c=NT)
    at = 8960 + T
    dts = arena[:, at:at + 80].rearrange("p (c m) -> p c m", c=NT)
    dA = arena[:, at + 80:at + 160].rearrange("p (c m) -> p c m", c=NT)
    w_end = arena[:, at + 160:at + 240].rearrange("p (r c h) -> p r c h", r=2, c=NT)
    chunk_decay = arena[:, at + 240:at + 280].rearrange("p (c r h) -> p c r h", c=NT, r=2)
    at += 280
    H = arena[:, at:at + 2048].rearrange("p (r c n) -> p r c n", r=2, c=4)
    H_end = arena[:, at + 2048:at + 2560].rearrange("p (r n) -> p r n", r=2)
    at += 2560
    xdt = arena[:, at:at + 1024].rearrange("p (r n) -> p r n", r=2)
    xw = [arena[:, at + 1024:at + 1536], arena[:, at + 1536:at + 2048]]
    at += 2048
    dA_tri = arena[:, at:at + 2048].rearrange("p (r n) -> p r n", r=2)
    E_seg = arena[:, at + 2048:at + 4096].rearrange("p (r n) -> p r n", r=2)
    dt_row = arena[0:16, at:at + T]
    init_rows = arena[0:64, at + 2048:at + 3072]
    sp_a, sp_b, sp_c = (arena[:, at + 3072 + 80 * i:at + 3152 + 80 * i] for i in range(3))
    at += 4096
    C_dec = arena[:, at:at + 1024].rearrange("p (r n) -> p r n", r=2)
    E_acc = C_dec
    end_rows = arena[0:64, at:at + 1024]
    G_tri = arena[:, at + 1024:at + 1536].rearrange("p (r g n) -> p r g n", r=2, g=2)
    at += 1536
    xskip = xbc[:, 0:4, :]
    assert at <= 20120
    ssmY = zg
    v_tok = arena[:, 2560:5120].rearrange("p (c n) -> p c n", c=NT)
    x2T = tiled(arena, 2560, 4)
    x1_tok = arena[:, 5120:7680].rearrange("p (c n) -> p c n", c=NT)
    fsum = arena[:, 7680:10240].rearrange("p (c n) -> p c n", c=NT)
    fdif = arena[:, 10240:12800].rearrange("p (c n) -> p c n", c=NT)
    Yr, Ys = fsum, fdif
    Kr = arena[:, 12800:15360].rearrange("p (c n) -> p c n", c=NT)
    Ks = arena[:, 15360:17920].rearrange("p (c n) -> p c n", c=NT)
    decay = arena[:, 17920:18944].rearrange("p (r n) -> p r n", r=2)
    w3 = arena[0:HID, 18944:19968]
    hid1 = arena[0:HID, 12800:13440]
    hid2 = arena[0:HID, 13440:14080]
    arg_k = arena[0:HID, 14080:14720]
    feat = arena[0:FEAT, 15744:15744 + T]
    hb_tmp = [arena[:, 14720:15232], arena[:, 15232:15744]]
    conv_raw = [arena[:, 15744 + T * i:15744 + T * (i + 1)] for i in range(2)]
    w1sb, w2sb = arena[0:FEAT, 20120:20120 + HID], arena[0:HID, 20184:20184 + HID]
    bias_row = arena[0:1, 20248:20760]
    hyY = tiled(arena, 5120, 4)
    prod_a, prod_b = decay[:, 0, :], decay[:, 1, :]
    attY = tiled(arena, 2560, 4)
    qT = tiled(arena, 7680, 4)
    kT = arena[:, 10240:10240 + T]
    v_att = arena[:, 10880:10880 + T].rearrange("p (c n) -> p c n", c=NT)
    k_rows = arena[:, 11520:11520 + P]
    kc_rows = arena[:, 11648:11648 + P]
    kcT = arena[:, 11776:11776 + P]
    v_ctx = arena[:, 11904:11904 + P]
    S_sb = [arena[:, 12032 + 1024 * i:12032 + 1024 * (i + 1)].rearrange("p (g n) -> p g n", g=2) for i in range(3)]
    PT_sb = [arena[:, 15104 + 1024 * i:15104 + 1024 * (i + 1)].rearrange("p (g n) -> p g n", g=2) for i in range(3)]
    rot_tmp = [arena[:, 18176 + 512 * i:18176 + 512 * (i + 1)] for i in range(2)]
    stat = arena[:, 19200:19200 + 200].rearrange("p (n c) -> p n c", c=10)
    merged = tiled(arena, 7680, 8)
    sig = [arena[:, 12800 + T * i:12800 + T * (i + 1)] for i in range(4)]
    part = [arena[:, 15360 + T * i:15360 + T * (i + 1)] for i in range(3)]
    mix = tiled(arena, 0, 8)
    act = tiled(arena, 0, KF)
    ffn_gate = [arena[:, 14080 + T * i:14080 + T * (i + 1)] for i in range(2)]
    mix2 = tiled(arena, 14080, 8)

    def k_major(a, lo, cols):
        return a[:, lo:lo + cols].rearrange("(k p) n -> p k n", p=P)

    w_in, ada = A["w_in"][layer], A["ada_w"][layer]
    blocks = []

    def block_of(name, parts):
        blocks.append((name, parts))

    def ring_view(n, k, cols, at=0):
        base = WB * (n % RING) + at
        return ring[:, base:base + k * cols].rearrange("p (k n) -> p k n", k=k)

    for j in range(12):
        block_of(("ada", j), [(0, 8, 512, k_major(ada, 512 * j, 512))])
    block_of(("z",), [(0, 8, 512, k_major(w_in, IN_Z, 512))])
    block_of(("xbc", 0), [(0, 8, 512, k_major(w_in, IN_XBC, 512))])
    block_of(("xbc", 1), [(0, 8, 272, k_major(w_in, IN_XBC + 512, 272))])
    for i in range(2):
        block_of(("hy", i), [(0, 8, 512, k_major(w_in, 512 * i, 512))])
    block_of(("hy", 2), [(0, 8, 512, k_major(w_in, 1024, 512))])
    block_of(("q",), [("q", 8, 512, w_in)])
    block_of(("kv",), [(0, 8, 256, k_major(w_in, IN_K, 256))])
    for og in range(2):
        for b in range(3):
            block_of(("gate", og, b), [(0, 8, 512, k_major(w_in, IN_G + D * b + 512 * og, 512))])
            block_of(("proj", og, b), [("att" if b == 2 else 0, 4, 512, None if b == 2 else k_major(
                (A["hy_proj"], A["ssm_proj"])[b][layer], 512 * og, 512))] + [(og,)] * (b == 2))
    for og in range(2):
        block_of(("out", og), [(0, 8, 512, k_major(A["w_out"][layer], 512 * og, 512))])
    FB = [(512 * j, min(512, FF - 512 * j)) for j in range((FF + 511) // 512)]
    for j, (lo, w) in enumerate(FB):
        block_of(("up", 0, j), [(0, 8, w, k_major(A["ffn_w_gate"][layer], lo, w))])
        block_of(("up", 1, j), [(0, 8, w, k_major(A["ffn_w_up"][layer], lo, w))])
    KH = KF // 2
    for oc in range(4):
        for half in range(2):
            src = A["ffn_w_down"][layer][half * KH * P:(half + 1) * KH * P, :]
            block_of(("down", oc, half), [(0, KH, 256, k_major(src, 256 * oc, 256))])
    index = {name: n for n, (name, _) in enumerate(blocks)}

    def weights(eng, *name):
        n = index[name]
        eng.wait_ge(weights_in[n % RING], 16 * (WDMA[n]))
        _, parts = blocks[n]
        return ring_view(n, parts[0][1], parts[0][2])

    WDMA, per = [], [0] * RING
    for n, (name, parts) in enumerate(blocks):
        per[n % RING] += 8 * KV if parts[0][0] == "q" else KV if parts[0][0] == "att" else 1
        WDMA.append(per[n % RING])

    uses = []

    def take(pe, *name):
        if len(uses) >= 4:
            engine, old = uses[-4]
            if engine == "V":
                pe.wait_ge(vector_done, Vc[old])
            else:
                pe.wait_ge(scalar_done, Sc[old])
        uses.append((name[0], name[1:]))
        s = (len(uses) - 1) % 4
        Tn.named[("slot",) + name[1:]] = s
        return s

    blocks_used = [0]

    def w_used(n=1):
        for _ in range(n):
            Tn.named[("used", blocks_used[0])] = Tn.count
            blocks_used[0] += 1

    def used(*name):
        return Tn.known.get(("slot",) + name, 0)

    def dense(pe, s, lhs, rhs):
        for k in range(len(lhs)):
            a, b = k == 0, k == len(lhs) - 1
            pe.matmul(tokens(s)[:, 0:LP], lhs[k], rhs[k][:, 0:LP], start=a, stop=b)
            m = pe.matmul(tokens(s)[:, LP:T], lhs[k], rhs[k][:, LP:T], start=a, stop=b)
        return m

    hk = [hT[:, k, :] for k in range(KD)]

    def channel_sum(pe, name, n):
        s = take(pe, "S", "ln", name)
        for k in range(n):
            pe.wait_ge(scalar_done, Sc["sq", name, k])
            sq = sq_of(name, k)
            pe.matmul(tokens(s)[:, 0:LP], K("ones"), sq[:, 0:LP], start=k == 0, stop=k == n - 1)
            Tn(pe.matmul(tokens(s)[:, LP:T], K("ones"), sq[:, LP:T], start=k == 0, stop=k == n - 1)
               .then_inc(tensor_done, 1), "sq", name, k)
        Tn.named[("sum", name)] = Tn.count

    def norm_sum(pe, name):
        channel_sum(pe, name, KD)

    def sq_of(name, k):
        return squares[k % 2] if name == "ssm" else squares[k % 3] if name in ("n1", "n2") else hT[:, k, :]

    def rstd_of(sc, name, width):
        sc.wait_ge(tensor_done, Tn["sum", name])
        s = used("ln", name)
        Sc(sc.activation(lnvar, tokens(s), ACT.Ln, scale=1.0 / width, bias=K("eps")).then_inc(scalar_done, 1), "ln", name)
        sc.wait_ge(scalar_done, Sc["ln", name])
        Sc(sc.activation(rstd, lnvar, ACT.Exp, scale=-0.5).then_inc(scalar_done, 1), "rstd", name)

    def pre_norm(sc, i, name):
        for k in range(KD):
            if i == 1:
                sc.wait_ge(vector_done, Vc["x", 0, k])
            if k >= 3:
                sc.wait_ge(tensor_done, Tn["sq", name, k - 3])
            Sc(sc.activation(squares[k % 3], xT[:, k, :], ACT.Square).then_inc(scalar_done, 1), "sq", name, k)
        rstd_of(sc, name, D)
        sc.wait_ge(vector_done, Vc["gains", 1])
        for k in range(KD):
            sc.wait_ge(vector_done, Vc["xn", name, k])
            for c, (lo, hi) in enumerate(((0, LP), (LP, T))):
                Sc(sc.activation(hT[:, k, lo:hi], hT[:, k, lo:hi], ACT.Identity, scale=scale_pre[:, i, k, c:c + 1],
                                 bias=modT[:, 24 * i + k, c:c + 1]).then_inc(scalar_done, 1), "h", name, k)

    def norm_apply(dve, name):
        dve.wait_ge(scalar_done, Sc["rstd", name])
        for k in range(KD):
            Vc(dve.tensor_tensor(hT[:, k, :], xT[:, k, :], rstd, ALU.mult).then_inc(vector_done, 1), "xn", name, k)

    def mixed(sc, i, dst, name):
        for o in range(KD):
            sc.wait_ge(tensor_done, Tn["mix", i, o])
            s = used("mix", i, o)
            Sc(sc.copy(dst[:, o, :], tokens(s)).then_inc(scalar_done, 1))
            Sc(sc.activation(hT[:, o, :], tokens(s), ACT.Square).then_inc(scalar_done, 1), "mix", i, o)
            Sc.named[("sq", name, o)] = Sc.count
        rstd_of(sc, name, D)

    def post_norm(dve, i, src, name):
        dve.wait_ge(scalar_done, Sc["rstd", name])
        for k in range(KD):
            Vc(dve.tensor_tensor(src[:, k, :], src[:, k, :], rstd, ALU.mult).then_inc(vector_done, 1))
            dve.wait_ge(vector_done, Vc.count)
            for c, (lo, hi) in enumerate(((0, LP), (LP, T))):
                Vc(dve.scalar_tensor_tensor(out=xT[:, k, lo:hi], in0=src[:, k, lo:hi], scalar=gain_post[:, i, k, c:c + 1],
                                            in1=xT[:, k, lo:hi], op0=ALU.mult, op1=ALU.add).then_inc(vector_done, 1), "x", i, k)

    CHAIN = [(0, 0), (0, 1), (1, 0), (4, 1), (2, 0), (3, 1), (3, 0), (2, 1)]
    UNITS = [(b, t) for b in range(NT) for t in range(4)]

    def key_tiles(b):
        return [0] if b == 0 else [-1] + list(range(max(1, b - 1), min(NT, b + 2)))

    def n_keys(b):
        return len(key_tiles(b))

    with nc.Block() as block:
        @block.tensor
        def _(pe):
            pe.wait_ge(rows_in, 16 * 10)
            s = take(pe, "V", "pcol")
            pe.transpose(slot(s)[:, 0:N_ROWS], prow[0:N_ROWS, :], K("ident", rows=N_ROWS)[:, 0:N_ROWS])
            Tn(pe.transpose(slot(s)[:, 512:560], brow[0:48, :], K("ident", 0, 48, 48)).then_inc(tensor_done, 1), "pcol")
            pe.wait_ge(hidden_in, 16 * 4)
            s = take(pe, "V", "bcol")
            Tn(pe.transpose(slot(s)[0:HID, 0:4], hrow, K("ident", 0, 4, 4)).then_inc(tensor_done, 1), "bcol")
            pe.wait_ge(scalar_done, Sc["cond"])
            s = take(pe, "V", "condT")
            Tn(pe.transpose(slot(s)[:, 0:16], crow[0:16, :], K("ident", 0, 16, 16)).then_inc(tensor_done, 1), "condT")
            pe.wait_ge(vector_done, Vc["condT"])
            cond = condT[:, :].rearrange("p (c k) -> p k c", c=2)
            for j in range(12):
                w = weights(pe, "ada", j)
                s = take(pe, "S", "mrow", j)
                for k in range(KD):
                    m = pe.matmul(slot(s)[0:2, 0:512], cond[:, k, :], w[:, k, :], start=k == 0, stop=k == KD - 1)
                Tn(m.then_inc(tensor_done, 1), "mrow", j)
                w_used()
            norm_sum(pe, "n1")
            pe.wait_ge(scalar_done, Sc["mrow", 11])
            s = take(pe, "V", "modT")
            for j in range(48):
                m = pe.transpose(slot(s)[:, 2 * j:2 * j + 2], mrow[:, j * P:(j + 1) * P], K("ident", 0, 2, 2))
            Tn(m.then_inc(tensor_done, 1), "modT")

            w = weights(pe, "z")
            for o in range(4):
                s = take(pe, "S", "z", o)
                if o == 0:
                    pe.wait_ge(scalar_done, Sc["h", "n1", KD - 1])
                m = Tn(dense(pe, s, [w[:, k, o * P:(o + 1) * P] for k in range(KD)], hk).then_inc(tensor_done, 1), "z", o)
            w_used()
            for o in range(6):
                if o % 4 == 0:
                    w = weights(pe, "xbc", o // 4)
                s = take(pe, "V", "conv", "xbc", o)
                Tn(dense(pe, s, [w[:, k, (o % 4) * P:(o % 4 + 1) * P] for k in range(KD)], hk)
                   .then_inc(tensor_done, 1), "conv", "xbc", o)
                if o == 3:
                    w_used()
            s = take(pe, "S", "dt_row")
            for k in range(KD):
                pe.matmul(tokens(s)[0:16, 0:LP], w[:, k, 256:272], hT[:, k, 0:LP], start=k == 0, stop=k == KD - 1)
                m = pe.matmul(tokens(s)[0:16, LP:T], w[:, k, 256:272], hT[:, k, LP:T], start=k == 0, stop=k == KD - 1)
            Tn(m.then_inc(tensor_done, 1), "dt_row")
            w_used()
            s = take(pe, "V", "dt_tok")
            pe.wait_ge(scalar_done, Sc["dt_row"])
            for c in range(NT):
                m = pe.transpose(slot(s)[:, 16 * c:16 * c + 16], dt_row[:, c * P:(c + 1) * P], K("ident", 0, 16, 16))
            Tn(m.then_inc(tensor_done, 1), "dt_tok")
            pe.wait_ge(state_in, 64)
            s = take(pe, "V", "H0")
            for i in range(8):
                m = pe.transpose(slot(s)[:, 64 * i:64 * i + 64], init_rows[:, 128 * i:128 * (i + 1)], K("ident", 0, 64, 64))
            Tn(m.then_inc(tensor_done, 1), "H0")
            pe.wait_ge(scalar_done, Sc["xbc", 5])
            for c in range(NT):
                s = take(pe, "V", "x_tok", c)
                for o in range(5):
                    m = pe.transpose(slot(s)[:, 128 * o:128 * (o + 1)], xbc[:, o, c * P:(c + 1) * P], K("ident"))
                Tn(m.then_inc(tensor_done, 1), "x_tok", c)
            pe.wait_ge(vector_done, Vc["dA"])
            s = take(pe, "S", "decays")
            for r, tri in enumerate(("t_gt_j", "t_lt_j")):
                pe.matmul(slot(s)[:, 40 * r:40 * r + 40].rearrange("p (c h) -> p c h", c=NT), K(tri),
                          dA[:, :, 8 * r:8 * r + 8], start=True, stop=True)
            dAg = dA.rearrange("p c (r g h) -> p c r g h", r=2, g=2)
            for g in range(2):
                for r in range(2):
                    m = pe.matmul(slot(s)[64 * g:64 * g + 64, 512 + 20 * r:532 + 20 * r].rearrange("p (c h) -> p c h", c=NT),
                                  K("ones", 0, 64), dAg[:, :, r, g, :], start=True, stop=True)
            Tn(m.then_inc(tensor_done, 1), "decays")
            for i, (c, r) in enumerate(CHAIN):
                pe.wait_ge(vector_done, Vc["xw", c, r])
                s = take(pe, "V", "state", c, r)
                for g in range(2):
                    m = pe.matmul(slot(s)[64 * g:64 * g + 64, 0:256], B_tok[:, c, 64 * g:64 * g + 64],
                                  xw[i % 2][:, 256 * g:256 * g + 256], start=True, stop=True)
                Tn(m.then_inc(tensor_done, 1), "state", c, r)
            s = take(pe, "V", "end_rows")
            for r in range(2):
                for hh in range(4):
                    m = pe.transpose(slot(s)[0:64, 512 * r + 128 * hh:512 * r + 128 * hh + 128],
                                     H_end[:, r, 64 * hh:64 * hh + 64], K("ident"))
            Tn(m.then_inc(tensor_done, 1), "end_rows")

            def decay_sums(c, r):
                pe.wait_ge(pool_done, Gp["dA_tri", c, r])
                s = take(pe, "S", "seg", c, r)
                for half in range(2):
                    m = pe.matmul(slot(s)[:, 512 * half:512 * half + 512], K(("t_gt_j", "t_lt_j")[r]),
                                  dA_tri[:, r, 512 * half:512 * half + 512], start=True, stop=True)
                Tn(m.then_inc(tensor_done, 1), "seg", c, r)
                if c >= 1:
                    s = take(pe, "S", "acc", c, r)
                    for g in range(2):
                        m = pe.matmul(slot(s)[64 * g:64 * g + 64, 0:512], K("ones", 0, 64),
                                      dA_tri[:, r, 512 * g:512 * g + 512], start=True, stop=True)
                    Tn(m.then_inc(tensor_done, 1), "acc", c, r)

            def outputs(c):
                pe.wait_ge(vector_done, Vc["S", c, 1])
                s = take(pe, "V", "y", c)
                for h in range(HEADS):
                    g, hh, e = h // 4, h % 4, 64 * (h % 2)
                    at = 512 * g + 128 * (hh // 2)
                    dst = slot(s)[e:e + 64, at:at + 128]
                    last = 2 if c == 0 else 4
                    i = 0
                    for r in range(2):
                        i += 1
                        m = pe.matmul(dst, xdt[:, r, 64 * h:64 * h + 64], E_seg[:, r, 128 * h:128 * h + 128],
                                      start=i == 1, stop=i == last)
                    if c >= 1:
                        for r in range(2):
                            i += 1
                            m = pe.matmul(dst, H[64 * g:64 * g + 64, r, c - 1, 64 * hh:64 * hh + 64],
                                          C_dec[64 * g:64 * g + 64, r, 128 * hh:128 * hh + 128], start=False, stop=i == last)
                Tn(m.then_inc(tensor_done, 1), "y", c)

            for c in range(NT):
                s = take(pe, "V", "G", c)
                for g in range(2):
                    m = pe.matmul(slot(s)[:, 512 * g:512 * g + 128], BT[64 * g:64 * g + 64, c * P:(c + 1) * P],
                                  CT[64 * g:64 * g + 64, c * P:(c + 1) * P], start=True, stop=True)
                Tn(m.then_inc(tensor_done, 1), "G", c)
                for r in range(2):
                    decay_sums(c, r)
                outputs(c)
            channel_sum(pe, "ssm", 4)

            def hidden(name, lhs, rhs):
                s = take(pe, "V", "arg", name)
                pe.matmul(tokens(s)[0:HID, 0:LP], lhs, rhs[:, 0:LP], start=True, stop=True)
                Tn(pe.matmul(tokens(s)[0:HID, LP:T], lhs, rhs[:, LP:T], start=True, stop=True)
                   .then_inc(tensor_done, 1), "arg", name)

            def filters(i):
                pe.wait_ge(vector_done, Vc["ssmY", 3])
                pe.wait_ge(w3_in, 32 * (i + 1))
                pe.wait_ge(filt_in, 16 * 3)
                hidden((i, 1), w1sb, feat)
                pe.wait_ge(scalar_done, Sc["hid", i, 1])
                hidden((i, 2), w2sb, hid1)
                pe.wait_ge(scalar_done, Sc["hid", i, 2])
                for c in range(NT):
                    s = take(pe, "V", "filt", i, c)
                    for r in range(2):
                        m = pe.matmul(slot(s)[:, 512 * r:512 * r + 512], hid2[:, c * P:(c + 1) * P],
                                      w3[:, 512 * r:512 * r + 512], start=True, stop=True)
                    Tn(m.then_inc(tensor_done, 1), "filt", i, c)

            def transform(name, i, cos_rhs, sin_rhs, engine, nyquist):
                for q in range(NT):
                    tail, k, toks = ("_p", 0, [0]) if q == 0 else ("", q - 1, [1, 2, 3, 4])
                    s = take(pe, engine, name, i, q)
                    for r, rhs in enumerate((cos_rhs, sin_rhs)):
                        for j, n in enumerate(toks):
                            at = (0 if q == 0 else LS * j) + k * P
                            m = pe.matmul(slot(s)[:, 512 * r:512 * r + 512], K(("dft_c", "dft_s")[r] + tail, at, at + P),
                                          rhs[:, n, :], start=j == 0, stop=j == len(toks) - 1)
                    Tn(m.then_inc(tensor_done, 1), name, i, q)
                    if nyquist and q <= 1:
                        s = take(pe, engine, name + "n", i, q)
                        for j, n in enumerate(toks):
                            at = 0 if q == 0 else LS * j
                            m = pe.matmul(slot(s)[0:1, 0:512], K("dft_s" + tail, at, at + 1), cos_rhs[:, n, :],
                                          start=j == 0, stop=j == len(toks) - 1)
                        Tn(m.then_inc(tensor_done, 1), name + "n", i, q)

            def hy_project(b, place, after):
                w = weights(pe, "hy", b)
                for o in range(4):
                    s = take(pe, "V", "conv", "hy", 4 * b + o)
                    Tn(dense(pe, s, [w[:, k, o * P:(o + 1) * P] for k in range(KD)], hk).then_inc(tensor_done, 1),
                       "conv", "hy", 4 * b + o)
                    if o == 3:
                        w_used()
                    if b < 2:
                        if o >= 1:
                            turn(b, o - 1)
                if b < 2:
                    turn(b, 3)

            def turn(b, o):
                pe.wait_ge(vector_done, Vc["conv4", "hy", 4 * b + o])
                s = take(pe, "S", "turn", b, o)
                for c in range(NT):
                    m = pe.transpose(tokens(s)[:, c * P:(c + 1) * P], conv_raw[o % 2][:, c * P:(c + 1) * P], K("ident"))
                Tn(m.then_inc(tensor_done, 1), "turn", b, o)

            filters(0)
            for b in range(2):
                hy_project(b, None, None)
            pe.wait_ge(vector_done, Vc["fsum", 0, 4])
            transform("K", 0, fsum, fdif, "S", True)
            pe.wait_ge(scalar_done, Sc["turn", 0, 3])
            transform("U", 0, v_tok, v_tok, "V", False)
            for c in range(NT):
                pe.wait_ge(vector_done, Vc["Y", 0, 0 if c == 0 else 4])
                s = take(pe, "V", "z1", c)
                for j, q in enumerate([0] if c == 0 else [1, 2, 3, 4]):
                    tail, at = ("_p", 0) if c == 0 else ("", LS * j + (c - 1) * P)
                    n = 1 if c == 0 else 4
                    pe.matmul(slot(s)[:, 0:512], K("dft_c" + tail, at, at + P), Yr[:, q, :], start=j == 0, stop=False)
                    m = pe.matmul(slot(s)[:, 0:512], K("idft_s" + tail, at, at + P), Ys[:, q, :], start=False, stop=j == n - 1)
                Tn(m.then_inc(tensor_done, 1), "z1", c)
            filters(1)
            hy_project(2, None, None)
            pe.wait_ge(vector_done, Vc["fsum", 1, 4])
            transform("K", 1, fsum, fdif, "S", True)
            transform("U", 1, x1_tok, x1_tok, "V", False)
            pe.wait_ge(vector_done, Vc["Y", 1, 4])
            for o in range(4):
                s = take(pe, "V", "hyY", o)
                oc = slice(o * P, (o + 1) * P)
                pe.matmul(tokens(s)[:, 0:LP], Yr[:, 0, oc], K("dft_c_p"), start=True, stop=False)
                pe.matmul(tokens(s)[:, 0:LP], Ys[:, 0, oc], K("idft_s_p"), start=False, stop=True)
                for q in range(4):
                    pe.matmul(tokens(s)[:, LP:T], Yr[:, 1 + q, oc], K("dft_c", LS * q, LS * (q + 1)), start=q == 0, stop=False)
                    m = pe.matmul(tokens(s)[:, LP:T], Ys[:, 1 + q, oc], K("idft_s", LS * q, LS * (q + 1)), start=False, stop=q == 3)
                Tn(m.then_inc(tensor_done, 1), "hyY", o)

            w = weights(pe, "q")
            for o in range(4):
                s = take(pe, "S", "q", o)
                if o == 0:
                    pe.wait_ge(vector_done, Vc["hyY", 3])
                Tn(dense(pe, s, [w[:, k, o * P:(o + 1) * P] for k in range(KD)], hk).then_inc(tensor_done, 1), "q", o)
            w_used()
            w = weights(pe, "kv")
            s = take(pe, "S", "q", 4)
            Tn(dense(pe, s, [w[:, k, 0:P] for k in range(KD)], hk).then_inc(tensor_done, 1), "q", 4)
            s = take(pe, "S", "v")
            for c in range(NT):
                for k in range(KD):
                    m = pe.matmul(tokens(s)[:, c * P:(c + 1) * P], hT[:, k, c * P:(c + 1) * P], w[:, k, P:2 * P],
                                  start=k == 0, stop=k == KD - 1)
            Tn(m.then_inc(tensor_done, 1), "v")
            w_used()
            for o in range(5):
                s = take(pe, "V", "rot", o)
                pe.wait_ge(scalar_done, Sc["q", o])
                src = (qT[:, o, :] if o < 4 else kT)
                Tn(pe.matmul(slot(s)[:, 0:512], K("rotate"), src[:, LP:T], start=True, stop=True)
                   .then_inc(tensor_done, 1), "rot", o)
            pe.wait_ge(cache_in, 32)
            s = take(pe, "S", "kcT")
            pe.transpose(slot(s)[:, 0:P], kc_rows, K("ident"))
            Tn(pe.transpose(slot(s)[:, 512:640], kT[:, 0:P], K("ident")).then_inc(tensor_done, 1), "kcT")

            def scores(n):
                b, t = UNITS[n]
                s = take(pe, "V", "max", n)
                for g in range(2):
                    q = qT[64 * g:64 * g + 64, t, b * P:(b + 1) * P]
                    if b == 0:
                        m = pe.matmul(slot(s)[:, 512 * g:512 * g + 128], q, kT[64 * g:64 * g + 64, 0:P], start=True, stop=True)
                    else:
                        lo, hi = max(1, b - 1), min(NT, b + 2)
                        pe.matmul(slot(s)[:, 512 * g:512 * g + 128], q, kcT[64 * g:64 * g + 64, :], start=True, stop=True)
                        m = pe.matmul(slot(s)[:, 512 * g + 128:512 * g + 128 + (hi - lo) * P], q,
                                      kT[64 * g:64 * g + 64, lo * P:hi * P], start=True, stop=True)
                Tn(m.then_inc(tensor_done, 1), "scores", n)

            def turn_probs(n):
                b, t = UNITS[n]
                pe.wait_ge(vector_done, Vc["probs", n])
                s = take(pe, "S", "PT", n)
                for g in range(2):
                    for j in range(n_keys(b)):
                        m = pe.transpose(slot(s)[:, 512 * g + 128 * j:512 * g + 128 * (j + 1)],
                                         S_sb[n % 3][:, g, 128 * j:128 * (j + 1)], K("ident"))
                Tn(m.then_inc(tensor_done, 1), "PT", n)

            def values(n):
                b, t = UNITS[n]
                pe.wait_ge(scalar_done, Sc["PT", n])
                s = take(pe, "V", "att", n)
                kt = key_tiles(b)
                for g in range(2):
                    for j, c in enumerate(kt):
                        v = v_ctx if c < 0 else v_att[:, c, :]
                        m = pe.matmul(slot(s)[64 * g:64 * g + 64, 0:128], v[:, 64 * g:64 * g + 64],
                                      PT_sb[n % 3][:, g, 128 * j:128 * (j + 1)], start=j == 0, stop=j == len(kt) - 1)
                Tn(m.then_inc(tensor_done, 1), "att", n)

            pe.wait_ge(vector_done, Vc["rope", 4])
            pe.wait_ge(scalar_done, Sc["kcT"])
            for n in range(len(UNITS) + 2):
                if n < len(UNITS):
                    scores(n)
                if 1 <= n <= len(UNITS):
                    turn_probs(n - 1)
                if n >= 2:
                    values(n - 2)

            for og in range(2):
                for b, y in enumerate((hyY, ssmY, attY)):
                    wg = weights(pe, "gate", og, b)
                    wp = weights(pe, "proj", og, b)
                    for o in range(4):
                        s = take(pe, "S", "gate", og, b, o)
                        Tn(dense(pe, s, [wg[:, k, o * P:(o + 1) * P] for k in range(KD)], hk)
                           .then_inc(tensor_done, 1), "gate", og, b, o)
                        if b == 2 and og == 0 and o == 0:
                            pe.wait_ge(vector_done, Vc["att", len(UNITS) - 1])
                        s = take(pe, "V", "proj", og, b, o)
                        Tn(dense(pe, s, [wp[:, k, o * P:(o + 1) * P] for k in range(4)], [y[:, k, :] for k in range(4)])
                           .then_inc(tensor_done, 1), "proj", og, b, o)
                    w_used(2)
            pe.wait_ge(pool_done, Gp["merged", 7, 2])
            for og in range(2):
                w = weights(pe, "out", og)
                for o in range(4):
                    s = take(pe, "S", "mix", 0, 4 * og + o)
                    Tn(dense(pe, s, [w[:, k, o * P:(o + 1) * P] for k in range(KD)], [merged[:, k, :] for k in range(KD)])
                       .then_inc(tensor_done, 1), "mix", 0, 4 * og + o)
                w_used()
            channel_sum(pe, "p1", KD)
            norm_sum(pe, "n2")

            for j, (lo, wid) in enumerate(FB):
                wg, wu = weights(pe, "up", 0, j), weights(pe, "up", 1, j)
                if j == 0:
                    pe.wait_ge(scalar_done, Sc["h", "n2", KD - 1])
                for o in range(wid // P):
                    f = lo // P + o
                    s = take(pe, "S", "fgate", f)
                    Tn(dense(pe, s, [wg[:, k, o * P:(o + 1) * P] for k in range(KD)], hk).then_inc(tensor_done, 1), "fgate", f)
                    s = take(pe, "V", "fup", f)
                    Tn(dense(pe, s, [wu[:, k, o * P:(o + 1) * P] for k in range(KD)], hk).then_inc(tensor_done, 1), "fup", f)
                w_used(2)
            pe.wait_ge(vector_done, Vc["fup", KF - 1])
            for oc in range(4):
                ss = [take(pe, "S", "mix", 1, 2 * oc + o) for o in range(2)]
                for half in range(2):
                    w = weights(pe, "down", oc, half)
                    for o in range(2):
                        for k in range(KH):
                            a, z = half == 0 and k == 0, half == 1 and k == KH - 1
                            lhs, rhs = w[:, k, o * P:(o + 1) * P], act[:, half * KH + k, :]
                            pe.matmul(tokens(ss[o])[:, 0:LP], lhs, rhs[:, 0:LP], start=a, stop=z)
                            m = pe.matmul(tokens(ss[o])[:, LP:T], lhs, rhs[:, LP:T], start=a, stop=z)
                        Tn(m.then_inc(tensor_done, 1), "mix" if half else "half", 1, 2 * oc + o)
                    w_used()
            channel_sum(pe, "p2", KD)

        @block.vector
        def _(dve):
            dve.wait_ge(tensor_done, Tn["pcol"])
            s = used("pcol")
            Vc(dve.tensor_copy(pcol[:, :], slot(s)[:, 0:N_ROWS]).then_inc(vector_done, 1))
            Vc(dve.tensor_copy(bcol[:, 0:48], slot(s)[:, 512:560]).then_inc(vector_done, 1), "pcol")
            dve.wait_ge(tensor_done, Tn["bcol"])
            Vc(dve.tensor_copy(bcol[0:HID, 48:52], slot(used("bcol"))[0:HID, 0:4]).then_inc(vector_done, 1), "bcol")
            dve.wait_ge(tensor_done, Tn["condT"])
            Vc(dve.tensor_copy(condT[:, :], slot(used("condT"))[:, 0:16]).then_inc(vector_done, 1), "condT")
            dve.wait_ge(rowvec_in, 16 * 4)
            for e in range(2):
                half = slice(64 * e, 64 * e + 64)
                Vc(dve.tensor_tensor(dskip[half, :], dskip2[half, e:8:2], dskip2[half, 8 + e:16:2], ALU.add)
                   .then_inc(vector_done, 1), "dskip")
            dve.wait_ge(scalar_done, Sc["exp_a"])
            Vc(dve.tensor_scalar(neg_a[:, :], neg_a[:, :], -1.0, None, ALU.mult).then_inc(vector_done, 1), "neg_a")
            norm_apply(dve, "n1")
            dve.wait_ge(tensor_done, Tn["modT"])
            ada_b = bcol[:, 0:48].unsqueeze(2).broadcast_to([P, 48, 2])
            Vc(dve.tensor_tensor(modT[:, :, :], slot(used("modT"))[:, 0:96].rearrange("p (n c) -> p n c", c=2), ada_b, ALU.add)
               .then_inc(vector_done, 1), "modT")
            dve.wait_ge(vector_done, Vc["modT"])
            for i in range(2):
                pre = row(("mix_pre", "ffn_pre")[i], 0, 8).unsqueeze(2).broadcast_to([P, 8, 2])
                post = row(("mix_post", "ffn_post")[i], 0, 8).unsqueeze(2).broadcast_to([P, 8, 2])
                Vc(dve.scalar_tensor_tensor(out=scale_pre[:, i], in0=modT[:, 24 * i + 8:24 * i + 16, :], scalar=1.0, in1=pre,
                                            op0=ALU.add, op1=ALU.mult).then_inc(vector_done, 1))
                Vc(dve.tensor_tensor(gain_post[:, i], modT[:, 24 * i + 16:24 * i + 24, :], post, ALU.mult)
                   .then_inc(vector_done, 1), "gains", i)

            def conv(kind, o, dst, name):
                dve.wait_ge(tensor_done, Tn["conv", kind, o])
                src = tokens(used("conv", kind, o))
                n = {"xbc": 6, "hy": 12}[kind]
                tag = {"xbc": "ssm", "hy": "hy"}[kind]
                w = [row(tag + "_w", n * j + o) for j in range(3)]
                Vc(dve.tensor_scalar(dst, src, w[1], row(tag + "_b", o), ALU.mult, ALU.add).then_inc(vector_done, 1))
                for lo, hi in ((0, LP), (LP, T)):
                    dve.wait_ge(vector_done, Vc.count)
                    Vc(dve.scalar_tensor_tensor(out=dst[:, lo + 1:hi], in0=src[:, lo:hi - 1], scalar=w[0],
                                                in1=dst[:, lo + 1:hi], op0=ALU.mult, op1=ALU.add).then_inc(vector_done, 1))
                    dve.wait_ge(vector_done, Vc.count)
                    Vc(dve.scalar_tensor_tensor(out=dst[:, lo:hi - 1], in0=src[:, lo + 1:hi], scalar=w[2],
                                                in1=dst[:, lo:hi - 1], op0=ALU.mult, op1=ALU.add).then_inc(vector_done, 1))
                Vc.named[("conv", kind, o)] = Vc.named[name] = Vc.count

            for o in range(6):
                conv("xbc", o, xbc[:, o, :], ("conv4", "xbc", o))
            dve.wait_ge(tensor_done, Tn["dt_tok"])
            raw = slot(used("dt_tok"))[:, 0:80].rearrange("p (c m) -> p c m", c=NT)
            v, e, u = sp_a, sp_b, sp_c
            v3 = v.rearrange("p (c m) -> p c m", c=NT)
            Vc(dve.tensor_tensor(v3, raw, dt_bias[:, :].unsqueeze(1).broadcast_to([P, NT, 16]), ALU.add)
               .then_inc(vector_done, 1), "dt_tok")
            dve.wait_ge(vector_done, Vc.count)
            Vc(dve.scalar_tensor_tensor(out=e, in0=v, scalar=-1.0, in1=v, op0=ALU.mult, op1=ALU.min)
               .then_inc(vector_done, 1), "dt_abs")
            dve.wait_ge(scalar_done, Sc["dt_exp"])
            Vc(dve.tensor_scalar(u, e, 1.0, None, ALU.add).then_inc(vector_done, 1), "dt_u")
            dve.wait_ge(vector_done, Vc.count)
            flat = dts.rearrange("p c m -> p (c m)")
            dAf = dA.rearrange("p c m -> p (c m)")
            Vc(dve.scalar_tensor_tensor(out=e, in0=u, scalar=-1.0, in1=e, op0=ALU.add, op1=ALU.subtract)
               .then_inc(vector_done, 1))
            Vc(dve.reciprocal(dAf, u).then_inc(vector_done, 1), "u_inverse")
            dve.wait_ge(vector_done, Vc.count)
            Vc(dve.tensor_tensor(e, e, dAf, ALU.mult).then_inc(vector_done, 1))
            dve.wait_ge(vector_done, Vc.count)
            Vc(dve.scalar_tensor_tensor(out=flat, in0=v, scalar=0.0, in1=e, op0=ALU.max, op1=ALU.subtract)
               .then_inc(vector_done, 1))
            dve.wait_ge(vector_done, Vc.count)
            dve.wait_ge(scalar_done, Sc["dt_ln"])
            Vc(dve.tensor_tensor(flat, flat, u, ALU.add).then_inc(vector_done, 1))
            dve.wait_ge(vector_done, Vc.count)
            Vc(dve.tensor_tensor(dA, dts, neg_a[:, :].unsqueeze(1).broadcast_to([P, NT, 16]), ALU.mult)
               .then_inc(vector_done, 1), "dA")
            dve.wait_ge(tensor_done, Tn["H0"])
            h0 = slot(used("H0"))[:, 0:512].rearrange("p (r n) -> p r n", r=2)
            Vc(dve.tensor_copy(H[:, 0, 0, :], h0[:, 0, :]).then_inc(vector_done, 1))
            Vc(dve.tensor_copy(H[:, 1, 3, :], h0[:, 1, :]).then_inc(vector_done, 1), "H0")
            for c in range(NT):
                dve.wait_ge(tensor_done, Tn["x_tok", c])
                s = used("x_tok", c)
                Vc(dve.tensor_copy(x_tok[:, c, :], slot(s)[:, 0:512]).then_inc(vector_done, 1))
                Vc(dve.tensor_copy(B_tok[:, c, :], slot(s)[:, 512:640]).then_inc(vector_done, 1), "x_tok", c)
            for o in range(4):
                Vc(dve.tensor_scalar(xskip[:, o, :], xskip[:, o, :], dskip[:, o:o + 1], None, ALU.mult)
                   .then_inc(vector_done, 1), "xskip", o)

            def heads(x):
                return x.rearrange("p (h n) -> p h n", h=HEADS)

            def dt_of(c, r):
                return dts[:, c, 8 * r:8 * r + 8].unsqueeze(2).broadcast_to([P, HEADS, HD])

            dve.wait_ge(scalar_done, Sc["decays"])

            def weighted(i):
                c, r = CHAIN[i]
                xwi = heads(xw[i % 2])
                Vc(dve.tensor_tensor(xwi, heads(x_tok[:, c, :]), dt_of(c, r), ALU.mult).then_inc(vector_done, 1))
                dve.wait_ge(vector_done, Vc.count)
                Vc(dve.tensor_tensor(xwi, xwi, w_end[:, r, c, :].unsqueeze(2).broadcast_to([P, HEADS, HD]), ALU.mult)
                   .then_inc(vector_done, 1), "xw", c, r)

            weighted(0)
            for i, (c, r) in enumerate(CHAIN):
                if i + 1 < len(CHAIN):
                    weighted(i + 1)
                dve.wait_ge(tensor_done, Tn["state", c, r])
                got = slot(used("state", c, r))[:, 0:256]
                if c == 0:
                    Vc(dve.tensor_copy(H_end[:, r, :], got).then_inc(vector_done, 1), "state", c, r)
                    continue
                to = c + 1 if r == 0 else c - 1
                dec = chunk_decay[:, c, r, :].unsqueeze(2).broadcast_to([P, 4, 64])
                Vc(dve.tensor_tensor(H[:, r, to - 1, :].rearrange("p (h n) -> p h n", h=4),
                                     H[:, r, c - 1, :].rearrange("p (h n) -> p h n", h=4), dec, ALU.mult)
                   .then_inc(vector_done, 1))
                dve.wait_ge(vector_done, Vc.count)
                Vc(dve.tensor_tensor(H[:, r, to - 1, :], H[:, r, to - 1, :], got, ALU.add)
                   .then_inc(vector_done, 1), "state", c, r)
            dve.wait_ge(tensor_done, Tn["end_rows"])
            Vc(dve.tensor_copy(end_rows, slot(used("end_rows"))[0:64, 0:1024]).then_inc(vector_done, 1), "end_rows")
            for c in range(NT):
                dve.wait_ge(tensor_done, Tn["G", c])
                s = used("G", c)
                if c >= 1:
                    dve.wait_ge(vector_done, Vc["S", c - 1, 1])
                for r, tri in enumerate(("t_le_i", "t_ge_i")):
                    for g in range(2):
                        Vc(dve.tensor_tensor(G_tri[:, r, g, :], slot(s)[:, 512 * g:512 * g + 128], K(tri), ALU.mult)
                           .then_inc(vector_done, 1), "G", c)
                for r in range(2):
                    if c >= 1:
                        dve.wait_ge(tensor_done, Tn["y", c - 1])
                    Vc(dve.tensor_tensor(heads(xdt[:, r, :]), heads(x_tok[:, c, :]), dt_of(c, r), ALU.mult).then_inc(vector_done, 1))
                for r in range(2):
                    dve.wait_ge(scalar_done, Sc["acc" if c else "seg", c, r])
                    if c:
                        cb = CT[:, c * P:(c + 1) * P].unsqueeze(1).broadcast_to([P, 4, P])
                        Vc(dve.tensor_tensor(C_dec[:, r, :].rearrange("p (h n) -> p h n", h=4),
                                             E_acc[:, r, :].rearrange("p (h n) -> p h n", h=4), cb, ALU.mult)
                           .then_inc(vector_done, 1))
                    dve.wait_ge(vector_done, Vc["G", c])
                    for g in range(2):
                        ev = E_seg[:, r, 512 * g:512 * g + 512].rearrange("p (h n) -> p h n", h=4)
                        Vc(dve.tensor_tensor(ev, ev, G_tri[:, r, g, :].unsqueeze(1).broadcast_to([P, 4, P]), ALU.mult)
                           .then_inc(vector_done, 1), "S", c, r)
                dve.wait_ge(tensor_done, Tn["y", c])
                yv = xskip.rearrange("p (g o) n -> p g o n", g=2)[:, :, :, c * P:(c + 1) * P]
                got = slot(used("y", c)).rearrange("p (g o n) -> p g o n", g=2, o=4)[:, :, 0:2, :]
                Vc(dve.tensor_tensor(yv, yv, got, ALU.add)
                   .then_inc(vector_done, 1), "y", c)
            dve.wait_ge(vector_done, Vc.count)
            for o in range(4):
                Vc(dve.tensor_tensor(zg[:, o, :], zg[:, o, :], xskip[:, o, :], ALU.mult).then_inc(vector_done, 1), "yz", o)
            dve.wait_ge(scalar_done, Sc["rstd", "ssm"])
            for o in range(4):
                Vc(dve.scalar_tensor_tensor(out=zg[:, o, :], in0=zg[:, o, :], scalar=row("ssm_norm", o), in1=rstd,
                                            op0=ALU.mult, op1=ALU.mult).then_inc(vector_done, 1), "ssmY", o)

            def arg(i, n):
                dve.wait_ge(tensor_done, Tn["arg", (i, n)])
                h = (hid1, hid2)[n - 1]
                b, fr = bcol[0:HID, 48 + 2 * (n - 1):49 + 2 * (n - 1)], bcol[0:HID, 49 + 2 * (n - 1):50 + 2 * (n - 1)]
                Vc(dve.tensor_scalar(h, tokens(used("arg", (i, n)))[0:HID, :], b, fr, ALU.add, ALU.mult)
                   .then_inc(vector_done, 1), "arg", (i, n))
                big = 1.5 * 2.0 ** 23
                hi = float(np.float32(6.28125))
                lo = float(np.float32(TWO_PI - hi))
                pi = float(np.nextafter(np.float32(np.pi), np.float32(0)))
                dve.wait_ge(vector_done, Vc.count)
                Vc(dve.tensor_scalar(arg_k, h, float(np.float32(1 / TWO_PI)), big, ALU.mult, ALU.add).then_inc(vector_done, 1))
                dve.wait_ge(vector_done, Vc.count)
                Vc(dve.tensor_scalar(arg_k, arg_k, -big, None, ALU.add).then_inc(vector_done, 1))
                for part_ in (hi, lo):
                    dve.wait_ge(vector_done, Vc.count)
                    Vc(dve.scalar_tensor_tensor(out=h, in0=arg_k, scalar=-part_, in1=h, op0=ALU.mult, op1=ALU.add)
                       .then_inc(vector_done, 1))
                dve.wait_ge(vector_done, Vc.count)
                Vc(dve.tensor_scalar(h, h, pi, -pi, ALU.min, ALU.max).then_inc(vector_done, 1), "arg_in", i, n)

            def filters(i):
                arg(i, 1)
                arg(i, 2)
                for c in range(NT):
                    dve.wait_ge(tensor_done, Tn["filt", i, c])
                    dve.wait_ge(scalar_done, Sc["decay", i, c])
                    s = used("filt", i, c)
                    hb = hb_tmp[c % 2]
                    Vc(dve.tensor_tensor(fsum[:, c, :], fsum[:, c, :], slot(s)[:, 0:512], ALU.mult).then_inc(vector_done, 1))
                    Vc(dve.tensor_tensor(hb, hb, slot(s)[:, 512:1024], ALU.mult).then_inc(vector_done, 1), "filt", i, c)
                    dve.wait_ge(vector_done, Vc.count)
                    if c <= 1:
                        if c == 0:
                            dve.wait_ge(filt_in, 16 * (3 + i))
                        Vc(dve.tensor_tensor(fsum[0:1, c, :], fsum[0:1, c, :], bias_row, ALU.add).then_inc(vector_done, 1))
                        Vc(dve.memset(hb[0:1, :], 0.0).then_inc(vector_done, 1), "bias", i, c)
                        dve.wait_ge(vector_done, Vc.count)
                    Vc(dve.tensor_tensor(fdif[:, c, :], fsum[:, c, :], hb, ALU.subtract).then_inc(vector_done, 1))
                    dve.wait_ge(vector_done, Vc.count)
                    Vc(dve.tensor_tensor(fsum[:, c, :], fsum[:, c, :], hb, ALU.add).then_inc(vector_done, 1), "fsum", i, c)

            def spectrum(i):
                for q in range(NT):
                    dve.wait_ge(tensor_done, Tn["U", i, q])
                    if q == 0:
                        dve.wait_ge(scalar_done, Sc["Kn", i, 1])
                        dve.wait_ge(scalar_done, Sc["K", i, 4])
                    s = used("U", i, q)
                    ur, us = slot(s)[:, 0:512], slot(s)[:, 512:1024]
                    Vc(dve.tensor_tensor(Yr[:, q, :], ur, Kr[:, q, :], ALU.mult).then_inc(vector_done, 1))
                    if q:
                        dve.wait_ge(vector_done, Vc["Y", i, q - 1])
                    elif i == 1:
                        pass
                    Vc(dve.tensor_tensor(prod_a, us, Ks[:, q, :], ALU.mult).then_inc(vector_done, 1))
                    Vc(dve.tensor_tensor(Ys[:, q, :], ur, Ks[:, q, :], ALU.mult).then_inc(vector_done, 1))
                    Vc(dve.tensor_tensor(prod_b, us, Kr[:, q, :], ALU.mult).then_inc(vector_done, 1))
                    dve.wait_ge(vector_done, Vc.count)
                    Vc(dve.tensor_tensor(Yr[:, q, :], Yr[:, q, :], prod_a, ALU.subtract).then_inc(vector_done, 1))
                    Vc(dve.tensor_tensor(Ys[:, q, :], Ys[:, q, :], prod_b, ALU.add).then_inc(vector_done, 1), "Y", i, q)
                    if q <= 1:
                        dve.wait_ge(vector_done, Vc.count)
                        Vc(dve.tensor_tensor(Yr[0:1, q, :], ur[0:1, :], Kr[0:1, q, :], ALU.mult).then_inc(vector_done, 1))
                        Vc(dve.tensor_tensor(Ys[0:1, q, :], us[0:1, :], Ks[0:1, q, :], ALU.mult)
                           .then_inc(vector_done, 1), "Y", i, q)
                    Vc.named[("U", i, q)] = Vc.count

            filters(0)
            for b in range(2):
                for o in range(4):
                    if 4 * b + o >= 2:
                        dve.wait_ge(tensor_done, Tn["turn", (4 * b + o - 2) // 4, (o - 2) % 4])
                    conv("hy", 4 * b + o, conv_raw[o % 2], ("conv4", "hy", 4 * b + o))
            spectrum(0)
            for c in range(NT):
                dve.wait_ge(tensor_done, Tn["z1", c])
                if c == 0:
                    dve.wait_ge(scalar_done, Sc["turn", 1, 3])
                Vc(dve.tensor_tensor(x1_tok[:, c, :], x1_tok[:, c, :], slot(used("z1", c))[:, 0:512], ALU.mult)
                   .then_inc(vector_done, 1), "z1", c)
            filters(1)
            for o in range(4):
                conv("hy", 8 + o, x2T[:, o, :], ("conv4", "hy", 8 + o))
            spectrum(1)
            dve.wait_ge(vector_done, Vc.count)
            for o in range(4):
                dve.wait_ge(tensor_done, Tn["hyY", o])
                Vc(dve.tensor_tensor(hyY[:, o, :], x2T[:, o, :], tokens(used("hyY", o)), ALU.mult)
                   .then_inc(vector_done, 1), "hyY", o)

            for o in range(5):
                x = (qT[:, o, :] if o < 4 else kT)[:, LP:T]
                dve.wait_ge(tensor_done, Tn["rot", o])
                if o >= 2:
                    dve.wait_ge(vector_done, Vc["rope", o - 2])
                Vc(dve.tensor_tensor(rot_tmp[o % 2], slot(used("rot", o))[:, 0:512], K("sin"), ALU.mult)
                   .then_inc(vector_done, 1), "rot", o)
                Vc(dve.tensor_tensor(x, x, K("cos"), ALU.mult).then_inc(vector_done, 1))
                dve.wait_ge(vector_done, Vc.count)
                Vc(dve.tensor_tensor(x, x, rot_tmp[o % 2], ALU.add).then_inc(vector_done, 1), "rope", o)

            def sink_of(n, g):
                return sinks[:, 4 * g + UNITS[n][1]:4 * g + UNITS[n][1] + 1]

            def softmax_max(n):
                b, _ = UNITS[n]
                w = n_keys(b) * P
                mask = K("mask_first") if b == 1 else K("mask")
                dve.wait_ge(tensor_done, Tn["scores", n])
                if n >= 3:
                    dve.wait_ge(tensor_done, Tn["PT", n - 3])
                for g in range(2):
                    Vc(dve.tensor_tensor_reduce(out=S_sb[n % 3][:, g, 0:w], in0=slot(used("max", n))[:, 512 * g:512 * g + w],
                                                in1=mask[:, 0:w], scale=HD ** -0.5, scalar=sink_of(n, g), op0=ALU.add,
                                                op1=ALU.max, accum_out=stat[:, n, g:g + 1]).then_inc(vector_done, 1), "max", n)
                dve.wait_ge(vector_done, Vc.count)
                Vc(dve.tensor_scalar(stat[:, n, 2:4], stat[:, n, 0:2], -1.0, None, ALU.mult).then_inc(vector_done, 1))
                sk = sinks[:, UNITS[n][1]:UNITS[n][1] + 5:4]
                dve.wait_ge(vector_done, Vc.count)
                Vc(dve.tensor_tensor(stat[:, n, 4:6], sk, stat[:, n, 2:4], ALU.add).then_inc(vector_done, 1), "negmax", n)

            def softmax_scale(n):
                b, _ = UNITS[n]
                w = n_keys(b) * P
                dve.wait_ge(scalar_done, Sc["exp", n])
                Vc(dve.tensor_tensor(stat[:, n, 6:8], stat[:, n, 6:8], stat[:, n, 4:6], ALU.add).then_inc(vector_done, 1))
                dve.wait_ge(vector_done, Vc.count)
                Vc(dve.reciprocal(stat[:, n, 8:10], stat[:, n, 6:8]).then_inc(vector_done, 1))
                dve.wait_ge(vector_done, Vc.count)
                for g in range(2):
                    Vc(dve.tensor_scalar(S_sb[n % 3][:, g, 0:w], S_sb[n % 3][:, g, 0:w], stat[:, n, 8 + g:9 + g], None, ALU.mult)
                       .then_inc(vector_done, 1), "probs", n)

            def attended(n):
                b, t = UNITS[n]
                dve.wait_ge(tensor_done, Tn["att", n])
                Vc(dve.tensor_copy(attY[:, t, b * P:(b + 1) * P], slot(used("att", n))[:, 0:P]).then_inc(vector_done, 1), "att", n)

            for n in range(len(UNITS) + 2):
                if n < len(UNITS):
                    softmax_max(n)
                if n >= 2:
                    attended(n - 2)
                if n < len(UNITS):
                    softmax_scale(n)

            i = 0
            for og in range(2):
                for b in range(3):
                    for o in range(4):
                        m, g = 4 * og + o, (12 * og + 4 * b + o)
                        dve.wait_ge(tensor_done, Tn["proj", og, b, o])
                        dve.wait_ge(scalar_done, Sc["gate", og, b, o])
                        if b == 0:
                            dst = merged[:, m, :]
                        else:
                            dst = part[i % 3]
                            if i >= 3:
                                dve.wait_ge(pool_done, Gp["part", i - 3])
                            i += 1
                        if g == 0:
                            dve.wait_ge(scalar_done, Sc["PT", len(UNITS) - 1])
                            dve.wait_ge(kv_out, 32)
                        Vc(dve.tensor_tensor(dst, sig[g % 4], tokens(used("proj", og, b, o)), ALU.mult)
                           .then_inc(vector_done, 1), "proj", og, b, o)
            post_norm(dve, 0, mix, "p1")
            norm_apply(dve, "n2")
            for f in range(KF):
                dve.wait_ge(tensor_done, Tn["fup", f])
                dve.wait_ge(scalar_done, Sc["fgate", f])
                Vc(dve.tensor_tensor(act[:, f, :], ffn_gate[f % 2], tokens(used("fup", f)), ALU.mult)
                   .then_inc(vector_done, 1), "fup", f)
            post_norm(dve, 1, mix2, "p2")

        @block.scalar
        def _(sc):
            sc.wait_ge(cond_in, 32)
            Sc(sc.activation(crow[0:16, :], crow[0:16, :], ACT.Silu).then_inc(scalar_done, 1), "cond")
            sc.wait_ge(rowvec_in, 16 * 4)
            Sc(sc.activation(neg_a[:, :], neg_a[:, :], ACT.Exp).then_inc(scalar_done, 1), "exp_a")
            for j in range(12):
                sc.wait_ge(tensor_done, Tn["mrow", j])
                Sc(sc.copy(mrow[:, 512 * j:512 * (j + 1)], slot(used("mrow", j))[0:2, 0:512]).then_inc(scalar_done, 1), "mrow", j)
            pre_norm(sc, 0, "n1")
            for o in range(4):
                sc.wait_ge(tensor_done, Tn["z", o])
                Sc(sc.activation(zg[:, o, :], tokens(used("z", o)), ACT.Silu).then_inc(scalar_done, 1), "z", o)
            for o in range(6):
                sc.wait_ge(vector_done, Vc["conv4", "xbc", o])
                Sc(sc.activation(xbc[:, o, :], xbc[:, o, :], ACT.Silu).then_inc(scalar_done, 1), "xbc", o)
            sc.wait_ge(tensor_done, Tn["dt_row"])
            Sc(sc.copy(dt_row, tokens(used("dt_row"))[0:16, :]).then_inc(scalar_done, 1), "dt_row")
            sc.wait_ge(vector_done, Vc["dt_abs"])
            Sc(sc.activation(sp_b, sp_b, ACT.Exp).then_inc(scalar_done, 1), "dt_exp")
            sc.wait_ge(vector_done, Vc["u_inverse"])
            Sc(sc.activation(sp_c, sp_c, ACT.Ln).then_inc(scalar_done, 1), "dt_ln")
            sc.wait_ge(tensor_done, Tn["decays"])
            s = used("decays")
            Sc(sc.activation(w_end.rearrange("p r c h -> p (r c h)"), slot(s)[:, 0:80], ACT.Exp).then_inc(scalar_done, 1))
            Sc(sc.activation(chunk_decay.rearrange("p c r h -> p r c h"),
                             slot(s)[:, 512:552].rearrange("p (r c h) -> p r c h", r=2, c=NT), ACT.Exp)
               .then_inc(scalar_done, 1), "decays")
            for c in range(NT):
                for r in range(2):
                    sc.wait_ge(tensor_done, Tn["seg", c, r])
                    if c >= 1:
                        sc.wait_ge(tensor_done, Tn["y", c - 1])
                    Sc(sc.activation(E_seg[:, r, :], slot(used("seg", c, r)), ACT.Exp).then_inc(scalar_done, 1), "seg", c, r)
                    if c == 1 and r == 0:
                        sc.wait_ge(state_out, 64)
                    if c:
                        sc.wait_ge(tensor_done, Tn["acc", c, r])
                        Sc(sc.activation(E_acc[:, r, :], slot(used("acc", c, r))[:, 0:512], ACT.Exp)
                           .then_inc(scalar_done, 1), "acc", c, r)
            for o in range(4):
                sc.wait_ge(vector_done, Vc["yz", o])
                if o >= 2:
                    sc.wait_ge(tensor_done, Tn["sq", "ssm", o - 2])
                Sc(sc.activation(squares[o % 2], zg[:, o, :], ACT.Square).then_inc(scalar_done, 1), "sq", "ssm", o)
            rstd_of(sc, "ssm", 512)

            def filters(i):
                for n in (1, 2):
                    sc.wait_ge(vector_done, Vc["arg_in", i, n])
                    h = (hid1, hid2)[n - 1]
                    Sc(sc.activation(h, h, ACT.Sin).then_inc(scalar_done, 1), "hid", i, n)
                sc.wait_ge(decay_in, 32 * (i + 1))
                for c in range(NT):
                    if c >= 2:
                        sc.wait_ge(vector_done, Vc["fsum", i, c - 2])
                    Sc(sc.activation(fsum[:, c, :], decay[:, 0, :], ACT.Exp, scale=K("neg_t", c, c + 1)).then_inc(scalar_done, 1))
                    Sc(sc.activation(hb_tmp[c % 2], decay[:, 1, :], ACT.Exp, scale=K("neg_t", c, c + 1))
                       .then_inc(scalar_done, 1), "decay", i, c)

            def filter_spectrum(i):
                for q in range(NT):
                    sc.wait_ge(tensor_done, Tn["K", i, q])
                    s = used("K", i, q)
                    w = K("spec_w", q, q + 1) if q <= 1 else 1.0 / LS
                    Sc(sc.activation(Kr[:, q, :], slot(s)[:, 0:512], ACT.Identity, scale=w).then_inc(scalar_done, 1))
                    Sc(sc.activation(Ks[:, q, :], slot(s)[:, 512:1024], ACT.Identity, scale=w)
                       .then_inc(scalar_done, 1), "K", i, q)
                    if q <= 1:
                        sc.wait_ge(tensor_done, Tn["Kn", i, q])
                        sc.wait_ge(scalar_done, Sc["K", i, q])
                        Sc(sc.activation(Ks[0:1, q, :], slot(used("Kn", i, q))[0:1, 0:512], ACT.Identity,
                                         scale=0.5 / (LP if q == 0 else LS)).then_inc(scalar_done, 1), "Kn", i, q)

            filters(0)
            for b in range(2):
                for o in range(4):
                    sc.wait_ge(tensor_done, Tn["turn", b, o])
                    dst = (v_tok, x1_tok)[b][:, :, o * P:(o + 1) * P]
                    Sc(sc.copy(dst, tokens(used("turn", b, o)).rearrange("p (c n) -> p c n", c=NT)).then_inc(scalar_done, 1), "turn", b, o)
            filter_spectrum(0)
            sc.wait_ge(tensor_done, Tn["z1", NT - 1])
            filters(1)
            filter_spectrum(1)

            sc.wait_ge(tensor_done, Tn["hyY", 3])
            for o in range(5):
                sc.wait_ge(tensor_done, Tn["q", o])
                Sc(sc.copy(qT[:, o, :] if o < 4 else kT, tokens(used("q", o))).then_inc(scalar_done, 1), "q", o)
            sc.wait_ge(tensor_done, Tn["v"])
            Sc(sc.copy(v_att.rearrange("p c n -> p (c n)"), tokens(used("v"))).then_inc(scalar_done, 1), "v")
            sc.wait_ge(tensor_done, Tn["kcT"])
            s = used("kcT")
            Sc(sc.copy(k_rows, slot(s)[:, 512:640]).then_inc(scalar_done, 1), "k_rows")
            Sc(sc.copy(kcT, slot(s)[:, 0:P]).then_inc(scalar_done, 1), "kcT")

            def exps(n):
                b, _ = UNITS[n]
                w = n_keys(b) * P
                sc.wait_ge(vector_done, Vc["negmax", n])
                for g in range(2):
                    Sc(sc.activation(S_sb[n % 3][:, g, 0:w], S_sb[n % 3][:, g, 0:w], ACT.Exp, bias=stat[:, n, 2 + g:3 + g],
                                     accum_out=stat[:, n, 6 + g:7 + g]).then_inc(scalar_done, 1))
                Sc(sc.activation(stat[:, n, 4:6], stat[:, n, 4:6], ACT.Exp).then_inc(scalar_done, 1), "exp", n)

            def probs_turned(n):
                b, _ = UNITS[n]
                w = n_keys(b) * P
                sc.wait_ge(tensor_done, Tn["PT", n])
                if n >= 3:
                    sc.wait_ge(tensor_done, Tn["att", n - 3])
                src = slot(used("PT", n)).rearrange("p (g n) -> p g n", g=2)
                Sc(sc.copy(PT_sb[n % 3][:, :, 0:w], src[:, :, 0:w]).then_inc(scalar_done, 1), "PT", n)

            for n in range(len(UNITS) + 1):
                if n < len(UNITS):
                    exps(n)
                if n >= 1:
                    probs_turned(n - 1)

            for og in range(2):
                for b in range(3):
                    for o in range(4):
                        g = 12 * og + 4 * b + o
                        sc.wait_ge(tensor_done, Tn["gate", og, b, o])
                        if g >= 4:
                            q = g - 4
                            sc.wait_ge(vector_done, Vc["proj", q // 12, q % 12 // 4, q % 4])
                        else:
                            sc.wait_ge(vector_done, Vc["probs", len(UNITS) - 1])
                            sc.wait_ge(tensor_done, Tn["att", len(UNITS) - 1])
                        Sc(sc.activation(sig[g % 4], tokens(used("gate", og, b, o)), ACT.Sigmoid)
                           .then_inc(scalar_done, 1), "gate", og, b, o)
            mixed(sc, 0, mix, "p1")
            pre_norm(sc, 1, "n2")
            for f in range(KF):
                sc.wait_ge(tensor_done, Tn["fgate", f])
                if f >= 2:
                    sc.wait_ge(vector_done, Vc["fup", f - 2])
                Sc(sc.activation(ffn_gate[f % 2], tokens(used("fgate", f)), ACT.Silu).then_inc(scalar_done, 1), "fgate", f)
            mixed(sc, 1, mix2, "p2")

        @block.gpsimd
        def _(pool):
            pool.wait_ge(vector_done, Vc["dA"])
            for c in range(NT):
                for r in range(2):
                    if c >= 1:
                        pool.wait_ge(tensor_done, Tn["acc", c - 1, r] if c > 1 else Tn["seg", 0, r])
                    tri = K(("t_le_i", "t_ge_i")[r]).unsqueeze(1).broadcast_to([P, HEADS, P])
                    d = dA[:, c, 8 * r:8 * r + 8].unsqueeze(2).broadcast_to([P, HEADS, P])
                    Gp(pool.tensor_tensor(dA_tri[:, r, :].rearrange("p (h n) -> p h n", h=HEADS), tri, d, ALU.mult)
                       .then_inc(pool_done, 1), "dA_tri", c, r)
            i = 0
            for og in range(2):
                for b in (1, 2):
                    for o in range(4):
                        m = 4 * og + o
                        pool.wait_ge(vector_done, Vc["proj", og, b, o])
                        if b == 2:
                            pool.wait_ge(pool_done, Gp["merged", m, 1])
                        Gp(pool.tensor_tensor(merged[:, m, :], merged[:, m, :], part[i % 3], ALU.add).then_inc(pool_done, 1), "part", i)
                        Gp.named[("merged", m, b)] = Gp.count
                        i += 1

        @block.sync
        def _(sp):
            l = layer
            sp.dma_start(crow[0:8, :], A["c_ctx"].rearrange("(k p) -> k p", p=P)).then_inc(cond_in, 16)
            sp.dma_start(crow[8:16, :], A["c"][0].rearrange("(k p) -> k p", p=P)).then_inc(cond_in, 16)
            for name, src in (("mix_pre", "norm_mix_pre"), ("mix_post", "norm_mix_post"), ("ffn_pre", "norm_ffn_pre"),
                              ("ffn_post", "norm_ffn_post"), ("hy_b", "hy_conv_b"), ("ssm_b", "ssm_conv_b"), ("ssm_norm", "ssm_norm")):
                at, w = ROWS[name]
                sp.dma_start(prow[at:at + w, :], A[src][l].rearrange("(k p) -> k p", p=P)).then_inc(rows_in, 16)
            for name, src in (("hy_w", "hy_conv_w"), ("ssm_w", "ssm_conv_w")):
                at, w = ROWS[name]
                sp.dma_start(prow[at:at + w, :], A[src][l].rearrange("j (k p) -> (j k) p", p=P)).then_inc(rows_in, 16)
            sp.dma_start(brow[0:48, :], A["ada_b"][l].rearrange("(k p) -> k p", p=P)).then_inc(rows_in, 16)
            for j, src in enumerate(("hy_b1", "hy_freq1", "hy_b2", "hy_freq2")):
                sp.dma_start(hrow[j:j + 1, :], A[src][l].unsqueeze(0)).then_inc(hidden_in, 16)
            sp.dma_start(dt_bias[:, :], A["ssm_dt_bias"][l].rearrange("r h -> (r h)").partition_broadcast(P)).then_inc(rowvec_in, 16)
            sp.dma_start(neg_a[:, :], A["ssm_a_log"][l].rearrange("r h -> (r h)").partition_broadcast(P)).then_inc(rowvec_in, 16)
            sp.dma_start(sinks[:, :], A["attn_sink"][l].partition_broadcast(P)).then_inc(rowvec_in, 16)
            sp.dma_start(dskip2[:, :], A["ssm_d"][l].rearrange("r h -> (r h)").partition_broadcast(P)).then_inc(rowvec_in, 16)
            for r in range(2):
                for g in range(2):
                    sp.dma_start(init_rows[:, 512 * r:512 * r + 512].rearrange("p (h g n) -> p h g n", h=4, g=2)[:, :, g, :],
                                   A["state_ssm"][0, l, r, 4 * g:4 * g + 4].rearrange("h p n -> p h n")).then_inc(state_in, 16)
            sp.dma_start(w1sb, A["hy_w1"][l]).then_inc(filt_in, 16)
            sp.dma_start(w2sb, A["hy_w2"][l]).then_inc(filt_in, 16)
            sp.dma_start(bias_row, A["hy_bias"][l][0:1, :]).then_inc(filt_in, 16)

            def filter_loads(i):
                sp.dma_start(w3, A["hy_w3"][l][:, 1024 * i:1024 * (i + 1)]).then_inc(w3_in, 16)
                sp.dma_start(feat, A["feat"]).then_inc(w3_in, 16)
                for r in range(2):
                    src = A["hy_decay"][l][1024 * i + 512 * r:1024 * i + 512 * r + 512]
                    sp.dma_start(decay[:, r, :], src.partition_broadcast(P)).then_inc(decay_in, 16)

            def beside(name):
                if name == ("q",):
                    sp.wait_ge(vector_done, Vc["end_rows"])
                    for r in range(2):
                        for g in range(2):
                            sp.dma_start(O["new_ssm"][0, l, r, 4 * g:4 * g + 4].rearrange("h p n -> p h n"),
                                         end_rows[:, 512 * r:512 * r + 512].rearrange("p (h g n) -> p h g n", h=4, g=2)[:, :, g, :]
                                         ).then_inc(state_out, 16)
                    sp.wait_ge(vector_done, Vc["y", NT - 1])
                    filter_loads(0)
                elif name == ("kv",):
                    sp.wait_ge(vector_done, Vc["bias", 0, 1])
                    sp.dma_start(bias_row, A["hy_bias"][l][1:2, :]).then_inc(filt_in, 16)
                elif name == ("gate", 0, 0):
                    sp.wait_ge(vector_done, Vc["Y", 0, NT - 1])
                    filter_loads(1)
                elif name == ("proj", 0, 0):
                    sp.wait_ge(tensor_done, Tn["hyY", 3])
                    sp.dma_start(kc_rows, A["cache_k"][0, l].rearrange("s g n -> s (g n)")).then_inc(cache_in, 16)
                    sp.dma_start(v_ctx, A["cache_v"][0, l].rearrange("s g n -> s (g n)")).then_inc(cache_in, 16)
                elif name == ("proj", 0, 1):
                    sp.wait_ge(scalar_done, Sc["k_rows"])
                    sp.dma_start(O["new_k"][0, l].rearrange("s g n -> s (g n)"), k_rows).then_inc(kv_out, 16)
                    sp.dma_start(O["new_v"][0, l].rearrange("s g n -> s (g n)"), v_att[:, 0, :]).then_inc(kv_out, 16)

            for n, (name, parts) in enumerate(blocks):
                beside(name)
                if n >= RING:
                    sp.wait_ge(tensor_done, Tn["used", n - RING])
                kind, k, cols, src = parts[0]
                view, landed = ring_view(n, k, cols), weights_in[n % RING]
                if kind == "q":
                    for g in range(KV):
                        for kk in range(KD):
                            sp.dma_start(view[:, kk, :].rearrange("p (t g n) -> p t g n", t=4, g=KV)[:, :, g, :],
                                         src[kk * P:(kk + 1) * P, IN_Q + 256 * g:IN_Q + 256 * g + 256]
                                         .rearrange("p (t n) -> p t n", t=4)).then_inc(landed, 16)
                elif kind == "att":
                    og = parts[1][0]
                    for g in range(KV):
                        sp.dma_start(view[64 * g:64 * g + 64, :, :],
                                     A["attn_proj"][l][256 * g:256 * g + 256, 512 * og:512 * og + 512]
                                     .rearrange("(t p) n -> p t n", p=HD)).then_inc(landed, 16)
                else:
                    sp.dma_start(view, src).then_inc(landed, 16)
            sp.wait_ge(state_out, 64)
            sp.wait_ge(kv_out, 32)

    return {"T": Tn.named, "V": Vc.named, "S": Sc.named, "G": Gp.named}


INPUTS = ["x_prompt", "x_sample", "c", "cache_k", "cache_v", "state_ssm", "c_ctx", "ada_w", "ada_b", "norm_mix_pre",
          "norm_mix_post", "norm_ffn_pre", "norm_ffn_post", "w_in", "hy_conv_w", "hy_conv_b", "hy_w1", "hy_b1", "hy_freq1",
          "hy_w2", "hy_b2", "hy_freq2", "hy_w3", "hy_decay", "hy_bias", "ssm_conv_w", "ssm_conv_b", "ssm_a_log",
          "ssm_dt_bias", "ssm_d", "ssm_norm", "attn_sink", "hy_proj", "ssm_proj", "attn_proj", "w_out", "ffn_w_gate",
          "ffn_w_up", "ffn_w_down"]
OUTPUTS = [("y_prompt", (1, LP, D)), ("y_sample", (1, LS, D)), ("new_k", (1, DEPTH, LP, KV, HD)),
           ("new_v", (1, DEPTH, LP, KV, HD)), ("new_ssm", (1, DEPTH, 2, HEADS, HD, 64))]


def kernel(**inputs):
    import concourse.bacc as bacc
    from concourse.bass_utils import run_bass_kernel_spmd as run

    arrays = {f"in_{n}_dram": np.ascontiguousarray(inputs[n]) for n in INPUTS}
    arrays["in_consts_dram"] = constant_tables()
    arrays["in_feat_dram"] = filter_features()

    def program(known):
        nc = bacc.Bacc("TRN2", target_bir_lowering=False, num_devices=1)
        A = {n: nc.dram_tensor(f"in_{n}_dram", arrays[f"in_{n}_dram"].shape, F32, kind="ExternalInput").ap()
             for n in INPUTS + ["consts", "feat"]}
        O = {n: nc.dram_tensor(f"out_{n}_dram", shape, F32, kind="ExternalOutput").ap() for n, shape in OUTPUTS}
        return nc, build(nc, A, O, known)

    _, steps = program({})
    nc, _ = program(steps)
    r = run(nc, [arrays], core_ids=[0])
    return tuple(r.results[0][f"out_{n}_dram"] for n, _ in OUTPUTS)
```

```python
from contextlib import ExitStack
import numpy as np
import concourse.bass as bass
from concourse import mybir

ALU = mybir.AluOpType
ACT = mybir.ActivationFunctionType
F32 = mybir.dt.float32
F32R = mybir.dt.float32r

P = 128
D = 1024
DEPTH = 2
LP, LS = 128, 512
T = LP + LS
NT = T // P
KD = D // P
GRID_W = 64
HY_W = 512
BANDS = 16
FEAT = 1 + 2 * BANDS
HID = 64
HEADS, HD = 8, 64
KV = 2
WINDOW = 128
FF = 2816
KF = FF // P
EPS = 1e-6
NEG = -1.0e30
IN_HY, IN_Z, IN_XBC, IN_DT, IN_Q, IN_K, IN_V, IN_G = 0, 1536, 2048, 2816, 2832, 3344, 3472, 3600
N_IN = 6672
QT = 2
WB = KD * QT * P
RAW = 2
PARTS = 2
ADA_RING = 3
RING_SIZE = (RAW + 2 * PARTS) * WB
ADA_WB = RING_SIZE // ADA_RING
FPARTS = ((0, 8), (8, 8), (16, 6))
TWO_PI = 2.0 * np.pi

CONST = {}
_at = 0
for _n, _w in (("ident", P), ("ones", P), ("t_le_i", P), ("t_ge_i", P), ("t_gt_j", P), ("t_lt_j", P), ("rotate", P),
               ("cos", LS), ("sin", LS), ("mask", 512), ("mask_first", 384), ("dft_c_p", P), ("dft_s_p", P),
               ("idft_s_p", P), ("spec_w", 2), ("neg_t", NT), ("eps", 1),
               ("dft_c", 4 * LS), ("dft_s", 4 * LS), ("idft_s", 4 * LS)):
    CONST[_n] = (_at, _w)
    _at += _w
N_CONST = CONST["dft_c"][0]
N_DFT = _at - N_CONST


def constant_tables():
    c = np.zeros((P, N_CONST + N_DFT), np.float64)

    def put(name, a):
        at, w = CONST[name]
        c[:a.shape[0], at:at + w] = a.reshape(a.shape[0], -1)

    p, f = np.arange(P)[:, None], np.arange(P)[None]
    put("ident", (p == f) * 1.0)
    put("ones", np.ones((P, P)))
    put("t_le_i", (p <= f) * 1.0)
    put("t_ge_i", (p >= f) * 1.0)
    put("t_gt_j", (p > f) * 1.0)
    put("t_lt_j", (p < f) * 1.0)
    rot = np.zeros((P, P))
    for m in range(P):
        if m % 32 < 16:
            rot[m + 16, m] = -1.0
        else:
            rot[m - 16, m] = 1.0
    put("rotate", rot)
    nq = HD // 4
    inv = 10000.0 ** (-np.arange(nq) / nq)
    tok = np.arange(LS)
    pos = np.stack([tok // GRID_W, tok % GRID_W])
    ang = np.zeros((P, LS))
    for m in range(P):
        ang[m] = pos[(m % HD) // 32] * np.float32(inv[m % 16])
    put("cos", np.cos(ang))
    put("sin", np.sin(ang))
    before = np.where(f >= p, 0.0, NEG)
    after = np.where(f <= p, 0.0, NEG)
    zero = np.zeros((P, P))
    put("mask", np.concatenate([zero, before, zero, after], 1))
    put("mask_first", np.concatenate([zero, zero, after], 1))
    for tail, n in (("_p", LP), ("", LS)):
        i = np.arange(n)
        cosine = np.cos(np.pi * np.outer(i, i) / n)
        sine = np.sin(np.pi * np.outer(i, i) / n)
        forward, inverse = sine.copy(), sine.copy()
        forward[:, 0] = (-1.0) ** i
        inverse[0, :] = (-1.0) ** i
        lay = lambda a: a.reshape(n // P, P, n).transpose(1, 0, 2)
        put("dft_c" + tail, lay(cosine))
        put("dft_s" + tail, lay(forward))
        put("idft_s" + tail, lay(inverse))
    w = np.stack([np.full(P, 1.0 / LP), np.full(P, 1.0 / LS)], 1)
    w[0] *= 0.5
    put("spec_w", w)
    t = np.concatenate([np.arange(LP) / LP, np.arange(LS) / LS])
    put("neg_t", -t.reshape(NT, P).T)
    put("eps", np.full((P, 1), EPS))
    return c.astype(np.float32)


def filter_features():
    t = np.concatenate([np.arange(LP) / LP, np.arange(LS) / LS])
    ang = 2.0 * np.pi * t[None] * np.arange(1, BANDS + 1)[:, None]
    return np.concatenate([t[None], np.cos(ang), np.sin(ang)]).astype(np.float32)


ROWS = {}
_at = 0
for _n, _w in (("mix_pre", 8), ("mix_post", 8), ("ffn_pre", 8), ("ffn_post", 8), ("hy_w", 36), ("hy_b", 12),
               ("ssm_w", 18), ("ssm_b", 6), ("ssm_norm", 4)):
    ROWS[_n] = (_at, _w)
    _at += _w
N_ROWS = _at


class Steps:

    def __init__(self, known):
        self.known, self.named, self.count = known, {}, 0

    def __call__(self, instruction, *name):
        self.count += 1
        if name:
            self.named[name] = self.count
        return instruction

    def __getitem__(self, name):
        return self.known.get(name if isinstance(name, tuple) else (name,), 1)


def build(nc, A, O, known):
    tiles = ExitStack()
    with tiles:
        def sb(name, cols, rows=P):
            return tiles.enter_context(nc.sbuf_tensor(name, [rows, cols], F32))

        def sem(name):
            return tiles.enter_context(nc.semaphore(name))

        const = sb("const", N_CONST)

        def K(name, a=0, b=None, rows=P):
            at, w = CONST[name]
            if at >= N_CONST:
                return arena[0:rows, DFT_AT + at - N_CONST + a:DFT_AT + at - N_CONST + (w if b is None else b)]
            return const[0:rows, at + a:at + (w if b is None else b)]

        def tiled(t, base, n, w=T):
            return t[:, base:base + n * w].rearrange("p (n w) -> p n w", n=n)

        def sb_and_parts(name, cols):
            buffer = sb(name, cols)
            return buffer, nc.alloc_sbuf_tensor_at(name + "_parts", [P, cols], F32R, offset=nc.sbuf_base - 4 * cols)

        xT = tiled(sb("residual", KD * T), 0, KD)
        normed, normed_parts = sb_and_parts("normed", KD * T)
        hT = tiled(normed, 0, KD)
        ring, ring_parts = sb_and_parts("weights", RING_SIZE)
        pcol = sb("param_cols", N_ROWS)
        bcol = sb("bias_cols", 52)
        modT = sb("modulation", 96)[:, :].rearrange("p (n c) -> p n c", c=2)
        scale_pre = sb("scale_pre", 32)[:, :].rearrange("p (s n c) -> p s n c", s=2, c=2)
        gain_post = sb("gain_post", 32)[:, :].rearrange("p (s n c) -> p s n c", s=2, c=2)
        condT = sb("cond", 16)
        dt_bias = sb("dt_bias", 16)
        neg_a = sb("neg_a", 16)
        dskip2 = sb("dskip2", 16)
        dskip = sb("dskip", 4)
        sinks = sb("sinks", 8)
        hy_bias = sb("hy_bias", 1, 1)
        DFT_AT = 20760
        arena, arena_parts = sb_and_parts("arena", DFT_AT + N_DFT)
        ps = tiles.enter_context(nc.psum_tensor("ps", [P, 4 * 1024], F32))

        tensor_done, vector_done = sem("tensor_done"), sem("vector_done")
        scalar_done, pool_done = sem("scalar_done"), sem("pool_done")
        weights_in = [sem(f"weights_in{i}") for i in range(RAW)]
        ada_in = [sem(f"ada_in{i}") for i in range(ADA_RING)]
        dft_in = sem("dft_in")
        const_in, x_in, y_out = sem("const_in"), sem("x_in"), sem("y_out")
        cond_in, rows_in, rowvec_in, filt_in = sem("cond_in"), sem("rows_in"), sem("rowvec_in"), sem("filt_in")
        decay_in, w3_in, state_in, cache_in = sem("decay_in"), sem("w3_in"), sem("state_in"), sem("cache_in")
        state_out, kv_out, hidden_in = sem("state_out"), sem("kv_out"), sem("hidden_in")
        layer_sems = [tensor_done, vector_done, scalar_done, pool_done, *weights_in, *ada_in, dft_in, cond_in, rows_in,
                      rowvec_in, filt_in, decay_in, w3_in, state_in, cache_in, state_out, kv_out, hidden_in]

        def new_steps():
            return [Steps(known.get(e, {})) for e in "TVSG"]

        def slot(s):
            return ps[:, 1024 * s:1024 * s + 1024]

        def tokens(s):
            return ps[:, 1024 * s + 512 - T // 2:1024 * s + 512 + T // 2]

        def token_tiles(s):
            return ps[:, 1024 * s + 384:1024 * s + 1024]

        xrows = arena[:, 0:NT * D].rearrange("p (n d) -> p n d", d=D)
        with nc.Block() as block:
            Tn, Vc, Sc, Gp = new_steps()

            @block.sync
            def _(sp):
                sp.dma_start(const[:, :], A["consts"][:, 0:N_CONST]).then_inc(const_in, 16)
                sp.dma_start(xrows[:, 0, :], A["x_prompt"][0]).then_inc(x_in, 16)
                sp.dma_start(xrows[:, 1:NT, :], A["x_sample"][0].rearrange("(n p) d -> p n d", p=P)).then_inc(x_in, 16)

            @block.tensor
            def _(pe):
                pe.wait_ge(const_in, 16)
                pe.wait_ge(x_in, 32)
                for k in range(KD):
                    if k >= 4:
                        pe.wait_ge(vector_done, k - 3)
                    for n in range(NT):
                        t = pe.transpose(token_tiles(k % 4)[:, n * P:(n + 1) * P], xrows[:, n, k * P:(k + 1) * P], K("ident"))
                    t.then_inc(tensor_done, 1)

            @block.vector
            def _(dve):
                for k in range(KD):
                    dve.wait_ge(tensor_done, k + 1)
                    dve.tensor_copy(xT[:, k, :], token_tiles(k % 4)).then_inc(vector_done, 1)

        nc.sync.sem_clear(tensor_done)
        nc.sync.sem_clear(vector_done)
        nc.all_engine_barrier()

        with nc.Fori(0, DEPTH) as layer:
            named = layer_body(nc, A, O, known, layer, locals())
            for s in layer_sems:
                nc.sync.sem_clear(s)
            nc.all_engine_barrier()

        with nc.Block() as block:
            @block.tensor
            def _(pe):
                for n in range(NT):
                    if n >= 4:
                        pe.wait_ge(vector_done, n - 3)
                    for k in range(KD):
                        t = pe.transpose(slot(n % 4)[:, k * P:(k + 1) * P], xT[:, k, n * P:(n + 1) * P], K("ident"))
                    t.then_inc(tensor_done, 1)

            @block.vector
            def _(dve):
                for n in range(NT):
                    dve.wait_ge(tensor_done, n + 1)
                    dve.tensor_copy(xrows[:, n, :], slot(n % 4)).then_inc(vector_done, 1)

            @block.sync
            def _(sp):
                for n in range(NT):
                    sp.wait_ge(vector_done, n + 1)
                    dst = O["y_prompt"][0] if n == 0 else O["y_sample"][0, (n - 1) * P:n * P, :]
                    sp.dma_start(dst, xrows[:, n, :]).then_inc(y_out, 16)
                sp.wait_ge(y_out, 16 * NT)
    return named


def layer_body(nc, A, O, known, layer, env):
    K, tiled, xT, hT, ring, pcol, bcol, modT = (env[n] for n in ("K", "tiled", "xT", "hT", "ring", "pcol", "bcol", "modT"))
    scale_pre, gain_post, condT, dt_bias, neg_a = (env[n] for n in ("scale_pre", "gain_post", "condT", "dt_bias", "neg_a"))
    dskip2, dskip, sinks, arena, slot, tokens = (env[n] for n in ("dskip2", "dskip", "sinks", "arena", "slot", "tokens"))
    tensor_done, vector_done, scalar_done, pool_done = (env[n] for n in ("tensor_done", "vector_done", "scalar_done", "pool_done"))
    weights_in, hidden_in, ada_in, dft_in = (env[n] for n in ("weights_in", "hidden_in", "ada_in", "dft_in"))
    normed_parts, ring_parts, arena_parts, token_tiles, DFT_AT = (
        env[n] for n in ("normed_parts", "ring_parts", "arena_parts", "token_tiles", "DFT_AT"))
    cond_in, rows_in, rowvec_in, filt_in, decay_in = (env[n] for n in ("cond_in", "rows_in", "rowvec_in", "filt_in", "decay_in"))
    w3_in, state_in, cache_in, state_out, kv_out = (env[n] for n in ("w3_in", "state_in", "cache_in", "state_out", "kv_out"))
    Tn, Vc, Sc, Gp = (Steps(known.get(e, {})) for e in "TVSG")

    def row(name, k, rows=1):
        return pcol[:, ROWS[name][0] + k:ROWS[name][0] + k + rows]

    prow = arena[:, 0:P]
    brow = arena[:, P:2 * P]
    crow = arena[:, 2 * P:3 * P]
    hrow = arena[0:4, 6600:6600 + HID]
    mrow = arena[0:2, 3 * P:3 * P + 6 * D]
    squares = [arena[:, 7000 + T * i:7000 + T * (i + 1)] for i in range(3)]
    rstd = arena[:, 7000 + 3 * T:7000 + 4 * T]
    lnvar = arena[:, 7000 + 4 * T:7000 + 5 * T]
    h_hi = tiled(arena_parts, DFT_AT, KD)
    h_lo = [tiled(arena_parts, 10240, KD), tiled(normed_parts, 0, KD)]
    zg = tiled(arena, 0, 4)
    xbc = tiled(arena, 2560, 6)
    BT, CT = xbc[:, 4, :], xbc[:, 5, :]
    x_tok = arena[:, 6400:6400 + NT * 512].rearrange("p (c n) -> p c n", c=NT)
    B_tok = arena[:, 8960:8960 + T].rearrange("p (c n) -> p c n", c=NT)
    at = 8960 + T
    dts = arena[:, at:at + 80].rearrange("p (c m) -> p c m", c=NT)
    dA = arena[:, at + 80:at + 160].rearrange("p (c m) -> p c m", c=NT)
    w_end = arena[:, at + 160:at + 240].rearrange("p (r c h) -> p r c h", r=2, c=NT)
    chunk_decay = arena[:, at + 240:at + 280].rearrange("p (c r h) -> p c r h", c=NT, r=2)
    at += 280
    H = arena[:, at:at + 2048].rearrange("p (r c n) -> p r c n", r=2, c=4)
    H_end = arena[:, at + 2048:at + 2560].rearrange("p (r n) -> p r n", r=2)
    at += 2560
    xdt = arena[:, at:at + 1024].rearrange("p (r n) -> p r n", r=2)
    xw = [arena[:, at + 1024:at + 1536], arena[:, at + 1536:at + 2048]]
    at += 2048
    dA_tri = arena[:, at:at + 2048].rearrange("p (r n) -> p r n", r=2)
    E_seg = arena[:, at + 2048:at + 4096].rearrange("p (r n) -> p r n", r=2)
    dt_row = arena[0:16, at:at + T]
    init_rows = arena[0:64, at + 2048:at + 3072]
    sp_a, sp_b, sp_c = (arena[:, at + 3072 + 80 * i:at + 3152 + 80 * i] for i in range(3))
    at += 4096
    C_dec = arena[:, at:at + 1024].rearrange("p (r n) -> p r n", r=2)
    E_acc = C_dec
    end_rows = arena[0:64, at:at + 1024]
    G_tri = arena[:, at + 1024:at + 1536].rearrange("p (r g n) -> p r g n", r=2, g=2)
    at += 1536
    xskip = xbc[:, 0:4, :]
    assert at <= 20120
    ssmY = zg
    v_tok = arena[:, 2560:5120].rearrange("p (c n) -> p c n", c=NT)
    x2T = tiled(arena, 2560, 4)
    x1_tok = arena[:, 5120:7680].rearrange("p (c n) -> p c n", c=NT)
    fsum = arena[:, 7680:10240].rearrange("p (c n) -> p c n", c=NT)
    fdif = arena[:, 10240:12800].rearrange("p (c n) -> p c n", c=NT)
    Yr, Ys = fsum, fdif
    Kr = arena[:, 12800:15360].rearrange("p (c n) -> p c n", c=NT)
    Ks = arena[:, 15360:17920].rearrange("p (c n) -> p c n", c=NT)
    decay = arena[:, 17920:18944].rearrange("p (r n) -> p r n", r=2)
    w3 = arena[0:HID, 18944:19968]
    hid1 = arena[0:HID, 12800:13440]
    hid2 = arena[0:HID, 13440:14080]
    arg_k = arena[0:HID, 14080:14720]
    feat = arena[0:FEAT, 15744:15744 + T]
    hb_tmp = [arena[:, 14720:15232], arena[:, 15232:15744]]
    conv_raw = [arena[:, 15744 + T * i:15744 + T * (i + 1)] for i in range(2)]
    w1sb, w2sb = arena[0:FEAT, 20120:20120 + HID], arena[0:HID, 20184:20184 + HID]
    bias_row = arena[0:1, 20248:20760]
    hyY = tiled(arena, 5120, 4)
    prod_a, prod_b = decay[:, 0, :], decay[:, 1, :]
    attY = tiled(arena, 2560, 4)
    qT = tiled(arena, 7680, 4)
    kT = arena[:, 10240:10240 + T]
    v_att = arena[:, 10880:10880 + T].rearrange("p (c n) -> p c n", c=NT)
    k_rows = arena[:, 11520:11520 + P]
    kc_rows = arena[:, 11648:11648 + P]
    kcT = arena[:, 11776:11776 + P]
    v_ctx = arena[:, 11904:11904 + P]
    S_sb = [arena[:, 12032 + 1024 * i:12032 + 1024 * (i + 1)].rearrange("p (g n) -> p g n", g=2) for i in range(3)]
    PT_sb = [arena[:, 15104 + 1024 * i:15104 + 1024 * (i + 1)].rearrange("p (g n) -> p g n", g=2) for i in range(3)]
    vT = arena[:, 19456:19456 + T]
    rot_tmp = [arena[:, 18176 + 512 * i:18176 + 512 * (i + 1)] for i in range(2)]
    stat = arena[:, 19200:19200 + 200].rearrange("p (n c) -> p n c", c=10)
    merged = tiled(arena, 7680, 8)
    sig = [arena[:, 12800 + T * i:12800 + T * (i + 1)] for i in range(4)]
    part = [arena[:, 15360 + T * i:15360 + T * (i + 1)] for i in range(3)]
    m_lo = tiled(arena_parts, 7680, 8)
    m_hi = [arena_parts[:, a:a + T] for a in [17280 + T * i for i in range(5)] + [DFT_AT + KD * T, DFT_AT, DFT_AT + T]]
    mix = tiled(arena, 0, 8)
    a_hi, a_lo = tiled(arena_parts, 0, KD), tiled(arena_parts, KD * T, KD)
    mix2 = tiled(arena, 10240, 8)
    ffn_gate = [arena[:, 15360 + T * i:15360 + T * (i + 1)] for i in range(4)]
    act = [arena[:, 17920 + T * i:17920 + T * (i + 1)] for i in range(2)]

    def k_major(a, lo, cols):
        return a[:, lo:lo + cols].rearrange("(k p) n -> p k n", p=P)

    w_in, ada = A["w_in"][layer], A["ada_w"][layer]
    blocks = []

    def block_of(name, kind, k, cols, src):
        blocks.append((name, kind, k, cols, src))

    def w_in_block(name, kind, lo, cols=QT * P):
        block_of(name, kind, KD, cols, k_major(w_in, lo, cols))

    for j in range(2):
        w_in_block(("z", j), "parts", IN_Z + QT * P * j)
    for j in range(3):
        w_in_block(("xbc", j), "parts", IN_XBC + QT * P * j)
    w_in_block(("dt",), "parts", IN_DT, 16)
    for j in range(6):
        w_in_block(("hy", j), "whole", IN_HY + QT * P * j)
    for j in range(2):
        block_of(("q", j), "q", KD, QT * P, j)
    w_in_block(("kv",), "parts", IN_K)
    for oq in range(4):
        for b in range(3):
            w_in_block(("gate", oq, b), "parts", IN_G + D * b + QT * P * oq)
            if b == 2:
                block_of(("proj", oq, b), "att", 4, QT * P, oq)
            else:
                block_of(("proj", oq, b), "whole", 4, QT * P,
                         k_major((A["hy_proj"], A["ssm_proj"])[b][layer], QT * P * oq, QT * P))
    for oq in range(4):
        block_of(("out", oq), "parts", KD, QT * P, k_major(A["w_out"][layer], QT * P * oq, QT * P))
    for part_at, (f0, nf) in enumerate(FPARTS):
        for j in range(f0 // QT, (f0 + nf) // QT):
            for u in range(2):
                block_of(("up", u, j), "parts", KD, QT * P,
                         k_major(A[("ffn_w_gate", "ffn_w_up")[u]][layer], QT * P * j, QT * P))
        for oq in range(4):
            block_of(("down", part_at, oq), "parts", nf, QT * P,
                     k_major(A["ffn_w_down"][layer][f0 * P:(f0 + nf) * P, :], QT * P * oq, QT * P))
    index = {blk[0]: n for n, blk in enumerate(blocks)}
    split_blocks = [n for n, blk in enumerate(blocks) if blk[1] in ("parts", "q")]
    split_index = {blocks[n][0]: m for m, n in enumerate(split_blocks)}

    landed_count, per = [], [0] * RAW
    for n, blk in enumerate(blocks):
        per[n % RAW] += {"q": KD * KV, "att": KV}.get(blk[1], 1)
        landed_count.append(per[n % RAW])

    def raw_view(n):
        _, _, k, cols, _ = blocks[n]
        base = WB * (n % RAW)
        return ring[:, base:base + k * cols].rearrange("p (k n) -> p k n", k=k)

    def landed(eng, n):
        eng.wait_ge(weights_in[n % RAW], 16 * landed_count[n])

    def ada_view(j):
        base = ADA_WB * (j % ADA_RING)
        return ring[:, base:base + KD * 512].rearrange("p (k n) -> p k n", k=KD)

    def part_view(m, low):
        _, _, k, cols, _ = blocks[split_blocks[m]]
        base = WB * (RAW + PARTS * low + m % PARTS)
        return ring_parts[:, base:base + k * cols].rearrange("p (k n) -> p k n", k=k)

    def weights(pe, *name):
        landed(pe, index[name])
        return raw_view(index[name])

    def weight_parts(pe, *name):
        m = split_index[name]
        pe.wait_ge(vector_done, Vc["part", m])
        return part_view(m, 0), part_view(m, 1)

    def split_hi(sc, m):
        if m >= len(split_blocks):
            return
        n = split_blocks[m]
        landed(sc, n)
        sc.wait_ge(tensor_done, Tn["used", split_blocks[m - PARTS]] if m >= PARTS else Tn["ada_used", 11])
        Sc(sc.copy(part_view(m, 0), raw_view(n)).then_inc(scalar_done, 1), "hi", m)

    def split_lo(dve, m):
        if m >= len(split_blocks):
            return
        n = split_blocks[m]
        dve.wait_ge(scalar_done, Sc["hi", m])
        Vc(dve.tensor_tensor(part_view(m, 1), raw_view(n), part_view(m, 0).bitcast(F32), ALU.subtract)
           .then_inc(vector_done, 1), "part", m)

    uses = []

    def take(pe, *name):
        if len(uses) >= 4:
            engine, old = uses[-4]
            if engine == "V":
                pe.wait_ge(vector_done, Vc[old])
            else:
                pe.wait_ge(scalar_done, Sc[old])
        uses.append((name[0], name[1:]))
        s = (len(uses) - 1) % 4
        Tn.named[("slot",) + name[1:]] = s
        return s

    def w_used(*name):
        Tn.named[("used", index[name])] = Tn.count

    def used(*name):
        return Tn.known.get(("slot",) + name, 0)

    HALVES = ((0, T // 2), (T // 2, T))

    def dense(pe, s, w, o, rhs):
        n = len(rhs)
        for k in range(n):
            for lo, hi in HALVES:
                m = pe.matmul(tokens(s)[:, lo:hi], w[:, k, o * P:(o + 1) * P], rhs[k][:, lo:hi], start=k == 0, stop=k == n - 1)
        return m

    def dense_parts(pe, s, w, o, rhs, cols=P, after=None):
        (w_hi, w_lo), (x_hi, x_lo) = w, rhs
        n = len(x_hi)
        for k in range(n):
            if after:
                after(k)
            oc = slice(o * cols, (o + 1) * cols)
            for i, (a, x) in enumerate(((w_hi, x_hi), (w_hi, x_lo), (w_lo, x_hi))):
                for lo, hi in HALVES:
                    m = pe.matmul(tokens(s)[0:cols, lo:hi], a[:, k, oc], x[k][:, lo:hi],
                                  start=k == 0 and i == 0, stop=k == n - 1 and i == 2)
        return m

    def tile_list(t, n=KD):
        return [t[:, k, :] for k in range(n)]

    hk = tile_list(hT)
    h1 = (tile_list(h_hi), tile_list(h_lo[0]))
    h2 = (tile_list(h_hi), tile_list(h_lo[1]))

    def channel_sum(pe, name, n):
        s = take(pe, "S", "ln", name)
        for k in range(n):
            pe.wait_ge(scalar_done, Sc["sq", name, k])
            sq = sq_of(name, k)
            for lo, hi in HALVES:
                m = pe.matmul(tokens(s)[:, lo:hi], K("ones"), sq[:, lo:hi], start=k == 0, stop=k == n - 1)
            Tn(m.then_inc(tensor_done, 1), "sq", name, k)
        Tn.named[("sum", name)] = Tn.count

    def norm_sum(pe, name):
        channel_sum(pe, name, KD)

    def sq_of(name, k):
        return squares[k % 2] if name == "ssm" else squares[k % 3] if name in ("n1", "n2") else hT[:, k, :]

    def rstd_of(sc, name, width):
        sc.wait_ge(tensor_done, Tn["sum", name])
        s = used("ln", name)
        Sc(sc.activation(lnvar, tokens(s), ACT.Ln, scale=1.0 / width, bias=K("eps")).then_inc(scalar_done, 1), "ln", name)
        sc.wait_ge(scalar_done, Sc["ln", name])
        Sc(sc.activation(rstd, lnvar, ACT.Exp, scale=-0.5).then_inc(scalar_done, 1), "rstd", name)

    def pre_norm(sc, i, name):
        for k in range(KD):
            if i == 1:
                sc.wait_ge(vector_done, Vc["x", 0, k])
            if k >= 3:
                sc.wait_ge(tensor_done, Tn["sq", name, k - 3])
            Sc(sc.activation(squares[k % 3], xT[:, k, :], ACT.Square).then_inc(scalar_done, 1), "sq", name, k)
        rstd_of(sc, name, D)
        sc.wait_ge(vector_done, Vc["gains", 1])
        for k in range(KD):
            sc.wait_ge(vector_done, Vc["xn", name, k])
            for c, (lo, hi) in enumerate(((0, LP), (LP, T))):
                Sc(sc.activation(hT[:, k, lo:hi], hT[:, k, lo:hi], ACT.Identity, scale=scale_pre[:, i, k, c:c + 1],
                                 bias=modT[:, 24 * i + k, c:c + 1]).then_inc(scalar_done, 1), "h", name, k)
            sc.wait_ge(scalar_done, Sc["h", name, k])
            Sc(sc.copy(h_hi[:, k, :], hT[:, k, :]).then_inc(scalar_done, 1), "h_hi", name, k)

    def norm_apply(dve, name):
        dve.wait_ge(scalar_done, Sc["rstd", name])
        for k in range(KD):
            Vc(dve.tensor_tensor(hT[:, k, :], xT[:, k, :], rstd, ALU.mult).then_inc(vector_done, 1), "xn", name, k)

    def normed_low(dve, name):
        for k in range(KD):
            dve.wait_ge(scalar_done, Sc["h_hi", name, k])
            lo = h_lo[0 if name == "n1" else 1]
            Vc(dve.tensor_tensor(lo[:, k, :], hT[:, k, :], h_hi[:, k, :].bitcast(F32), ALU.subtract)
               .then_inc(vector_done, 1), "h_lo", name, k)

    def mixed(sc, i, dst, name):
        for o in range(KD):
            if o % QT == 0:
                split_hi(sc, split_index[("out", o // QT)] + 1)
            sc.wait_ge(tensor_done, Tn["mix", i, o])
            s = used("mix", i, o)
            Sc(sc.copy(dst[:, o, :], tokens(s)).then_inc(scalar_done, 1))
            Sc(sc.activation(hT[:, o, :], tokens(s), ACT.Square).then_inc(scalar_done, 1), "mix", i, o)
            Sc.named[("sq", name, o)] = Sc.count
        rstd_of(sc, name, D)

    def post_norm(dve, i, src, name):
        dve.wait_ge(scalar_done, Sc["rstd", name])
        for k in range(KD):
            Vc(dve.tensor_tensor(src[:, k, :], src[:, k, :], rstd, ALU.mult).then_inc(vector_done, 1))
            dve.wait_ge(vector_done, Vc.count)
            for c, (lo, hi) in enumerate(((0, LP), (LP, T))):
                Vc(dve.scalar_tensor_tensor(out=xT[:, k, lo:hi], in0=src[:, k, lo:hi], scalar=gain_post[:, i, k, c:c + 1],
                                            in1=xT[:, k, lo:hi], op0=ALU.mult, op1=ALU.add).then_inc(vector_done, 1), "x", i, k)

    CHAIN = [(0, 0), (0, 1), (1, 0), (4, 1), (2, 0), (3, 1), (3, 0), (2, 1)]
    UNITS = [(b, t) for b in range(NT) for t in range(4)]

    def key_tiles(b):
        return [0] if b == 0 else [-1] + list(range(max(1, b - 1), min(NT, b + 2)))

    def n_keys(b):
        return len(key_tiles(b))

    with nc.Block() as block:
        @block.tensor
        def _(pe):
            pe.wait_ge(rows_in, 16 * 10)
            s = take(pe, "V", "pcol")
            pe.transpose(slot(s)[:, 0:N_ROWS], prow[0:N_ROWS, :], K("ident", rows=N_ROWS)[:, 0:N_ROWS])
            Tn(pe.transpose(slot(s)[:, 512:560], brow[0:48, :], K("ident", 0, 48, 48)).then_inc(tensor_done, 1), "pcol")
            pe.wait_ge(hidden_in, 16 * 4)
            s = take(pe, "V", "bcol")
            Tn(pe.transpose(slot(s)[0:HID, 0:4], hrow, K("ident", 0, 4, 4)).then_inc(tensor_done, 1), "bcol")
            pe.wait_ge(scalar_done, Sc["cond"])
            s = take(pe, "V", "condT")
            Tn(pe.transpose(slot(s)[:, 0:16], crow[0:16, :], K("ident", 0, 16, 16)).then_inc(tensor_done, 1), "condT")
            pe.wait_ge(vector_done, Vc["condT"])
            cond = condT[:, :].rearrange("p (c k) -> p k c", c=2)
            for j in range(12):
                pe.wait_ge(ada_in[j % ADA_RING], 16 * (j // ADA_RING + 1))
                w = ada_view(j)
                s = take(pe, "S", "mrow", j)
                for k in range(KD):
                    m = pe.matmul(slot(s)[0:2, 0:512], cond[:, k, :], w[:, k, :], start=k == 0, stop=k == KD - 1)
                Tn(m.then_inc(tensor_done, 1), "mrow", j)
                Tn.named[("ada_used", j)] = Tn.count
            norm_sum(pe, "n1")
            pe.wait_ge(scalar_done, Sc["mrow", 11])
            s = take(pe, "V", "modT")
            for j in range(48):
                m = pe.transpose(slot(s)[:, 2 * j:2 * j + 2], mrow[:, j * P:(j + 1) * P], K("ident", 0, 2, 2))
            Tn(m.then_inc(tensor_done, 1), "modT")

            def h1_tile(k):
                pe.wait_ge(vector_done, Vc["h_lo", "n1", k])

            for o in range(4):
                if o % QT == 0:
                    w = weight_parts(pe, "z", o // QT)
                s = take(pe, "S", "z", o)
                Tn(dense_parts(pe, s, w, o % QT, h1, after=None if o else h1_tile).then_inc(tensor_done, 1), "z", o)
                if o % QT == QT - 1:
                    w_used("z", o // QT)
            for o in range(6):
                if o % QT == 0:
                    w = weight_parts(pe, "xbc", o // QT)
                s = take(pe, "V", "conv", "xbc", o)
                Tn(dense_parts(pe, s, w, o % QT, h1).then_inc(tensor_done, 1), "conv", "xbc", o)
                if o % QT == QT - 1:
                    w_used("xbc", o // QT)
            w = weight_parts(pe, "dt")
            s = take(pe, "S", "dt_row")
            Tn(dense_parts(pe, s, w, 0, h1, cols=16).then_inc(tensor_done, 1), "dt_row")
            w_used("dt")
            s = take(pe, "V", "dt_tok")
            pe.wait_ge(scalar_done, Sc["dt_row"])
            for c in range(NT):
                m = pe.transpose(slot(s)[:, 16 * c:16 * c + 16], dt_row[:, c * P:(c + 1) * P], K("ident", 0, 16, 16))
            Tn(m.then_inc(tensor_done, 1), "dt_tok")
            pe.wait_ge(state_in, 64)
            s = take(pe, "V", "H0")
            for i in range(8):
                m = pe.transpose(slot(s)[:, 64 * i:64 * i + 64], init_rows[:, 128 * i:128 * (i + 1)], K("ident", 0, 64, 64))
            Tn(m.then_inc(tensor_done, 1), "H0")
            pe.wait_ge(scalar_done, Sc["xbc", 5])
            for c in range(NT):
                s = take(pe, "V", "x_tok", c)
                for o in range(5):
                    m = pe.transpose(slot(s)[:, 128 * o:128 * (o + 1)], xbc[:, o, c * P:(c + 1) * P], K("ident"))
                Tn(m.then_inc(tensor_done, 1), "x_tok", c)
            pe.wait_ge(vector_done, Vc["dA"])
            s = take(pe, "S", "decays")
            for r, tri in enumerate(("t_gt_j", "t_lt_j")):
                pe.matmul(slot(s)[:, 40 * r:40 * r + 40].rearrange("p (c h) -> p c h", c=NT), K(tri),
                          dA[:, :, 8 * r:8 * r + 8], start=True, stop=True)
            dAg = dA.rearrange("p c (r g h) -> p c r g h", r=2, g=2)
            for g in range(2):
                for r in range(2):
                    m = pe.matmul(slot(s)[64 * g:64 * g + 64, 512 + 20 * r:532 + 20 * r].rearrange("p (c h) -> p c h", c=NT),
                                  K("ones", 0, 64), dAg[:, :, r, g, :], start=True, stop=True)
            Tn(m.then_inc(tensor_done, 1), "decays")
            for i, (c, r) in enumerate(CHAIN):
                pe.wait_ge(vector_done, Vc["xw", c, r])
                s = take(pe, "V", "state", c, r)
                for g in range(2):
                    m = pe.matmul(slot(s)[64 * g:64 * g + 64, 0:256], B_tok[:, c, 64 * g:64 * g + 64],
                                  xw[i % 2][:, 256 * g:256 * g + 256], start=True, stop=True)
                Tn(m.then_inc(tensor_done, 1), "state", c, r)
            s = take(pe, "V", "end_rows")
            for r in range(2):
                for hh in range(4):
                    m = pe.transpose(slot(s)[0:64, 512 * r + 128 * hh:512 * r + 128 * hh + 128],
                                     H_end[:, r, 64 * hh:64 * hh + 64], K("ident"))
            Tn(m.then_inc(tensor_done, 1), "end_rows")

            def decay_sums(c, r):
                pe.wait_ge(pool_done, Gp["dA_tri", c, r])
                s = take(pe, "S", "seg", c, r)
                for half in range(2):
                    m = pe.matmul(slot(s)[:, 512 * half:512 * half + 512], K(("t_gt_j", "t_lt_j")[r]),
                                  dA_tri[:, r, 512 * half:512 * half + 512], start=True, stop=True)
                Tn(m.then_inc(tensor_done, 1), "seg", c, r)
                if c >= 1:
                    s = take(pe, "S", "acc", c, r)
                    for g in range(2):
                        m = pe.matmul(slot(s)[64 * g:64 * g + 64, 0:512], K("ones", 0, 64),
                                      dA_tri[:, r, 512 * g:512 * g + 512], start=True, stop=True)
                    Tn(m.then_inc(tensor_done, 1), "acc", c, r)

            def outputs(c):
                pe.wait_ge(vector_done, Vc["S", c, 1])
                s = take(pe, "V", "y", c)
                for h in range(HEADS):
                    g, hh, e = h // 4, h % 4, 64 * (h % 2)
                    at = 512 * g + 128 * (hh // 2)
                    dst = slot(s)[e:e + 64, at:at + 128]
                    last = 2 if c == 0 else 4
                    i = 0
                    for r in range(2):
                        i += 1
                        m = pe.matmul(dst, xdt[:, r, 64 * h:64 * h + 64], E_seg[:, r, 128 * h:128 * h + 128],
                                      start=i == 1, stop=i == last)
                    if c >= 1:
                        for r in range(2):
                            i += 1
                            m = pe.matmul(dst, H[64 * g:64 * g + 64, r, c - 1, 64 * hh:64 * hh + 64],
                                          C_dec[64 * g:64 * g + 64, r, 128 * hh:128 * hh + 128], start=False, stop=i == last)
                Tn(m.then_inc(tensor_done, 1), "y", c)

            for c in range(NT):
                s = take(pe, "V", "G", c)
                for g in range(2):
                    m = pe.matmul(slot(s)[:, 512 * g:512 * g + 128], BT[64 * g:64 * g + 64, c * P:(c + 1) * P],
                                  CT[64 * g:64 * g + 64, c * P:(c + 1) * P], start=True, stop=True)
                Tn(m.then_inc(tensor_done, 1), "G", c)
                for r in range(2):
                    decay_sums(c, r)
                outputs(c)
            channel_sum(pe, "ssm", 4)

            def hidden(name, lhs, rhs):
                s = take(pe, "V", "arg", name)
                for lo, hi in HALVES:
                    m = pe.matmul(tokens(s)[0:HID, lo:hi], lhs, rhs[:, lo:hi], start=True, stop=True)
                Tn(m.then_inc(tensor_done, 1), "arg", name)

            def filters(i):
                pe.wait_ge(vector_done, Vc["ssmY", 3])
                pe.wait_ge(w3_in, 32 * (i + 1))
                pe.wait_ge(filt_in, 16 * 3)
                hidden((i, 1), w1sb, feat)
                pe.wait_ge(scalar_done, Sc["hid", i, 1])
                hidden((i, 2), w2sb, hid1)
                pe.wait_ge(scalar_done, Sc["hid", i, 2])
                for c in range(NT):
                    s = take(pe, "V", "filt", i, c)
                    for r in range(2):
                        m = pe.matmul(slot(s)[:, 512 * r:512 * r + 512], hid2[:, c * P:(c + 1) * P],
                                      w3[:, 512 * r:512 * r + 512], start=True, stop=True)
                    Tn(m.then_inc(tensor_done, 1), "filt", i, c)

            def transform(name, i, cos_rhs, sin_rhs, engine, nyquist):
                for q in range(NT):
                    tail, k, toks = ("_p", 0, [0]) if q == 0 else ("", q - 1, [1, 2, 3, 4])
                    s = take(pe, engine, name, i, q)
                    for r, rhs in enumerate((cos_rhs, sin_rhs)):
                        for j, n in enumerate(toks):
                            at = (0 if q == 0 else LS * j) + k * P
                            m = pe.matmul(slot(s)[:, 512 * r:512 * r + 512], K(("dft_c", "dft_s")[r] + tail, at, at + P),
                                          rhs[:, n, :], start=j == 0, stop=j == len(toks) - 1)
                    Tn(m.then_inc(tensor_done, 1), name, i, q)
                    if nyquist and q <= 1:
                        s = take(pe, engine, name + "n", i, q)
                        for j, n in enumerate(toks):
                            at = 0 if q == 0 else LS * j
                            m = pe.matmul(slot(s)[0:1, 0:512], K("dft_s" + tail, at, at + 1), cos_rhs[:, n, :],
                                          start=j == 0, stop=j == len(toks) - 1)
                        Tn(m.then_inc(tensor_done, 1), name + "n", i, q)

            def hy_project(b):
                for o in range(4):
                    if o % QT == 0:
                        w = weights(pe, "hy", 2 * b + o // QT)
                    s = take(pe, "V", "conv", "hy", 4 * b + o)
                    Tn(dense(pe, s, w, o % QT, hk).then_inc(tensor_done, 1), "conv", "hy", 4 * b + o)
                    if o % QT == QT - 1:
                        w_used("hy", 2 * b + o // QT)
                    if b < 2:
                        if o >= 1:
                            turn(b, o - 1)
                if b < 2:
                    turn(b, 3)

            def turn(b, o):
                pe.wait_ge(vector_done, Vc["conv4", "hy", 4 * b + o])
                s = take(pe, "S", "turn", b, o)
                for c in range(NT):
                    m = pe.transpose(token_tiles(s)[:, c * P:(c + 1) * P], conv_raw[o % 2][:, c * P:(c + 1) * P], K("ident"))
                Tn(m.then_inc(tensor_done, 1), "turn", b, o)

            filters(0)
            for b in range(2):
                hy_project(b)
            pe.wait_ge(vector_done, Vc["fsum", 0, 4])
            pe.wait_ge(dft_in, 16)
            transform("K", 0, fsum, fdif, "S", True)
            pe.wait_ge(scalar_done, Sc["turn", 0, 3])
            transform("U", 0, v_tok, v_tok, "V", False)
            for c in range(NT):
                pe.wait_ge(vector_done, Vc["Y", 0, 0 if c == 0 else 4])
                s = take(pe, "V", "z1", c)
                for j, q in enumerate([0] if c == 0 else [1, 2, 3, 4]):
                    tail, at = ("_p", 0) if c == 0 else ("", LS * j + (c - 1) * P)
                    n = 1 if c == 0 else 4
                    pe.matmul(slot(s)[:, 0:512], K("dft_c" + tail, at, at + P), Yr[:, q, :], start=j == 0, stop=False)
                    m = pe.matmul(slot(s)[:, 0:512], K("idft_s" + tail, at, at + P), Ys[:, q, :], start=False, stop=j == n - 1)
                Tn(m.then_inc(tensor_done, 1), "z1", c)
            filters(1)
            hy_project(2)
            pe.wait_ge(vector_done, Vc["fsum", 1, 4])
            transform("K", 1, fsum, fdif, "S", True)
            transform("U", 1, x1_tok, x1_tok, "V", False)
            pe.wait_ge(vector_done, Vc["Y", 1, 4])
            for o in range(4):
                s = take(pe, "V", "hyY", o)
                oc = slice(o * P, (o + 1) * P)
                pe.matmul(token_tiles(s)[:, 0:LP], Yr[:, 0, oc], K("dft_c_p"), start=True, stop=False)
                pe.matmul(token_tiles(s)[:, 0:LP], Ys[:, 0, oc], K("idft_s_p"), start=False, stop=True)
                for q in range(4):
                    pe.matmul(token_tiles(s)[:, LP:T], Yr[:, 1 + q, oc], K("dft_c", LS * q, LS * (q + 1)), start=q == 0, stop=False)
                    m = pe.matmul(token_tiles(s)[:, LP:T], Ys[:, 1 + q, oc], K("idft_s", LS * q, LS * (q + 1)), start=False, stop=q == 3)
                Tn(m.then_inc(tensor_done, 1), "hyY", o)

            def h2_tile(name):
                return lambda k: pe.wait_ge(vector_done, Vc["h_lo", name, k])

            for o in range(4):
                if o % QT == 0:
                    w = weight_parts(pe, "q", o // QT)
                s = take(pe, "S", "q", o)
                Tn(dense_parts(pe, s, w, o % QT, h2, after=None if o else h2_tile("att")).then_inc(tensor_done, 1), "q", o)
                if o % QT == QT - 1:
                    w_used("q", o // QT)
            w = weight_parts(pe, "kv")
            for o, name in enumerate((("q", 4), ("vT",))):
                s = take(pe, "S", *name)
                Tn(dense_parts(pe, s, w, o, h2).then_inc(tensor_done, 1), *name)
            w_used("kv")
            s = take(pe, "S", "v")
            pe.wait_ge(scalar_done, Sc["vT"])
            for c in range(NT):
                m = pe.transpose(token_tiles(s)[:, c * P:(c + 1) * P], vT[:, c * P:(c + 1) * P], K("ident"))
            Tn(m.then_inc(tensor_done, 1), "v")
            for o in range(5):
                s = take(pe, "V", "rot", o)
                pe.wait_ge(scalar_done, Sc["q", o])
                src = (qT[:, o, :] if o < 4 else kT)
                Tn(pe.matmul(slot(s)[:, 0:512], K("rotate"), src[:, LP:T], start=True, stop=True)
                   .then_inc(tensor_done, 1), "rot", o)
            pe.wait_ge(cache_in, 32)
            s = take(pe, "S", "kcT")
            pe.transpose(slot(s)[:, 0:P], kc_rows, K("ident"))
            Tn(pe.transpose(slot(s)[:, 512:640], kT[:, 0:P], K("ident")).then_inc(tensor_done, 1), "kcT")

            def scores(n):
                b, t = UNITS[n]
                s = take(pe, "V", "max", n)
                for g in range(2):
                    q = qT[64 * g:64 * g + 64, t, b * P:(b + 1) * P]
                    if b == 0:
                        m = pe.matmul(slot(s)[:, 512 * g:512 * g + 128], q, kT[64 * g:64 * g + 64, 0:P], start=True, stop=True)
                    else:
                        lo, hi = max(1, b - 1), min(NT, b + 2)
                        pe.matmul(slot(s)[:, 512 * g:512 * g + 128], q, kcT[64 * g:64 * g + 64, :], start=True, stop=True)
                        m = pe.matmul(slot(s)[:, 512 * g + 128:512 * g + 128 + (hi - lo) * P], q,
                                      kT[64 * g:64 * g + 64, lo * P:hi * P], start=True, stop=True)
                Tn(m.then_inc(tensor_done, 1), "scores", n)

            def turn_probs(n):
                b, t = UNITS[n]
                pe.wait_ge(vector_done, Vc["probs", n])
                s = take(pe, "S", "PT", n)
                for g in range(2):
                    for j in range(n_keys(b)):
                        m = pe.transpose(slot(s)[:, 512 * g + 128 * j:512 * g + 128 * (j + 1)],
                                         S_sb[n % 3][:, g, 128 * j:128 * (j + 1)], K("ident"))
                Tn(m.then_inc(tensor_done, 1), "PT", n)

            def values(n):
                b, t = UNITS[n]
                pe.wait_ge(scalar_done, Sc["PT", n])
                s = take(pe, "V", "att", n)
                kt = key_tiles(b)
                for g in range(2):
                    for j, c in enumerate(kt):
                        v = v_ctx if c < 0 else v_att[:, c, :]
                        m = pe.matmul(slot(s)[64 * g:64 * g + 64, 0:128], v[:, 64 * g:64 * g + 64],
                                      PT_sb[n % 3][:, g, 128 * j:128 * (j + 1)], start=j == 0, stop=j == len(kt) - 1)
                Tn(m.then_inc(tensor_done, 1), "att", n)

            pe.wait_ge(vector_done, Vc["rope", 4])
            pe.wait_ge(scalar_done, Sc["kcT"])
            for n in range(len(UNITS) + 2):
                if n < len(UNITS):
                    scores(n)
                if 1 <= n <= len(UNITS):
                    turn_probs(n - 1)
                if n >= 2:
                    values(n - 2)

            for oq in range(4):
                for b, y in enumerate((hyY, ssmY, attY)):
                    wg = weight_parts(pe, "gate", oq, b)
                    for o in range(QT):
                        s = take(pe, "S", "gate", oq, b, o)
                        Tn(dense_parts(pe, s, wg, o, h2).then_inc(tensor_done, 1), "gate", oq, b, o)
                        if o == QT - 1:
                            w_used("gate", oq, b)
                        if b == 2 and oq == 0 and o == 0:
                            pe.wait_ge(vector_done, Vc["att", len(UNITS) - 1])
                        if o == 0:
                            wp = weights(pe, "proj", oq, b)
                        s = take(pe, "V", "proj", oq, b, o)
                        Tn(dense(pe, s, wp, o, tile_list(y, 4)).then_inc(tensor_done, 1), "proj", oq, b, o)
                    w_used("proj", oq, b)
            for o in range(KD):
                if o % QT == 0:
                    w = weight_parts(pe, "out", o // QT)
                s = take(pe, "S", "mix", 0, o)
                Tn(dense_parts(pe, s, w, o % QT, (m_hi, tile_list(m_lo)),
                               after=None if o else lambda k: pe.wait_ge(vector_done, Vc["m_lo", k]))
                   .then_inc(tensor_done, 1), "mix", 0, o)
                if o % QT == QT - 1:
                    w_used("out", o // QT)
            channel_sum(pe, "p1", KD)
            norm_sum(pe, "n2")

            for i, (f0, nf) in enumerate(FPARTS):
                for j in range(f0 // QT, (f0 + nf) // QT):
                    for u, name in enumerate(("fgate", "fup")):
                        w = weight_parts(pe, "up", u, j)
                        for o in range(QT):
                            s = take(pe, "SV"[u], name, QT * j + o)
                            Tn(dense_parts(pe, s, w, o, h2, after=h2_tile("n2") if u == j == o == 0 else None)
                               .then_inc(tensor_done, 1), name, QT * j + o)
                        w_used("up", u, j)
                for o in range(KD):
                    if o % QT == 0:
                        w = weight_parts(pe, "down", i, o // QT)
                    s = take(pe, "V" if i else "S", "down", i, o)
                    Tn(dense_parts(pe, s, w, o % QT, (tile_list(a_hi, nf), tile_list(a_lo, nf)),
                                   after=None if o else lambda k: pe.wait_ge(vector_done, Vc["a_lo", f0 + k]))
                       .then_inc(tensor_done, 1), "down", i, o)
                    if o % QT == QT - 1:
                        w_used("down", i, o // QT)
            channel_sum(pe, "p2", KD)

        @block.vector
        def _(dve):
            dve.wait_ge(tensor_done, Tn["pcol"])
            s = used("pcol")
            Vc(dve.tensor_copy(pcol[:, :], slot(s)[:, 0:N_ROWS]).then_inc(vector_done, 1))
            Vc(dve.tensor_copy(bcol[:, 0:48], slot(s)[:, 512:560]).then_inc(vector_done, 1), "pcol")
            dve.wait_ge(tensor_done, Tn["bcol"])
            Vc(dve.tensor_copy(bcol[0:HID, 48:52], slot(used("bcol"))[0:HID, 0:4]).then_inc(vector_done, 1), "bcol")
            dve.wait_ge(tensor_done, Tn["condT"])
            Vc(dve.tensor_copy(condT[:, :], slot(used("condT"))[:, 0:16]).then_inc(vector_done, 1), "condT")
            dve.wait_ge(rowvec_in, 16 * 4)
            for e in range(2):
                half = slice(64 * e, 64 * e + 64)
                Vc(dve.tensor_tensor(dskip[half, :], dskip2[half, e:8:2], dskip2[half, 8 + e:16:2], ALU.add)
                   .then_inc(vector_done, 1), "dskip")
            dve.wait_ge(scalar_done, Sc["exp_a"])
            Vc(dve.tensor_scalar(neg_a[:, :], neg_a[:, :], -1.0, None, ALU.mult).then_inc(vector_done, 1), "neg_a")
            norm_apply(dve, "n1")
            dve.wait_ge(tensor_done, Tn["modT"])
            ada_b = bcol[:, 0:48].unsqueeze(2).broadcast_to([P, 48, 2])
            Vc(dve.tensor_tensor(modT[:, :, :], slot(used("modT"))[:, 0:96].rearrange("p (n c) -> p n c", c=2), ada_b, ALU.add)
               .then_inc(vector_done, 1), "modT")
            dve.wait_ge(vector_done, Vc["modT"])
            for i in range(2):
                pre = row(("mix_pre", "ffn_pre")[i], 0, 8).unsqueeze(2).broadcast_to([P, 8, 2])
                post = row(("mix_post", "ffn_post")[i], 0, 8).unsqueeze(2).broadcast_to([P, 8, 2])
                Vc(dve.scalar_tensor_tensor(out=scale_pre[:, i], in0=modT[:, 24 * i + 8:24 * i + 16, :], scalar=1.0, in1=pre,
                                            op0=ALU.add, op1=ALU.mult).then_inc(vector_done, 1))
                Vc(dve.tensor_tensor(gain_post[:, i], modT[:, 24 * i + 16:24 * i + 24, :], post, ALU.mult)
                   .then_inc(vector_done, 1), "gains", i)
            split_lo(dve, 0)
            normed_low(dve, "n1")
            for m in range(1, split_index["xbc", 0] + 1):
                split_lo(dve, m)

            def conv(kind, o, dst, name):
                dve.wait_ge(tensor_done, Tn["conv", kind, o])
                src = tokens(used("conv", kind, o))
                n = {"xbc": 6, "hy": 12}[kind]
                tag = {"xbc": "ssm", "hy": "hy"}[kind]
                w = [row(tag + "_w", n * j + o) for j in range(3)]
                Vc(dve.tensor_scalar(dst, src, w[1], row(tag + "_b", o), ALU.mult, ALU.add).then_inc(vector_done, 1))
                for lo, hi in ((0, LP), (LP, T)):
                    dve.wait_ge(vector_done, Vc.count)
                    Vc(dve.scalar_tensor_tensor(out=dst[:, lo + 1:hi], in0=src[:, lo:hi - 1], scalar=w[0],
                                                in1=dst[:, lo + 1:hi], op0=ALU.mult, op1=ALU.add).then_inc(vector_done, 1))
                    dve.wait_ge(vector_done, Vc.count)
                    Vc(dve.scalar_tensor_tensor(out=dst[:, lo:hi - 1], in0=src[:, lo + 1:hi], scalar=w[2],
                                                in1=dst[:, lo:hi - 1], op0=ALU.mult, op1=ALU.add).then_inc(vector_done, 1))
                Vc.named[("conv", kind, o)] = Vc.named[name] = Vc.count

            for o in range(6):
                if o % QT == 0:
                    split_lo(dve, split_index["xbc", o // QT] + 1)
                conv("xbc", o, xbc[:, o, :], ("conv4", "xbc", o))
            dve.wait_ge(tensor_done, Tn["dt_tok"])
            raw = slot(used("dt_tok"))[:, 0:80].rearrange("p (c m) -> p c m", c=NT)
            v, e, u = sp_a, sp_b, sp_c
            v3 = v.rearrange("p (c m) -> p c m", c=NT)
            Vc(dve.tensor_tensor(v3, raw, dt_bias[:, :].unsqueeze(1).broadcast_to([P, NT, 16]), ALU.add)
               .then_inc(vector_done, 1), "dt_tok")
            dve.wait_ge(vector_done, Vc.count)
            Vc(dve.scalar_tensor_tensor(out=e, in0=v, scalar=-1.0, in1=v, op0=ALU.mult, op1=ALU.min)
               .then_inc(vector_done, 1), "dt_abs")
            dve.wait_ge(scalar_done, Sc["dt_exp"])
            Vc(dve.tensor_scalar(u, e, 1.0, None, ALU.add).then_inc(vector_done, 1), "dt_u")
            dve.wait_ge(vector_done, Vc.count)
            flat = dts.rearrange("p c m -> p (c m)")
            dAf = dA.rearrange("p c m -> p (c m)")
            Vc(dve.scalar_tensor_tensor(out=e, in0=u, scalar=-1.0, in1=e, op0=ALU.add, op1=ALU.subtract)
               .then_inc(vector_done, 1))
            Vc(dve.reciprocal(dAf, u).then_inc(vector_done, 1), "u_inverse")
            dve.wait_ge(vector_done, Vc.count)
            Vc(dve.tensor_tensor(e, e, dAf, ALU.mult).then_inc(vector_done, 1))
            dve.wait_ge(vector_done, Vc.count)
            Vc(dve.scalar_tensor_tensor(out=flat, in0=v, scalar=0.0, in1=e, op0=ALU.max, op1=ALU.subtract)
               .then_inc(vector_done, 1))
            dve.wait_ge(vector_done, Vc.count)
            dve.wait_ge(scalar_done, Sc["dt_ln"])
            Vc(dve.tensor_tensor(flat, flat, u, ALU.add).then_inc(vector_done, 1))
            dve.wait_ge(vector_done, Vc.count)
            Vc(dve.tensor_tensor(dA, dts, neg_a[:, :].unsqueeze(1).broadcast_to([P, NT, 16]), ALU.mult)
               .then_inc(vector_done, 1), "dA")
            dve.wait_ge(tensor_done, Tn["H0"])
            h0 = slot(used("H0"))[:, 0:512].rearrange("p (r n) -> p r n", r=2)
            Vc(dve.tensor_copy(H[:, 0, 0, :], h0[:, 0, :]).then_inc(vector_done, 1))
            Vc(dve.tensor_copy(H[:, 1, 3, :], h0[:, 1, :]).then_inc(vector_done, 1), "H0")
            for c in range(NT):
                dve.wait_ge(tensor_done, Tn["x_tok", c])
                s = used("x_tok", c)
                Vc(dve.tensor_copy(x_tok[:, c, :], slot(s)[:, 0:512]).then_inc(vector_done, 1))
                Vc(dve.tensor_copy(B_tok[:, c, :], slot(s)[:, 512:640]).then_inc(vector_done, 1), "x_tok", c)
            for o in range(4):
                Vc(dve.tensor_scalar(xskip[:, o, :], xskip[:, o, :], dskip[:, o:o + 1], None, ALU.mult)
                   .then_inc(vector_done, 1), "xskip", o)

            def heads(x):
                return x.rearrange("p (h n) -> p h n", h=HEADS)

            def dt_of(c, r):
                return dts[:, c, 8 * r:8 * r + 8].unsqueeze(2).broadcast_to([P, HEADS, HD])

            dve.wait_ge(scalar_done, Sc["decays"])

            def weighted(i):
                c, r = CHAIN[i]
                xwi = heads(xw[i % 2])
                Vc(dve.tensor_tensor(xwi, heads(x_tok[:, c, :]), dt_of(c, r), ALU.mult).then_inc(vector_done, 1))
                dve.wait_ge(vector_done, Vc.count)
                Vc(dve.tensor_tensor(xwi, xwi, w_end[:, r, c, :].unsqueeze(2).broadcast_to([P, HEADS, HD]), ALU.mult)
                   .then_inc(vector_done, 1), "xw", c, r)

            weighted(0)
            for i, (c, r) in enumerate(CHAIN):
                if i + 1 < len(CHAIN):
                    weighted(i + 1)
                dve.wait_ge(tensor_done, Tn["state", c, r])
                got = slot(used("state", c, r))[:, 0:256]
                if c == 0:
                    Vc(dve.tensor_copy(H_end[:, r, :], got).then_inc(vector_done, 1), "state", c, r)
                    continue
                to = c + 1 if r == 0 else c - 1
                dec = chunk_decay[:, c, r, :].unsqueeze(2).broadcast_to([P, 4, 64])
                Vc(dve.tensor_tensor(H[:, r, to - 1, :].rearrange("p (h n) -> p h n", h=4),
                                     H[:, r, c - 1, :].rearrange("p (h n) -> p h n", h=4), dec, ALU.mult)
                   .then_inc(vector_done, 1))
                dve.wait_ge(vector_done, Vc.count)
                Vc(dve.tensor_tensor(H[:, r, to - 1, :], H[:, r, to - 1, :], got, ALU.add)
                   .then_inc(vector_done, 1), "state", c, r)
            dve.wait_ge(tensor_done, Tn["end_rows"])
            Vc(dve.tensor_copy(end_rows, slot(used("end_rows"))[0:64, 0:1024]).then_inc(vector_done, 1), "end_rows")
            for c in range(NT):
                dve.wait_ge(tensor_done, Tn["G", c])
                s = used("G", c)
                if c >= 1:
                    dve.wait_ge(vector_done, Vc["S", c - 1, 1])
                for r, tri in enumerate(("t_le_i", "t_ge_i")):
                    for g in range(2):
                        Vc(dve.tensor_tensor(G_tri[:, r, g, :], slot(s)[:, 512 * g:512 * g + 128], K(tri), ALU.mult)
                           .then_inc(vector_done, 1), "G", c)
                for r in range(2):
                    if c >= 1:
                        dve.wait_ge(tensor_done, Tn["y", c - 1])
                    Vc(dve.tensor_tensor(heads(xdt[:, r, :]), heads(x_tok[:, c, :]), dt_of(c, r), ALU.mult).then_inc(vector_done, 1))
                for r in range(2):
                    dve.wait_ge(scalar_done, Sc["acc" if c else "seg", c, r])
                    if c:
                        cb = CT[:, c * P:(c + 1) * P].unsqueeze(1).broadcast_to([P, 4, P])
                        Vc(dve.tensor_tensor(C_dec[:, r, :].rearrange("p (h n) -> p h n", h=4),
                                             E_acc[:, r, :].rearrange("p (h n) -> p h n", h=4), cb, ALU.mult)
                           .then_inc(vector_done, 1))
                    dve.wait_ge(vector_done, Vc["G", c])
                    for g in range(2):
                        ev = E_seg[:, r, 512 * g:512 * g + 512].rearrange("p (h n) -> p h n", h=4)
                        Vc(dve.tensor_tensor(ev, ev, G_tri[:, r, g, :].unsqueeze(1).broadcast_to([P, 4, P]), ALU.mult)
                           .then_inc(vector_done, 1), "S", c, r)
                dve.wait_ge(tensor_done, Tn["y", c])
                yv = xskip.rearrange("p (g o) n -> p g o n", g=2)[:, :, :, c * P:(c + 1) * P]
                got = slot(used("y", c)).rearrange("p (g o n) -> p g o n", g=2, o=4)[:, :, 0:2, :]
                Vc(dve.tensor_tensor(yv, yv, got, ALU.add)
                   .then_inc(vector_done, 1), "y", c)
            dve.wait_ge(vector_done, Vc.count)
            for o in range(4):
                Vc(dve.tensor_tensor(zg[:, o, :], zg[:, o, :], xskip[:, o, :], ALU.mult).then_inc(vector_done, 1), "yz", o)
            dve.wait_ge(scalar_done, Sc["rstd", "ssm"])
            for o in range(4):
                Vc(dve.scalar_tensor_tensor(out=zg[:, o, :], in0=zg[:, o, :], scalar=row("ssm_norm", o), in1=rstd,
                                            op0=ALU.mult, op1=ALU.mult).then_inc(vector_done, 1), "ssmY", o)

            def arg(i, n):
                dve.wait_ge(tensor_done, Tn["arg", (i, n)])
                h = (hid1, hid2)[n - 1]
                b, fr = bcol[0:HID, 48 + 2 * (n - 1):49 + 2 * (n - 1)], bcol[0:HID, 49 + 2 * (n - 1):50 + 2 * (n - 1)]
                Vc(dve.tensor_scalar(h, tokens(used("arg", (i, n)))[0:HID, :], b, fr, ALU.add, ALU.mult)
                   .then_inc(vector_done, 1), "arg", (i, n))
                big = 1.5 * 2.0 ** 23
                hi = float(np.float32(6.28125))
                lo = float(np.float32(TWO_PI - hi))
                pi = float(np.nextafter(np.float32(np.pi), np.float32(0)))
                dve.wait_ge(vector_done, Vc.count)
                Vc(dve.tensor_scalar(arg_k, h, float(np.float32(1 / TWO_PI)), big, ALU.mult, ALU.add).then_inc(vector_done, 1))
                dve.wait_ge(vector_done, Vc.count)
                Vc(dve.tensor_scalar(arg_k, arg_k, -big, None, ALU.add).then_inc(vector_done, 1))
                for part_ in (hi, lo):
                    dve.wait_ge(vector_done, Vc.count)
                    Vc(dve.scalar_tensor_tensor(out=h, in0=arg_k, scalar=-part_, in1=h, op0=ALU.mult, op1=ALU.add)
                       .then_inc(vector_done, 1))
                dve.wait_ge(vector_done, Vc.count)
                Vc(dve.tensor_scalar(h, h, pi, -pi, ALU.min, ALU.max).then_inc(vector_done, 1), "arg_in", i, n)

            def filters(i):
                arg(i, 1)
                arg(i, 2)
                for c in range(NT):
                    dve.wait_ge(tensor_done, Tn["filt", i, c])
                    dve.wait_ge(scalar_done, Sc["decay", i, c])
                    s = used("filt", i, c)
                    hb = hb_tmp[c % 2]
                    Vc(dve.tensor_tensor(fsum[:, c, :], fsum[:, c, :], slot(s)[:, 0:512], ALU.mult).then_inc(vector_done, 1))
                    Vc(dve.tensor_tensor(hb, hb, slot(s)[:, 512:1024], ALU.mult).then_inc(vector_done, 1), "filt", i, c)
                    dve.wait_ge(vector_done, Vc.count)
                    if c <= 1:
                        if c == 0:
                            dve.wait_ge(filt_in, 16 * (3 + i))
                        Vc(dve.tensor_tensor(fsum[0:1, c, :], fsum[0:1, c, :], bias_row, ALU.add).then_inc(vector_done, 1))
                        Vc(dve.memset(hb[0:1, :], 0.0).then_inc(vector_done, 1), "bias", i, c)
                        dve.wait_ge(vector_done, Vc.count)
                    Vc(dve.tensor_tensor(fdif[:, c, :], fsum[:, c, :], hb, ALU.subtract).then_inc(vector_done, 1))
                    dve.wait_ge(vector_done, Vc.count)
                    Vc(dve.tensor_tensor(fsum[:, c, :], fsum[:, c, :], hb, ALU.add).then_inc(vector_done, 1), "fsum", i, c)

            def spectrum(i):
                for q in range(NT):
                    dve.wait_ge(tensor_done, Tn["U", i, q])
                    if q == 0:
                        dve.wait_ge(scalar_done, Sc["Kn", i, 1])
                        dve.wait_ge(scalar_done, Sc["K", i, 4])
                    s = used("U", i, q)
                    ur, us = slot(s)[:, 0:512], slot(s)[:, 512:1024]
                    Vc(dve.tensor_tensor(Yr[:, q, :], ur, Kr[:, q, :], ALU.mult).then_inc(vector_done, 1))
                    if q:
                        dve.wait_ge(vector_done, Vc["Y", i, q - 1])
                    elif i == 1:
                        pass
                    Vc(dve.tensor_tensor(prod_a, us, Ks[:, q, :], ALU.mult).then_inc(vector_done, 1))
                    Vc(dve.tensor_tensor(Ys[:, q, :], ur, Ks[:, q, :], ALU.mult).then_inc(vector_done, 1))
                    Vc(dve.tensor_tensor(prod_b, us, Kr[:, q, :], ALU.mult).then_inc(vector_done, 1))
                    dve.wait_ge(vector_done, Vc.count)
                    Vc(dve.tensor_tensor(Yr[:, q, :], Yr[:, q, :], prod_a, ALU.subtract).then_inc(vector_done, 1))
                    Vc(dve.tensor_tensor(Ys[:, q, :], Ys[:, q, :], prod_b, ALU.add).then_inc(vector_done, 1), "Y", i, q)
                    if q <= 1:
                        dve.wait_ge(vector_done, Vc.count)
                        Vc(dve.tensor_tensor(Yr[0:1, q, :], ur[0:1, :], Kr[0:1, q, :], ALU.mult).then_inc(vector_done, 1))
                        Vc(dve.tensor_tensor(Ys[0:1, q, :], us[0:1, :], Ks[0:1, q, :], ALU.mult)
                           .then_inc(vector_done, 1), "Y", i, q)
                    Vc.named[("U", i, q)] = Vc.count

            filters(0)
            for b in range(2):
                for o in range(4):
                    if 4 * b + o >= 2:
                        dve.wait_ge(tensor_done, Tn["turn", (4 * b + o - 2) // 4, (o - 2) % 4])
                    conv("hy", 4 * b + o, conv_raw[o % 2], ("conv4", "hy", 4 * b + o))
            spectrum(0)
            for c in range(NT):
                dve.wait_ge(tensor_done, Tn["z1", c])
                if c == 0:
                    dve.wait_ge(scalar_done, Sc["turn", 1, 3])
                Vc(dve.tensor_tensor(x1_tok[:, c, :], x1_tok[:, c, :], slot(used("z1", c))[:, 0:512], ALU.mult)
                   .then_inc(vector_done, 1), "z1", c)
            filters(1)
            for o in range(4):
                conv("hy", 8 + o, x2T[:, o, :], ("conv4", "hy", 8 + o))
            split_lo(dve, split_index["q", 0])
            spectrum(1)
            dve.wait_ge(vector_done, Vc.count)
            for o in range(4):
                dve.wait_ge(tensor_done, Tn["hyY", o])
                Vc(dve.tensor_tensor(hyY[:, o, :], x2T[:, o, :], token_tiles(used("hyY", o)), ALU.mult)
                   .then_inc(vector_done, 1), "hyY", o)

            normed_low(dve, "att")
            for m in range(split_index["q", 1], split_index["gate", 0, 0] + 1):
                split_lo(dve, m)
            for o in range(5):
                x = (qT[:, o, :] if o < 4 else kT)[:, LP:T]
                dve.wait_ge(tensor_done, Tn["rot", o])
                if o >= 2:
                    dve.wait_ge(vector_done, Vc["rope", o - 2])
                Vc(dve.tensor_tensor(rot_tmp[o % 2], slot(used("rot", o))[:, 0:512], K("sin"), ALU.mult)
                   .then_inc(vector_done, 1), "rot", o)
                Vc(dve.tensor_tensor(x, x, K("cos"), ALU.mult).then_inc(vector_done, 1))
                dve.wait_ge(vector_done, Vc.count)
                Vc(dve.tensor_tensor(x, x, rot_tmp[o % 2], ALU.add).then_inc(vector_done, 1), "rope", o)

            def sink_of(n, g):
                return sinks[:, 4 * g + UNITS[n][1]:4 * g + UNITS[n][1] + 1]

            def softmax_max(n):
                b, _ = UNITS[n]
                w = n_keys(b) * P
                mask = K("mask_first") if b == 1 else K("mask")
                dve.wait_ge(tensor_done, Tn["scores", n])
                if n >= 3:
                    dve.wait_ge(tensor_done, Tn["PT", n - 3])
                for g in range(2):
                    Vc(dve.tensor_tensor_reduce(out=S_sb[n % 3][:, g, 0:w], in0=slot(used("max", n))[:, 512 * g:512 * g + w],
                                                in1=mask[:, 0:w], scale=HD ** -0.5, scalar=sink_of(n, g), op0=ALU.add,
                                                op1=ALU.max, accum_out=stat[:, n, g:g + 1]).then_inc(vector_done, 1), "max", n)
                dve.wait_ge(vector_done, Vc.count)
                Vc(dve.tensor_scalar(stat[:, n, 2:4], stat[:, n, 0:2], -1.0, None, ALU.mult).then_inc(vector_done, 1))
                sk = sinks[:, UNITS[n][1]:UNITS[n][1] + 5:4]
                dve.wait_ge(vector_done, Vc.count)
                Vc(dve.tensor_tensor(stat[:, n, 4:6], sk, stat[:, n, 2:4], ALU.add).then_inc(vector_done, 1), "negmax", n)

            def softmax_scale(n):
                b, _ = UNITS[n]
                w = n_keys(b) * P
                dve.wait_ge(scalar_done, Sc["exp", n])
                Vc(dve.tensor_tensor(stat[:, n, 6:8], stat[:, n, 6:8], stat[:, n, 4:6], ALU.add).then_inc(vector_done, 1))
                dve.wait_ge(vector_done, Vc.count)
                Vc(dve.reciprocal(stat[:, n, 8:10], stat[:, n, 6:8]).then_inc(vector_done, 1))
                dve.wait_ge(vector_done, Vc.count)
                for g in range(2):
                    Vc(dve.tensor_scalar(S_sb[n % 3][:, g, 0:w], S_sb[n % 3][:, g, 0:w], stat[:, n, 8 + g:9 + g], None, ALU.mult)
                       .then_inc(vector_done, 1), "probs", n)

            def attended(n):
                b, t = UNITS[n]
                dve.wait_ge(tensor_done, Tn["att", n])
                Vc(dve.tensor_copy(attY[:, t, b * P:(b + 1) * P], slot(used("att", n))[:, 0:P]).then_inc(vector_done, 1), "att", n)

            for n in range(len(UNITS) + 2):
                if n < len(UNITS):
                    softmax_max(n)
                if n >= 2:
                    attended(n - 2)
                if n < len(UNITS):
                    softmax_scale(n)

            i = 0
            def merged_low(oq):
                for m in range(QT * oq, QT * (oq + 1)):
                    dve.wait_ge(scalar_done, Sc["m_hi", m])
                    Vc(dve.tensor_tensor(m_lo[:, m, :], merged[:, m, :], m_hi[m].bitcast(F32), ALU.subtract)
                       .then_inc(vector_done, 1), "m_lo", m)

            g = 0
            for oq in range(4):
                for b in range(3):
                    split_lo(dve, split_index["gate", oq, b] + 1)
                    for o in range(QT):
                        m = QT * oq + o
                        dve.wait_ge(tensor_done, Tn["proj", oq, b, o])
                        dve.wait_ge(scalar_done, Sc["gate", oq, b, o])
                        if b == 0:
                            dst = merged[:, m, :]
                        else:
                            dst = part[i % 3]
                            if i >= 3:
                                dve.wait_ge(pool_done, Gp["part", i - 3])
                            i += 1
                        if g == 0:
                            dve.wait_ge(scalar_done, Sc["PT", len(UNITS) - 1])
                            dve.wait_ge(kv_out, 32)
                        Vc(dve.tensor_tensor(dst, sig[g % 4], tokens(used("proj", oq, b, o)), ALU.mult)
                           .then_inc(vector_done, 1), "proj", oq, b, o)
                        g += 1
                    if b == 0 and oq:
                        merged_low(oq - 1)
            merged_low(3)
            for oq in range(4):
                split_lo(dve, split_index["out", oq] + 1)
            post_norm(dve, 0, mix, "p1")
            norm_apply(dve, "n2")
            normed_low(dve, "n2")

            def act_low(f):
                f0 = max(f0 for f0, _ in FPARTS if f0 <= f)
                dve.wait_ge(scalar_done, Sc["a_hi", f])
                Vc(dve.tensor_tensor(a_lo[:, f - f0, :], act[f % 2], a_hi[:, f - f0, :].bitcast(F32), ALU.subtract)
                   .then_inc(vector_done, 1), "a_lo", f)

            for i, (f0, nf) in enumerate(FPARTS):
                for j in range(f0 // QT, (f0 + nf) // QT):
                    split_lo(dve, split_index["up", 0, j] + 1)
                    split_lo(dve, split_index["up", 1, j] + 1)
                    for f in range(QT * j, QT * (j + 1)):
                        dve.wait_ge(tensor_done, Tn["fup", f])
                        dve.wait_ge(scalar_done, Sc["fgate", f])
                        Vc(dve.tensor_tensor(act[f % 2], ffn_gate[f % 4], tokens(used("fup", f)), ALU.mult)
                           .then_inc(vector_done, 1), "fup", f)
                    for f in range(QT * j, QT * (j + 1)):
                        act_low(f)
                for o in range(KD):
                    if o % QT == 0:
                        split_lo(dve, split_index["down", i, o // QT] + 1)
                    if i:
                        dve.wait_ge(tensor_done, Tn["down", i, o])
                        dve.wait_ge(vector_done, Vc["down", i - 1, o]) if i > 1 else dve.wait_ge(scalar_done, Sc["down", 0, o])
                        Vc(dve.tensor_tensor(mix2[:, o, :], mix2[:, o, :], tokens(used("down", i, o)), ALU.add)
                           .then_inc(vector_done, 1), "down", i, o)
            post_norm(dve, 1, mix2, "p2")

        @block.scalar
        def _(sc):
            sc.wait_ge(cond_in, 32)
            Sc(sc.activation(crow[0:16, :], crow[0:16, :], ACT.Silu).then_inc(scalar_done, 1), "cond")
            sc.wait_ge(rowvec_in, 16 * 4)
            Sc(sc.activation(neg_a[:, :], neg_a[:, :], ACT.Exp).then_inc(scalar_done, 1), "exp_a")
            for j in range(12):
                sc.wait_ge(tensor_done, Tn["mrow", j])
                Sc(sc.copy(mrow[:, 512 * j:512 * (j + 1)], slot(used("mrow", j))[0:2, 0:512]).then_inc(scalar_done, 1), "mrow", j)
            pre_norm(sc, 0, "n1")
            split_hi(sc, 0)
            for o in range(4):
                if o % QT == 0:
                    split_hi(sc, split_index["z", o // QT] + 1)
                sc.wait_ge(tensor_done, Tn["z", o])
                Sc(sc.activation(zg[:, o, :], tokens(used("z", o)), ACT.Silu).then_inc(scalar_done, 1), "z", o)
            for o in range(6):
                if o % QT == 0:
                    split_hi(sc, split_index["xbc", o // QT] + 1)
                sc.wait_ge(vector_done, Vc["conv4", "xbc", o])
                Sc(sc.activation(xbc[:, o, :], xbc[:, o, :], ACT.Silu).then_inc(scalar_done, 1), "xbc", o)
            sc.wait_ge(tensor_done, Tn["dt_row"])
            Sc(sc.copy(dt_row, tokens(used("dt_row"))[0:16, :]).then_inc(scalar_done, 1), "dt_row")
            sc.wait_ge(vector_done, Vc["dt_abs"])
            Sc(sc.activation(sp_b, sp_b, ACT.Exp).then_inc(scalar_done, 1), "dt_exp")
            sc.wait_ge(vector_done, Vc["u_inverse"])
            Sc(sc.activation(sp_c, sp_c, ACT.Ln).then_inc(scalar_done, 1), "dt_ln")
            sc.wait_ge(tensor_done, Tn["decays"])
            s = used("decays")
            Sc(sc.activation(w_end.rearrange("p r c h -> p (r c h)"), slot(s)[:, 0:80], ACT.Exp).then_inc(scalar_done, 1))
            Sc(sc.activation(chunk_decay.rearrange("p c r h -> p r c h"),
                             slot(s)[:, 512:552].rearrange("p (r c h) -> p r c h", r=2, c=NT), ACT.Exp)
               .then_inc(scalar_done, 1), "decays")
            for c in range(NT):
                for r in range(2):
                    sc.wait_ge(tensor_done, Tn["seg", c, r])
                    if c >= 1:
                        sc.wait_ge(tensor_done, Tn["y", c - 1])
                    Sc(sc.activation(E_seg[:, r, :], slot(used("seg", c, r)), ACT.Exp).then_inc(scalar_done, 1), "seg", c, r)
                    if c == 1 and r == 0:
                        sc.wait_ge(state_out, 64)
                    if c:
                        sc.wait_ge(tensor_done, Tn["acc", c, r])
                        Sc(sc.activation(E_acc[:, r, :], slot(used("acc", c, r))[:, 0:512], ACT.Exp)
                           .then_inc(scalar_done, 1), "acc", c, r)
            for o in range(4):
                sc.wait_ge(vector_done, Vc["yz", o])
                if o >= 2:
                    sc.wait_ge(tensor_done, Tn["sq", "ssm", o - 2])
                Sc(sc.activation(squares[o % 2], zg[:, o, :], ACT.Square).then_inc(scalar_done, 1), "sq", "ssm", o)
            rstd_of(sc, "ssm", 512)

            def filters(i):
                for n in (1, 2):
                    sc.wait_ge(vector_done, Vc["arg_in", i, n])
                    h = (hid1, hid2)[n - 1]
                    Sc(sc.activation(h, h, ACT.Sin).then_inc(scalar_done, 1), "hid", i, n)
                sc.wait_ge(decay_in, 32 * (i + 1))
                for c in range(NT):
                    if c >= 2:
                        sc.wait_ge(vector_done, Vc["fsum", i, c - 2])
                    Sc(sc.activation(fsum[:, c, :], decay[:, 0, :], ACT.Exp, scale=K("neg_t", c, c + 1)).then_inc(scalar_done, 1))
                    Sc(sc.activation(hb_tmp[c % 2], decay[:, 1, :], ACT.Exp, scale=K("neg_t", c, c + 1))
                       .then_inc(scalar_done, 1), "decay", i, c)

            def filter_spectrum(i):
                for q in range(NT):
                    sc.wait_ge(tensor_done, Tn["K", i, q])
                    s = used("K", i, q)
                    w = K("spec_w", q, q + 1) if q <= 1 else 1.0 / LS
                    Sc(sc.activation(Kr[:, q, :], slot(s)[:, 0:512], ACT.Identity, scale=w).then_inc(scalar_done, 1))
                    Sc(sc.activation(Ks[:, q, :], slot(s)[:, 512:1024], ACT.Identity, scale=w)
                       .then_inc(scalar_done, 1), "K", i, q)
                    if q <= 1:
                        sc.wait_ge(tensor_done, Tn["Kn", i, q])
                        sc.wait_ge(scalar_done, Sc["K", i, q])
                        Sc(sc.activation(Ks[0:1, q, :], slot(used("Kn", i, q))[0:1, 0:512], ACT.Identity,
                                         scale=0.5 / (LP if q == 0 else LS)).then_inc(scalar_done, 1), "Kn", i, q)

            filters(0)
            for b in range(2):
                for o in range(4):
                    sc.wait_ge(tensor_done, Tn["turn", b, o])
                    dst = (v_tok, x1_tok)[b][:, :, o * P:(o + 1) * P]
                    Sc(sc.copy(dst, token_tiles(used("turn", b, o)).rearrange("p (c n) -> p c n", c=NT)).then_inc(scalar_done, 1), "turn", b, o)
            filter_spectrum(0)
            sc.wait_ge(tensor_done, Tn["z1", NT - 1])
            filters(1)
            split_hi(sc, split_index["q", 0])
            filter_spectrum(1)

            sc.wait_ge(tensor_done, Tn["hyY", 3])
            for k in range(KD):
                Sc(sc.copy(h_hi[:, k, :], hT[:, k, :]).then_inc(scalar_done, 1), "h_hi", "att", k)
            for o in range(5):
                if o % QT == 0:
                    split_hi(sc, split_index[("q", o // QT) if o < 4 else ("kv",)] + 1)
                sc.wait_ge(tensor_done, Tn["q", o])
                Sc(sc.copy(qT[:, o, :] if o < 4 else kT, tokens(used("q", o))).then_inc(scalar_done, 1), "q", o)
            sc.wait_ge(tensor_done, Tn["vT"])
            Sc(sc.copy(vT, tokens(used("vT"))).then_inc(scalar_done, 1), "vT")
            sc.wait_ge(tensor_done, Tn["v"])
            Sc(sc.copy(v_att.rearrange("p c n -> p (c n)"), token_tiles(used("v"))).then_inc(scalar_done, 1), "v")
            sc.wait_ge(tensor_done, Tn["kcT"])
            s = used("kcT")
            Sc(sc.copy(k_rows, slot(s)[:, 512:640]).then_inc(scalar_done, 1), "k_rows")
            Sc(sc.copy(kcT, slot(s)[:, 0:P]).then_inc(scalar_done, 1), "kcT")

            def exps(n):
                b, _ = UNITS[n]
                w = n_keys(b) * P
                sc.wait_ge(vector_done, Vc["negmax", n])
                for g in range(2):
                    Sc(sc.activation(S_sb[n % 3][:, g, 0:w], S_sb[n % 3][:, g, 0:w], ACT.Exp, bias=stat[:, n, 2 + g:3 + g],
                                     accum_out=stat[:, n, 6 + g:7 + g]).then_inc(scalar_done, 1))
                Sc(sc.activation(stat[:, n, 4:6], stat[:, n, 4:6], ACT.Exp).then_inc(scalar_done, 1), "exp", n)

            def probs_turned(n):
                b, _ = UNITS[n]
                w = n_keys(b) * P
                sc.wait_ge(tensor_done, Tn["PT", n])
                if n >= 3:
                    sc.wait_ge(tensor_done, Tn["att", n - 3])
                src = slot(used("PT", n)).rearrange("p (g n) -> p g n", g=2)
                Sc(sc.copy(PT_sb[n % 3][:, :, 0:w], src[:, :, 0:w]).then_inc(scalar_done, 1), "PT", n)

            for n in range(len(UNITS) + 1):
                if n < len(UNITS):
                    exps(n)
                if n >= 1:
                    probs_turned(n - 1)

            def merged_high(oq):
                for m in range(QT * oq, QT * (oq + 1)):
                    sc.wait_ge(pool_done, Gp["merged", m, 2])
                    if m == 6:
                        sc.wait_ge(tensor_done, Tn["gate", 3, 2, 1])
                    Sc(sc.copy(m_hi[m], merged[:, m, :]).then_inc(scalar_done, 1), "m_hi", m)

            order = [(oq, b, o) for oq in range(4) for b in range(3) for o in range(QT)]
            for g, (oq, b, o) in enumerate(order):
                if o == 0:
                    split_hi(sc, split_index["gate", oq, b] + 1)
                sc.wait_ge(tensor_done, Tn["gate", oq, b, o])
                if g >= 4:
                    sc.wait_ge(vector_done, Vc[("proj",) + order[g - 4]])
                else:
                    sc.wait_ge(vector_done, Vc["probs", len(UNITS) - 1])
                    sc.wait_ge(tensor_done, Tn["att", len(UNITS) - 1])
                Sc(sc.activation(sig[g % 4], tokens(used("gate", oq, b, o)), ACT.Sigmoid)
                   .then_inc(scalar_done, 1), "gate", oq, b, o)
                if b == 0 and o == QT - 1 and oq:
                    merged_high(oq - 1)
            merged_high(3)
            mixed(sc, 0, mix, "p1")
            pre_norm(sc, 1, "n2")
            for i, (f0, nf) in enumerate(FPARTS):
                for j in range(f0 // QT, (f0 + nf) // QT):
                    split_hi(sc, split_index["up", 0, j] + 1)
                    for f in range(QT * j, QT * (j + 1)):
                        sc.wait_ge(tensor_done, Tn["fgate", f])
                        if f >= 4:
                            sc.wait_ge(vector_done, Vc["fup", f - 4])
                        Sc(sc.activation(ffn_gate[f % 4], tokens(used("fgate", f)), ACT.Silu)
                           .then_inc(scalar_done, 1), "fgate", f)
                    split_hi(sc, split_index["up", 1, j] + 1)
                    for f in range(QT * j, QT * (j + 1)):
                        sc.wait_ge(vector_done, Vc["fup", f])
                        Sc(sc.copy(a_hi[:, f - f0, :], act[f % 2]).then_inc(scalar_done, 1), "a_hi", f)
                for o in range(KD):
                    if o % QT == 0:
                        split_hi(sc, split_index["down", i, o // QT] + 1)
                    if i == 0:
                        sc.wait_ge(tensor_done, Tn["down", i, o])
                        Sc(sc.copy(mix2[:, o, :], tokens(used("down", i, o))).then_inc(scalar_done, 1), "down", i, o)
                    elif i == len(FPARTS) - 1:
                        sc.wait_ge(vector_done, Vc["down", i, o])
                        Sc(sc.activation(hT[:, o, :], mix2[:, o, :], ACT.Square).then_inc(scalar_done, 1), "sq", "p2", o)
            rstd_of(sc, "p2", D)

        @block.gpsimd
        def _(pool):
            pool.wait_ge(vector_done, Vc["dA"])
            for c in range(NT):
                for r in range(2):
                    if c >= 1:
                        pool.wait_ge(tensor_done, Tn["acc", c - 1, r] if c > 1 else Tn["seg", 0, r])
                    tri = K(("t_le_i", "t_ge_i")[r]).unsqueeze(1).broadcast_to([P, HEADS, P])
                    d = dA[:, c, 8 * r:8 * r + 8].unsqueeze(2).broadcast_to([P, HEADS, P])
                    Gp(pool.tensor_tensor(dA_tri[:, r, :].rearrange("p (h n) -> p h n", h=HEADS), tri, d, ALU.mult)
                       .then_inc(pool_done, 1), "dA_tri", c, r)
            i = 0
            for oq in range(4):
                for b in (1, 2):
                    for o in range(QT):
                        m = QT * oq + o
                        pool.wait_ge(vector_done, Vc["proj", oq, b, o])
                        if b == 2:
                            pool.wait_ge(pool_done, Gp["merged", m, 1])
                        Gp(pool.tensor_tensor(merged[:, m, :], merged[:, m, :], part[i % 3], ALU.add).then_inc(pool_done, 1), "part", i)
                        Gp.named[("merged", m, b)] = Gp.count
                        i += 1

        @block.sync
        def _(sp):
            l = layer
            sp.dma_start(crow[0:8, :], A["c_ctx"].rearrange("(k p) -> k p", p=P)).then_inc(cond_in, 16)
            sp.dma_start(crow[8:16, :], A["c"][0].rearrange("(k p) -> k p", p=P)).then_inc(cond_in, 16)
            for name, src in (("mix_pre", "norm_mix_pre"), ("mix_post", "norm_mix_post"), ("ffn_pre", "norm_ffn_pre"),
                              ("ffn_post", "norm_ffn_post"), ("hy_b", "hy_conv_b"), ("ssm_b", "ssm_conv_b"), ("ssm_norm", "ssm_norm")):
                at, w = ROWS[name]
                sp.dma_start(prow[at:at + w, :], A[src][l].rearrange("(k p) -> k p", p=P)).then_inc(rows_in, 16)
            for name, src in (("hy_w", "hy_conv_w"), ("ssm_w", "ssm_conv_w")):
                at, w = ROWS[name]
                sp.dma_start(prow[at:at + w, :], A[src][l].rearrange("j (k p) -> (j k) p", p=P)).then_inc(rows_in, 16)
            sp.dma_start(brow[0:48, :], A["ada_b"][l].rearrange("(k p) -> k p", p=P)).then_inc(rows_in, 16)
            for j, src in enumerate(("hy_b1", "hy_freq1", "hy_b2", "hy_freq2")):
                sp.dma_start(hrow[j:j + 1, :], A[src][l].unsqueeze(0)).then_inc(hidden_in, 16)
            sp.dma_start(dt_bias[:, :], A["ssm_dt_bias"][l].rearrange("r h -> (r h)").partition_broadcast(P)).then_inc(rowvec_in, 16)
            sp.dma_start(neg_a[:, :], A["ssm_a_log"][l].rearrange("r h -> (r h)").partition_broadcast(P)).then_inc(rowvec_in, 16)
            sp.dma_start(sinks[:, :], A["attn_sink"][l].partition_broadcast(P)).then_inc(rowvec_in, 16)
            sp.dma_start(dskip2[:, :], A["ssm_d"][l].rearrange("r h -> (r h)").partition_broadcast(P)).then_inc(rowvec_in, 16)
            for r in range(2):
                for g in range(2):
                    sp.dma_start(init_rows[:, 512 * r:512 * r + 512].rearrange("p (h g n) -> p h g n", h=4, g=2)[:, :, g, :],
                                   A["state_ssm"][0, l, r, 4 * g:4 * g + 4].rearrange("h p n -> p h n")).then_inc(state_in, 16)
            sp.dma_start(w1sb, A["hy_w1"][l]).then_inc(filt_in, 16)
            sp.dma_start(w2sb, A["hy_w2"][l]).then_inc(filt_in, 16)
            sp.dma_start(bias_row, A["hy_bias"][l][0:1, :]).then_inc(filt_in, 16)

            def filter_loads(i):
                sp.dma_start(w3, A["hy_w3"][l][:, 1024 * i:1024 * (i + 1)]).then_inc(w3_in, 16)
                sp.dma_start(feat, A["feat"]).then_inc(w3_in, 16)
                for r in range(2):
                    src = A["hy_decay"][l][1024 * i + 512 * r:1024 * i + 512 * r + 512]
                    sp.dma_start(decay[:, r, :], src.partition_broadcast(P)).then_inc(decay_in, 16)

            def beside(name):
                if name == ("hy", 0):
                    sp.wait_ge(tensor_done, Tn["dt_row"])
                    sp.dma_start(arena[:, DFT_AT:DFT_AT + N_DFT], A["consts"][:, N_CONST:N_CONST + N_DFT]).then_inc(dft_in, 16)
                elif name == ("hy", 2):
                    sp.wait_ge(vector_done, Vc["end_rows"])
                    for r in range(2):
                        for g in range(2):
                            sp.dma_start(O["new_ssm"][0, l, r, 4 * g:4 * g + 4].rearrange("h p n -> p h n"),
                                         end_rows[:, 512 * r:512 * r + 512].rearrange("p (h g n) -> p h g n", h=4, g=2)[:, :, g, :]
                                         ).then_inc(state_out, 16)
                    sp.wait_ge(vector_done, Vc["y", NT - 1])
                    filter_loads(0)
                elif name == ("hy", 3):
                    sp.wait_ge(vector_done, Vc["bias", 0, 1])
                    sp.dma_start(bias_row, A["hy_bias"][l][1:2, :]).then_inc(filt_in, 16)
                elif name == ("q", 0):
                    sp.wait_ge(vector_done, Vc["Y", 0, NT - 1])
                    filter_loads(1)
                elif name == ("kv",):
                    sp.wait_ge(tensor_done, Tn["hyY", 3])
                    sp.dma_start(kc_rows, A["cache_k"][0, l].rearrange("s g n -> s (g n)")).then_inc(cache_in, 16)
                    sp.dma_start(v_ctx, A["cache_v"][0, l].rearrange("s g n -> s (g n)")).then_inc(cache_in, 16)
                elif name == ("proj", 0, 0):
                    sp.wait_ge(scalar_done, Sc["k_rows"])
                    sp.dma_start(O["new_k"][0, l].rearrange("s g n -> s (g n)"), k_rows).then_inc(kv_out, 16)
                    sp.dma_start(O["new_v"][0, l].rearrange("s g n -> s (g n)"), v_att[:, 0, :]).then_inc(kv_out, 16)

            for j in range(12):
                if j >= ADA_RING:
                    sp.wait_ge(tensor_done, Tn["ada_used", j - ADA_RING])
                sp.dma_start(ada_view(j), k_major(ada, 512 * j, 512)).then_inc(ada_in[j % ADA_RING], 16)
            for n, (name, kind, k, cols, src) in enumerate(blocks):
                beside(name)
                if n < RAW:
                    sp.wait_ge(tensor_done, Tn["ada_used", 9])
                elif n - RAW in split_blocks:
                    sp.wait_ge(vector_done, Vc["part", split_blocks.index(n - RAW)])
                else:
                    sp.wait_ge(tensor_done, Tn["used", n - RAW])
                view, arrived = raw_view(n), weights_in[n % RAW]
                if kind == "q":
                    for g in range(KV):
                        for kk in range(KD):
                            at = IN_Q + 256 * g + P * src
                            sp.dma_start(view[:, kk, :].rearrange("p (t g n) -> p t g n", t=QT, g=KV)[:, :, g, :],
                                         w_in[kk * P:(kk + 1) * P, at:at + P].rearrange("p (t n) -> p t n", t=QT)
                                         ).then_inc(arrived, 16)
                elif kind == "att":
                    for g in range(KV):
                        sp.dma_start(view[64 * g:64 * g + 64, :, :],
                                     A["attn_proj"][l][256 * g:256 * g + 256, QT * P * src:QT * P * (src + 1)]
                                     .rearrange("(t p) n -> p t n", p=HD)).then_inc(arrived, 16)
                else:
                    sp.dma_start(view, src).then_inc(arrived, 16)
            sp.wait_ge(state_out, 64)
            sp.wait_ge(kv_out, 32)

    return {"T": Tn.named, "V": Vc.named, "S": Sc.named, "G": Gp.named}


INPUTS = ["x_prompt", "x_sample", "c", "cache_k", "cache_v", "state_ssm", "c_ctx", "ada_w", "ada_b", "norm_mix_pre",
          "norm_mix_post", "norm_ffn_pre", "norm_ffn_post", "w_in", "hy_conv_w", "hy_conv_b", "hy_w1", "hy_b1", "hy_freq1",
          "hy_w2", "hy_b2", "hy_freq2", "hy_w3", "hy_decay", "hy_bias", "ssm_conv_w", "ssm_conv_b", "ssm_a_log",
          "ssm_dt_bias", "ssm_d", "ssm_norm", "attn_sink", "hy_proj", "ssm_proj", "attn_proj", "w_out", "ffn_w_gate",
          "ffn_w_up", "ffn_w_down"]
OUTPUTS = [("y_prompt", (1, LP, D)), ("y_sample", (1, LS, D)), ("new_k", (1, DEPTH, LP, KV, HD)),
           ("new_v", (1, DEPTH, LP, KV, HD)), ("new_ssm", (1, DEPTH, 2, HEADS, HD, 64))]


def kernel(**inputs):
    import concourse.bacc as bacc
    from concourse.bass_utils import run_bass_kernel_spmd as run

    arrays = {f"in_{n}_dram": np.ascontiguousarray(inputs[n]) for n in INPUTS}
    arrays["in_consts_dram"] = constant_tables()
    arrays["in_feat_dram"] = filter_features()

    def program(known):
        nc = bacc.Bacc("TRN2", target_bir_lowering=False, num_devices=1)
        A = {n: nc.dram_tensor(f"in_{n}_dram", arrays[f"in_{n}_dram"].shape, F32, kind="ExternalInput").ap()
             for n in INPUTS + ["consts", "feat"]}
        O = {n: nc.dram_tensor(f"out_{n}_dram", shape, F32, kind="ExternalOutput").ap() for n, shape in OUTPUTS}
        return nc, build(nc, A, O, known)

    _, steps = program({})
    nc, _ = program(steps)
    r = run(nc, [arrays], core_ids=[0])
    return tuple(r.results[0][f"out_{n}_dram"] for n, _ in OUTPUTS)
```

```python
from contextlib import ExitStack
import numpy as np
import concourse.bass as bass
from concourse import mybir

ALU = mybir.AluOpType
ACT = mybir.ActivationFunctionType
F32 = mybir.dt.float32
F32R = mybir.dt.float32r

P = 128
D = 1024
DEPTH = 2
LP, LS = 128, 512
T = LP + LS
NT = T // P
KD = D // P
GRID_W = 64
HY_W = 512
BANDS = 16
FEAT = 1 + 2 * BANDS
HID = 64
HEADS, HD = 8, 64
KV = 2
WINDOW = 128
FF = 2816
KF = FF // P
EPS = 1e-6
NEG = -1.0e30
IN_HY, IN_Z, IN_XBC, IN_DT, IN_Q, IN_K, IN_V, IN_G = 0, 1536, 2048, 2816, 2832, 3344, 3472, 3600
N_IN = 6672
QT = 2
WB = KD * QT * P
RAW = 2
PARTS = 2
ADA_RING = 3
ADA_FIRST = 6
ADA_HY, ADA_LAST = 3, 4
RING_SIZE = (RAW + 2 * PARTS) * WB
ADA_WB = RING_SIZE // ADA_RING
FPARTS = ((0, 8), (8, 8), (16, 6))
TWO_PI = 2.0 * np.pi

CONST = {}
_at = 0
for _n, _w in (("ident", P), ("ones", P), ("t_le_i", P), ("t_ge_i", P), ("t_gt_j", P), ("t_lt_j", P), ("rotate", P),
               ("cos", LS), ("sin", LS), ("mask", 512), ("mask_first", 384), ("dft_c_p", P), ("dft_s_p", P),
               ("idft_s_p", P), ("spec_w", 3), ("neg_t", NT), ("eps", 1),
               ("cos_even", LS), ("cos_odd", LS), ("sin_even", LS), ("sin_odd", LS),
               ("cos_odd_t", LS), ("sin_even_t", LS), ("sin_odd_t", LS)):
    CONST[_n] = (_at, _w)
    _at += _w
N_CONST = CONST["cos_even"][0]
N_DFT = _at - N_CONST
LH = LS // 2


def latents_by_parity(a):
    return np.concatenate([a[..., 0::2], a[..., 1::2]], -1)


def constant_tables():
    c = np.zeros((P, N_CONST + N_DFT), np.float64)

    def put(name, a):
        at, w = CONST[name]
        c[:a.shape[0], at:at + w] = a.reshape(a.shape[0], -1)

    p, f = np.arange(P)[:, None], np.arange(P)[None]
    put("ident", (p == f) * 1.0)
    put("ones", np.ones((P, P)))
    put("t_le_i", (p <= f) * 1.0)
    put("t_ge_i", (p >= f) * 1.0)
    put("t_gt_j", (p > f) * 1.0)
    put("t_lt_j", (p < f) * 1.0)
    rot = np.zeros((P, P))
    for m in range(P):
        if m % 32 < 16:
            rot[m + 16, m] = -1.0
        else:
            rot[m - 16, m] = 1.0
    put("rotate", rot)
    nq = HD // 4
    inv = 10000.0 ** (-np.arange(nq) / nq)
    tok = np.arange(LS)
    pos = np.stack([tok // GRID_W, tok % GRID_W])
    ang = np.zeros((P, LS))
    for m in range(P):
        ang[m] = pos[(m % HD) // 32] * np.float32(inv[m % 16])
    put("cos", np.cos(ang))
    put("sin", np.sin(ang))
    before = np.where(f >= p, 0.0, NEG)
    after = np.where(f <= p, 0.0, NEG)
    zero = np.zeros((P, P))
    put("mask", np.concatenate([zero, before, zero, after], 1))
    put("mask_first", np.concatenate([zero, zero, after], 1))
    i = np.arange(LP)
    cosine, sine = np.cos(np.pi * np.outer(i, i) / LP), np.sin(np.pi * np.outer(i, i) / LP)
    forward, inverse = sine.copy(), sine.copy()
    forward[:, 0] = (-1.0) ** i
    inverse[0, :] = (-1.0) ** i
    put("dft_c_p", cosine)
    put("dft_s_p", forward)
    put("idft_s_p", inverse)
    u = np.arange(LH)
    lay = lambda a: a.reshape(2, P, LH).transpose(1, 0, 2)
    for parity, name in enumerate(("even", "odd")):
        angle = np.pi * np.outer(2 * u + parity, u) / LS
        cosine, sine = np.cos(angle), np.sin(angle)
        sine[:, 0] = (-1.0) ** u
        put("cos_" + name, lay(cosine))
        put("sin_" + name, lay(sine))
        put("sin_" + name + "_t", lay(sine.T))
    put("cos_odd_t", lay(cosine.T))
    w = np.stack([np.full(P, 1.0 / LP), np.full(P, 1.0 / LS), np.full(P, 1.0 / LS)], 1)
    w[0] *= (0.5, 0.5, 0.0)
    put("spec_w", w)
    t = np.concatenate([np.arange(LP) / LP, latents_by_parity(np.arange(LS) / LS)])
    put("neg_t", -t.reshape(NT, P).T)
    put("eps", np.full((P, 1), EPS))
    return c.astype(np.float32)


def filter_features():
    t = np.concatenate([np.arange(LP) / LP, latents_by_parity(np.arange(LS) / LS)])
    ang = 2.0 * np.pi * t[None] * np.arange(1, BANDS + 1)[:, None]
    return np.concatenate([t[None], np.cos(ang), np.sin(ang)]).astype(np.float32)


ROWS = {}
_at = 0
for _n, _w in (("mix_pre", 8), ("mix_post", 8), ("ffn_pre", 8), ("ffn_post", 8), ("hy_w", 36), ("hy_b", 12),
               ("ssm_w", 18), ("ssm_b", 6), ("ssm_norm", 4)):
    ROWS[_n] = (_at, _w)
    _at += _w
N_ROWS = _at


class Steps:

    def __init__(self, known):
        self.known, self.named, self.count = known, {}, 0

    def __call__(self, instruction, *name):
        self.count += 1
        if name:
            self.named[name] = self.count
        return instruction

    def __getitem__(self, name):
        return self.known.get(name if isinstance(name, tuple) else (name,), 1)


def build(nc, A, O, known):
    tiles = ExitStack()
    with tiles:
        def sb(name, cols, rows=P):
            return tiles.enter_context(nc.sbuf_tensor(name, [rows, cols], F32))

        def sem(name):
            return tiles.enter_context(nc.semaphore(name))

        const = sb("const", N_CONST)

        def K(name, a=0, b=None, rows=P):
            at, w = CONST[name]
            if at >= N_CONST:
                return arena[0:rows, DFT_AT + at - N_CONST + a:DFT_AT + at - N_CONST + (w if b is None else b)]
            return const[0:rows, at + a:at + (w if b is None else b)]

        def tiled(t, base, n, w=T):
            return t[:, base:base + n * w].rearrange("p (n w) -> p n w", n=n)

        def sb_and_parts(name, cols):
            buffer = sb(name, cols)
            return buffer, nc.alloc_sbuf_tensor_at(name + "_parts", [P, cols], F32R, offset=nc.sbuf_base - 4 * cols)

        xT = tiled(sb("residual", KD * T), 0, KD)
        normed, normed_parts = sb_and_parts("normed", KD * T)
        hT = tiled(normed, 0, KD)
        ring, ring_parts = sb_and_parts("weights", RING_SIZE)
        pcol = sb("param_cols", N_ROWS)
        bcol = sb("bias_cols", 52)
        modT = sb("modulation", 96)[:, :].rearrange("p (n c) -> p n c", c=2)
        scale_pre = sb("scale_pre", 32)[:, :].rearrange("p (s n c) -> p s n c", s=2, c=2)
        gain_post = sb("gain_post", 32)[:, :].rearrange("p (s n c) -> p s n c", s=2, c=2)
        condT = sb("cond", 16)
        dt_bias = sb("dt_bias", 16)
        neg_a = sb("neg_a", 16)
        dskip2 = sb("dskip2", 16)
        dskip = sb("dskip", 4)
        sinks = sb("sinks", 8)
        hy_bias = sb("hy_bias", 1, 1)
        DFT_AT = 20760
        arena, arena_parts = sb_and_parts("arena", DFT_AT + (KD + 1) * T)
        ps = tiles.enter_context(nc.psum_tensor("ps", [P, 4 * 1024], F32))

        tensor_done, vector_done = sem("tensor_done"), sem("vector_done")
        scalar_done, pool_done = sem("scalar_done"), sem("pool_done")
        weights_in = [sem(f"weights_in{i}") for i in range(RAW)]
        ada_in = [sem(f"ada_in{i}") for i in range(ADA_RING)]
        dft_in, ada_first_in = sem("dft_in"), sem("ada_first_in")
        const_in, x_in, y_out = sem("const_in"), sem("x_in"), sem("y_out")
        cond_in, rows_in, rowvec_in, filt_in = sem("cond_in"), sem("rows_in"), sem("rowvec_in"), sem("filt_in")
        decay_in, w3_in, state_in, cache_in = sem("decay_in"), sem("w3_in"), sem("state_in"), sem("cache_in")
        state_out, kv_out, hidden_in = sem("state_out"), sem("kv_out"), sem("hidden_in")
        layer_sems = [tensor_done, vector_done, scalar_done, pool_done, *weights_in, *ada_in, dft_in, ada_first_in, rows_in,
                      rowvec_in, filt_in, decay_in, w3_in, state_in, cache_in, state_out, kv_out, hidden_in]

        def new_steps():
            return [Steps(known.get(e, {})) for e in "TVSG"]

        def slot(s):
            return ps[:, 1024 * s:1024 * s + 1024]

        def tokens(s):
            return ps[:, 1024 * s + 512 - T // 2:1024 * s + 512 + T // 2]

        def token_tiles(s):
            return ps[:, 1024 * s + 384:1024 * s + 1024]

        mix2 = tiled(arena, 10240, 8)
        rstd = arena[:, 8920:8920 + T]

        def add_to_residual(dve, Vc, i, src, k, normed_elsewhere=False):
            if not normed_elsewhere:
                Vc(dve.tensor_tensor(src[:, k, :], src[:, k, :], rstd, ALU.mult).then_inc(vector_done, 1))
                dve.wait_ge(vector_done, Vc.count)
            for c, (lo, hi) in enumerate(((0, LP), (LP, T))):
                Vc(dve.scalar_tensor_tensor(out=xT[:, k, lo:hi], in0=src[:, k, lo:hi], scalar=gain_post[:, i, k, c:c + 1],
                                            in1=xT[:, k, lo:hi], op0=ALU.mult, op1=ALU.add).then_inc(vector_done, 1), "x", i, k)

        xrows = arena[:, 0:NT * D].rearrange("p (n d) -> p n d", d=D)
        crow = arena[0:16, NT * D:NT * D + P]
        with nc.Block() as block:
            Tn, Vc, Sc, Gp = new_steps()

            @block.sync
            def _(sp):
                sp.dma_start(const[:, :], A["consts"][:, 0:N_CONST]).then_inc(const_in, 16)
                sp.dma_start(crow[0:8, :], A["c_ctx"].rearrange("(k p) -> k p", p=P)).then_inc(cond_in, 16)
                sp.dma_start(crow[8:16, :], A["c"][0].rearrange("(k p) -> k p", p=P)).then_inc(cond_in, 16)
                sp.dma_start(xrows[:, 0, :], A["x_prompt"][0]).then_inc(x_in, 16)
                sp.dma_start(xrows[:, 1:NT, :], A["x_sample"][0].rearrange("(n p) d -> p n d", p=P)).then_inc(x_in, 16)

            @block.tensor
            def _(pe):
                pe.wait_ge(const_in, 16)
                pe.wait_ge(x_in, 32)
                for k in range(KD):
                    if k >= 4:
                        pe.wait_ge(vector_done, k - 3)
                    for n in range(NT):
                        t = pe.transpose(token_tiles(k % 4)[:, n * P:(n + 1) * P], xrows[:, n, k * P:(k + 1) * P], K("ident"))
                    t.then_inc(tensor_done, 1)
                pe.wait_ge(vector_done, KD - 3)
                pe.wait_ge(scalar_done, 1)
                pe.transpose(slot(0)[:, 0:16], crow, K("ident", 0, 16, 16)).then_inc(tensor_done, 1)

            @block.scalar
            def _(sc):
                sc.wait_ge(cond_in, 32)
                sc.activation(crow, crow, ACT.Silu).then_inc(scalar_done, 1)

            @block.vector
            def _(dve):
                dve.memset(arena[:, 10240:10240 + KD * T], 0.0)
                dve.memset(rstd, 0.0)
                dve.memset(gain_post[:, 1], 0.0)
                for k in range(KD):
                    dve.wait_ge(tensor_done, k + 1)
                    dve.tensor_copy(xT[:, k, :], token_tiles(k % 4)).then_inc(vector_done, 1)
                dve.wait_ge(tensor_done, KD + 1)
                dve.tensor_copy(condT[:, :], slot(0)[:, 0:16]).then_inc(vector_done, 1)

        nc.sync.sem_clear(tensor_done)
        nc.sync.sem_clear(vector_done)
        nc.sync.sem_clear(scalar_done)
        nc.all_engine_barrier()

        with nc.Fori(0, DEPTH) as layer:
            named = layer_body(nc, A, O, known, layer, locals())
            for s in layer_sems:
                nc.sync.sem_clear(s)
            nc.all_engine_barrier()

        last_update = Steps({})
        with nc.Block() as block:
            @block.vector
            def _(dve):
                for k in range(KD):
                    add_to_residual(dve, last_update, 1, mix2, k)
                for n in range(NT):
                    dve.wait_ge(tensor_done, n + 1)
                    dve.tensor_copy(xrows[:, n, :], slot(n % 4)).then_inc(vector_done, 1)

            @block.tensor
            def _(pe):
                pe.wait_ge(vector_done, last_update.count)
                for n in range(NT):
                    if n >= 4:
                        pe.wait_ge(vector_done, last_update.count + n - 3)
                    for k in range(KD):
                        t = pe.transpose(slot(n % 4)[:, k * P:(k + 1) * P], xT[:, k, n * P:(n + 1) * P], K("ident"))
                    t.then_inc(tensor_done, 1)

            @block.sync
            def _(sp):
                for n in range(NT):
                    sp.wait_ge(vector_done, last_update.count + n + 1)
                    dst = O["y_prompt"][0] if n == 0 else O["y_sample"][0, (n - 1) * P:n * P, :]
                    sp.dma_start(dst, xrows[:, n, :]).then_inc(y_out, 16)
                sp.wait_ge(y_out, 16 * NT)
    return named


def layer_body(nc, A, O, known, layer, env):
    K, tiled, xT, hT, ring, pcol, bcol, modT = (env[n] for n in ("K", "tiled", "xT", "hT", "ring", "pcol", "bcol", "modT"))
    scale_pre, gain_post, condT, dt_bias, neg_a = (env[n] for n in ("scale_pre", "gain_post", "condT", "dt_bias", "neg_a"))
    dskip2, dskip, sinks, arena, slot, tokens = (env[n] for n in ("dskip2", "dskip", "sinks", "arena", "slot", "tokens"))
    tensor_done, vector_done, scalar_done, pool_done = (env[n] for n in ("tensor_done", "vector_done", "scalar_done", "pool_done"))
    weights_in, hidden_in, ada_in, dft_in, ada_first_in = (
        env[n] for n in ("weights_in", "hidden_in", "ada_in", "dft_in", "ada_first_in"))
    normed_parts, ring_parts, arena_parts, token_tiles, DFT_AT = (
        env[n] for n in ("normed_parts", "ring_parts", "arena_parts", "token_tiles", "DFT_AT"))
    mix2, rstd, add_to_residual = (env[n] for n in ("mix2", "rstd", "add_to_residual"))
    rows_in, rowvec_in, filt_in, decay_in = (env[n] for n in ("rows_in", "rowvec_in", "filt_in", "decay_in"))
    w3_in, state_in, cache_in, state_out, kv_out = (env[n] for n in ("w3_in", "state_in", "cache_in", "state_out", "kv_out"))
    Tn, Vc, Sc, Gp = (Steps(known.get(e, {})) for e in "TVSG")

    def row(name, k, rows=1):
        return pcol[:, ROWS[name][0] + k:ROWS[name][0] + k + rows]

    prow = arena[:, 0:P]
    brow = arena[:, P:2 * P]
    hrow = arena[0:4, 6600:6600 + HID]
    mrow = arena[0:2, 3 * P:3 * P + 6 * D]
    squares = [arena[:, 7000 + T * i:7000 + T * (i + 1)] for i in range(3)]
    lnvar = arena[:, 7000 + 4 * T:7000 + 5 * T]
    apart = {2: (4 * ADA_FIRST, 4 * ADA_FIRST + QT * ADA_HY, arena[0:2, 18944:18944 + QT * P * ADA_HY]),
             3: (4 * ADA_FIRST + QT * ADA_HY, 48 - QT * ADA_LAST, ring[0:2, RAW * WB:(RAW + 1) * WB]),
             4: (48 - QT * ADA_LAST, 48, arena[0:2, 15360:15360 + QT * P * ADA_LAST])}

    def ffn_row(i, j, n=1):
        lo, _, rows = apart[i]
        return rows[:, (j - lo) * P:(j - lo + n) * P]

    h_hi = tiled(arena_parts, DFT_AT, KD)
    h_lo = [tiled(arena_parts, 10240, KD), tiled(normed_parts, 0, KD)]
    zg = tiled(arena, 0, 4)
    xbc = tiled(arena, 2560, 6)
    BT, CT = xbc[:, 4, :], xbc[:, 5, :]
    x_tok = arena[:, 6400:6400 + NT * 512].rearrange("p (c n) -> p c n", c=NT)
    B_tok = arena[:, 8960:8960 + T].rearrange("p (c n) -> p c n", c=NT)
    at = 8960 + T
    dts = arena[:, at:at + 80].rearrange("p (c m) -> p c m", c=NT)
    dA = arena[:, at + 80:at + 160].rearrange("p (c m) -> p c m", c=NT)
    w_end = arena[:, at + 160:at + 240].rearrange("p (r c h) -> p r c h", r=2, c=NT)
    chunk_decay = arena[:, at + 240:at + 280].rearrange("p (c r h) -> p c r h", c=NT, r=2)
    at += 280
    H = arena[:, at:at + 2048].rearrange("p (r c n) -> p r c n", r=2, c=4)
    H_end = arena[:, at + 2048:at + 2560].rearrange("p (r n) -> p r n", r=2)
    at += 2560
    SSD_AT = RAW * WB + T + 4096
    xdt = [[arena[:, at:at + 512], arena[:, at + 512:at + 1024]],
           [H_end.rearrange("p r n -> p (r n)"), ring[:, SSD_AT + 2560:SSD_AT + 3072]]]
    xw_at = at + 1024
    xw = [arena[:, at + 1024:at + 1536], arena[:, at + 1536:at + 2048]]
    at += 2048
    dA_tri = arena[:, at:at + 2048].rearrange("p (r n) -> p r n", r=2)
    E_seg = [a.rearrange("p (r n) -> p r n", r=2) for a in (arena[:, at + 2048:at + 4096], ring[:, SSD_AT:SSD_AT + 2048])]
    dt_row = arena[0:16, at:at + T]
    init_rows = arena[0:64, at + 2048:at + 3072]
    sp_a, sp_b, sp_c = (arena[:, at + 3072 + 80 * i:at + 3152 + 80 * i] for i in range(3))
    at += 4096
    C_dec = [arena[:, a:a + 1024].rearrange("p (r n) -> p r n", r=2) for a in (at, xw_at)]
    E_acc = C_dec
    end_rows = arena[0:64, at:at + 1024]
    G_tri = [a.rearrange("p (r g n) -> p r g n", r=2, g=2)
             for a in (arena[:, at + 1024:at + 1536], ring[:, SSD_AT + 2048:SSD_AT + 2560])]
    at += 1536
    xskip = xbc[:, 0:4, :]
    assert at <= 20120
    ssmY = zg
    v_tok = arena[:, 2560:5120].rearrange("p (c n) -> p c n", c=NT)
    x2T = tiled(arena, 2560, 4)
    x1_tok = arena[:, 5120:7680].rearrange("p (c n) -> p c n", c=NT)
    fsum = arena[:, 7680:10240].rearrange("p (c n) -> p c n", c=NT)
    fdif = arena[:, 10240:12800].rearrange("p (c n) -> p c n", c=NT)
    Yr, Ys = fsum, fdif
    Kr = arena[:, 12800:15360].rearrange("p (c n) -> p c n", c=NT)
    Ks = arena[:, 15360:17920].rearrange("p (c n) -> p c n", c=NT)
    FILT_AT = RAW * WB
    hid2 = ring[0:HID, FILT_AT:FILT_AT + T]
    w3 = [ring[0:HID, FILT_AT + T + 1024 * i:FILT_AT + T + 1024 * (i + 1)] for i in range(2)]
    decay = [ring[:, FILT_AT + T + 1024 * i:FILT_AT + T + 1024 * (i + 1)].rearrange("p (r n) -> p r n", r=2) for i in (2, 3)]
    arg_2 = arena[0:HID, 15360:15360 + T]
    feat = arena[0:FEAT, 17800:17800 + T]
    hid1 = arena[0:HID, 18440:18440 + T]
    arg_k = arena[0:HID, 19080:19080 + T]
    hb_tmp = [arena[:, 14720:15232], arena[:, 15232:15744]]
    conv_raw = [arena[:, 18944 + T * i:18944 + T * (i + 1)] for i in range(2)]
    w1sb, w2sb = arena[0:FEAT, 20120:20120 + HID], arena[0:HID, 20184:20184 + HID]
    bias_row = arena[0:1, 20248:20760]
    hyY = tiled(arena, 5120, 4)
    U_c, U_s, T_c, T_s = (arena[:, DFT_AT + N_DFT + 512 * i:DFT_AT + N_DFT + 512 * (i + 1)] for i in range(4))
    K_mid = [ring[0:1, FILT_AT + T + 2048 + 512 * i:FILT_AT + T + 2048 + 512 * (i + 1)] for i in range(2)]
    U_mid = arena[0:1, 19712:20224]
    mid_a, mid_b = (ring[0:1, FILT_AT + T + 512 * i:FILT_AT + T + 512 * (i + 1)] for i in range(2))
    ODD_AT = (RAW + PARTS + 1) * WB
    U_odd = [[ring[:, ODD_AT + 1024 * a + 512 * i:ODD_AT + 1024 * a + 512 * (i + 1)] for i in range(2)] for a in range(2)]
    prod_a, prod_b = arena[:, 17920:18432], arena[:, 18432:18944]
    attY = tiled(arena, 2560, 4)
    qT = tiled(arena, 7680, 4)
    kT = arena[:, 10240:10240 + T]
    v_att = arena[:, 10880:10880 + T].rearrange("p (c n) -> p c n", c=NT)
    k_rows = arena[:, 11520:11520 + P]
    kc_rows = arena[:, 11648:11648 + P]
    kcT = arena[:, 11776:11776 + P]
    v_ctx = arena[:, 11904:11904 + P]
    S_sb = [arena[:, 12032 + 1024 * i:12032 + 1024 * (i + 1)].rearrange("p (g n) -> p g n", g=2) for i in range(3)]
    PT_sb = [arena[:, 15104 + 1024 * i:15104 + 1024 * (i + 1)].rearrange("p (g n) -> p g n", g=2) for i in range(3)]
    vT = arena[:, 19456:19456 + T]
    rot_tmp = [arena[:, 18176 + 512 * i:18176 + 512 * (i + 1)] for i in range(2)]
    stat = arena[:, 19200:19200 + 200].rearrange("p (n c) -> p n c", c=10)
    merged = tiled(arena, 7680, 8)
    place = [arena[:, 12800 + T * i:12800 + T * (i + 1)] for i in range(5)]
    sig, part = place[0:3], place[3:5]
    y_lo = [tiled(arena_parts, a, 4) for a in (5120, 0, 2560)]
    hi_a = [arena_parts[:, 16000 + T * i:16000 + T * (i + 1)] for i in range(4)]
    hi_b = [arena_parts[:, a:a + T] for a in (18560, 19200, 19840, DFT_AT + KD * T)]
    y_hi = [hi_a, hi_b, hi_a]
    m_lo = tiled(arena_parts, 7680, 8)
    m_hi = [arena_parts[:, a + T * i:a + T * (i + 1)] for a in (5120, 0) for i in range(4)]
    mix = tiled(arena, DFT_AT, 8)
    a_hi, a_lo = tiled(arena_parts, 0, KD), tiled(arena_parts, KD * T, KD)
    ffn_gate = [arena[:, 15360 + T * i:15360 + T * (i + 1)] for i in range(4)]
    act = [arena[:, 17920 + T * i:17920 + T * (i + 1)] for i in range(2)]

    def k_major(a, lo, cols):
        return a[:, lo:lo + cols].rearrange("(k p) n -> p k n", p=P)

    w_in, ada = A["w_in"][layer], A["ada_w"][layer]
    blocks = []

    def block_of(name, kind, k, cols, src):
        blocks.append((name, kind, k, cols, src))

    def w_in_block(name, kind, lo, cols=QT * P):
        block_of(name, kind, KD, cols, k_major(w_in, lo, cols))

    for j in range(2):
        w_in_block(("z", j), "parts", IN_Z + QT * P * j)
    for j in range(3):
        w_in_block(("xbc", j), "parts", IN_XBC + QT * P * j)
    w_in_block(("dt",), "parts", IN_DT, 16)
    for j in range(6):
        w_in_block(("hy", j), "whole", IN_HY + QT * P * j)

    def ada_blocks(lo, hi):
        for j in range(lo, hi):
            block_of(("ada", j), "whole", KD, QT * P, k_major(ada, QT * P * j, QT * P))

    ada_blocks(2 * ADA_FIRST, 2 * ADA_FIRST + ADA_HY)
    for j in range(2):
        block_of(("q", j), "q", KD, QT * P, j)
    w_in_block(("kv",), "parts", IN_K)
    ada_blocks(2 * ADA_FIRST + ADA_HY, 24 - ADA_LAST)
    for b in range(3):
        for oq in range(4):
            w_in_block(("gate", oq, b), "parts", IN_G + D * b + QT * P * oq)
            if b == 2:
                block_of(("proj", oq, b), "att", 4, QT * P, oq)
            else:
                block_of(("proj", oq, b), "parts", 4, QT * P,
                         k_major((A["hy_proj"], A["ssm_proj"])[b][layer], QT * P * oq, QT * P))
    for oq in range(4):
        block_of(("out", oq), "parts", KD, QT * P, k_major(A["w_out"][layer], QT * P * oq, QT * P))
    ada_blocks(24 - ADA_LAST, 24)
    for part_at, (f0, nf) in enumerate(FPARTS):
        for j in range(f0 // QT, (f0 + nf) // QT):
            for u in range(2):
                block_of(("up", u, j), "parts", KD, QT * P,
                         k_major(A[("ffn_w_gate", "ffn_w_up")[u]][layer], QT * P * j, QT * P))
        for oq in range(4):
            block_of(("down", part_at, oq), "parts", nf, QT * P,
                     k_major(A["ffn_w_down"][layer][f0 * P:(f0 + nf) * P, :], QT * P * oq, QT * P))
    index = {blk[0]: n for n, blk in enumerate(blocks)}
    split_blocks = [n for n, blk in enumerate(blocks) if blk[1] != "whole"]
    split_index = {blocks[n][0]: m for m, n in enumerate(split_blocks)}

    landed_count, per = [], [0] * RAW
    for n, blk in enumerate(blocks):
        per[n % RAW] += {"q": KD * KV, "att": KV}.get(blk[1], 1)
        landed_count.append(per[n % RAW])

    def raw_view(n):
        _, _, k, cols, _ = blocks[n]
        base = WB * (n % RAW)
        return ring[:, base:base + k * cols].rearrange("p (k n) -> p k n", k=k)

    def landed(eng, n):
        eng.wait_ge(weights_in[n % RAW], 16 * landed_count[n])

    def ada_view(j):
        base = ADA_WB * (j % ADA_RING)
        return ring[:, base:base + KD * 512].rearrange("p (k n) -> p k n", k=KD)

    def part_view(m, low):
        _, _, k, cols, _ = blocks[split_blocks[m]]
        base = WB * (RAW + PARTS * low + m % PARTS)
        return ring_parts[:, base:base + k * cols].rearrange("p (k n) -> p k n", k=k)

    def weights(pe, *name):
        landed(pe, index[name])
        return raw_view(index[name])

    def weight_parts(pe, *name):
        m = split_index[name]
        pe.wait_ge(vector_done, Vc["part", m])
        return part_view(m, 0), part_view(m, 1)

    def split_hi(sc, m):
        if m >= len(split_blocks):
            return
        n = split_blocks[m]
        landed(sc, n)
        sc.wait_ge(tensor_done, Tn["used", split_blocks[m - PARTS]] if m >= PARTS else Tn["ada_used", ADA_FIRST - 1])
        if m == split_index["proj", 0, 0]:
            sc.wait_ge(tensor_done, Tn["modT", 3])
        Sc(sc.copy(part_view(m, 0), raw_view(n)).then_inc(scalar_done, 1), "hi", m)

    def split_lo(dve, m):
        if m >= len(split_blocks):
            return
        n = split_blocks[m]
        dve.wait_ge(scalar_done, Sc["hi", m])
        Vc(dve.tensor_tensor(part_view(m, 1), raw_view(n), part_view(m, 0).bitcast(F32), ALU.subtract)
           .then_inc(vector_done, 1), "part", m)

    uses = []

    def take(pe, *name):
        if len(uses) >= 4:
            engine, old = uses[-4]
            if engine == "V":
                pe.wait_ge(vector_done, Vc[old])
            else:
                pe.wait_ge(scalar_done, Sc[old])
        uses.append((name[0], name[1:]))
        s = (len(uses) - 1) % 4
        Tn.named[("slot",) + name[1:]] = s
        return s

    def w_used(*name):
        Tn.named[("used", index[name])] = Tn.count

    def used(*name):
        return Tn.known.get(("slot",) + name, 0)

    HALVES = ((0, T // 2), (T // 2, T))

    def dense(pe, s, w, o, rhs):
        n = len(rhs)
        for k in range(n):
            for lo, hi in HALVES:
                m = pe.matmul(tokens(s)[:, lo:hi], w[:, k, o * P:(o + 1) * P], rhs[k][:, lo:hi], start=k == 0, stop=k == n - 1)
        return m

    def dense_parts(pe, s, w, o, rhs, cols=P, after=None):
        (w_hi, w_lo), (x_hi, x_lo) = w, rhs
        n = len(x_hi)
        for k in range(n):
            if after:
                after(k)
            oc = slice(o * cols, (o + 1) * cols)
            for i, (a, x) in enumerate(((w_hi, x_hi), (w_hi, x_lo), (w_lo, x_hi))):
                for lo, hi in HALVES:
                    m = pe.matmul(tokens(s)[0:cols, lo:hi], a[:, k, oc], x[k][:, lo:hi],
                                  start=k == 0 and i == 0, stop=k == n - 1 and i == 2)
        return m

    def tile_list(t, n=KD):
        return [t[:, k, :] for k in range(n)]

    hk = tile_list(hT)
    h1 = (tile_list(h_hi), tile_list(h_lo[0]))
    h2 = (tile_list(h_hi), tile_list(h_lo[1]))

    def channel_sum(pe, name):
        pe.wait_ge(pool_done, Gp["sq", name])
        s = take(pe, "S", "ln", name)
        for lo, hi in HALVES:
            m = pe.matmul(tokens(s)[:, lo:hi], K("ones"), sq_of(name, 0)[:, lo:hi], start=True, stop=True)
        Tn(m.then_inc(tensor_done, 1), "sum", name)

    def add_squares(pool, name, n):
        for k in range(1, n):
            pool.wait_ge(scalar_done, Sc["sq", name, k])
            if k > 1:
                pool.wait_ge(pool_done, Gp.count)
            Gp(pool.tensor_tensor(sq_of(name, 0), sq_of(name, 0), sq_of(name, k), ALU.add).then_inc(pool_done, 1),
               "sq", name, k)
        Gp.named[("sq", name)] = Gp.count

    def sq_of(name, k):
        if name == "ssm":
            return squares[k and 1 + k % 2]
        return hT[:, k, :]

    def rstd_of(sc, name, width):
        sc.wait_ge(tensor_done, Tn["sum", name])
        s = used("ln", name)
        Sc(sc.activation(lnvar, tokens(s), ACT.Ln, scale=1.0 / width, bias=K("eps")).then_inc(scalar_done, 1), "ln", name)
        sc.wait_ge(scalar_done, Sc["ln", name])
        Sc(sc.activation(rstd, lnvar, ACT.Exp, scale=-0.5).then_inc(scalar_done, 1), "rstd", name)

    def pre_squares(sc, i, name, after=None):
        for k in range(KD):
            sc.wait_ge(vector_done, Vc["x", 1 - i, k])
            if i == 1 and k == 0:
                sc.wait_ge(tensor_done, Tn["sum", "p1"])
            Sc(sc.activation(hT[:, k, :], xT[:, k, :], ACT.Square).then_inc(scalar_done, 1), "sq", name, k)
            if after:
                after(k)

    def pre_norm(sc, i, name):
        sc.wait_ge(vector_done, Vc["gains", i])
        for k in range(KD):
            sc.wait_ge(vector_done, Vc["xn", name, k])
            for c, (lo, hi) in enumerate(((0, LP), (LP, T))):
                Sc(sc.activation(hT[:, k, lo:hi], hT[:, k, lo:hi], ACT.Identity, scale=scale_pre[:, i, k, c:c + 1],
                                 bias=modT[:, 24 * i + k, c:c + 1]).then_inc(scalar_done, 1), "h", name, k)
            sc.wait_ge(scalar_done, Sc["h", name, k])
            Sc(sc.copy(h_hi[:, k, :], hT[:, k, :]).then_inc(scalar_done, 1), "h_hi", name, k)

    def norm_apply(dve, name):
        dve.wait_ge(scalar_done, Sc["rstd", name])
        for k in range(KD):
            Vc(dve.tensor_tensor(hT[:, k, :], xT[:, k, :], rstd, ALU.mult).then_inc(vector_done, 1), "xn", name, k)

    def normed_low(dve, name):
        for k in range(KD):
            dve.wait_ge(scalar_done, Sc["h_hi", name, k])
            lo = h_lo[0 if name == "n1" else 1]
            Vc(dve.tensor_tensor(lo[:, k, :], hT[:, k, :], h_hi[:, k, :].bitcast(F32), ALU.subtract)
               .then_inc(vector_done, 1), "h_lo", name, k)

    def mixed(sc, i, dst, name):
        for o in range(KD):
            if o % QT == 0 and o < KD - QT:
                split_hi(sc, split_index["out", o // QT] + 1)
            sc.wait_ge(tensor_done, Tn["mix", i, o])
            s = used("mix", i, o)
            Sc(sc.copy(dst[:, o, :], tokens(s)).then_inc(scalar_done, 1))
            Sc(sc.activation(hT[:, o, :], tokens(s), ACT.Square).then_inc(scalar_done, 1), "mix", i, o)
            Sc.named[("sq", name, o)] = Sc.count
        rstd_of(sc, name, D)

    CHAIN = [(0, 0), (0, 1), (1, 0), (4, 1), (2, 0), (3, 1), (3, 0), (2, 1)]
    ADA_AT = [-1, 0, 1, 8, 16]
    assert len(ADA_AT) == 24 - 2 * ADA_FIRST - ADA_HY - ADA_LAST
    SPLIT_AT = ADA_AT[-1] + 1
    UNITS = [(b, t) for b in range(NT) for t in range(4)]

    def key_tiles(b):
        return [0] if b == 0 else [-1] + list(range(max(1, b - 1), min(NT, b + 2)))

    def n_keys(b):
        return len(key_tiles(b))

    with nc.Block() as block:
        @block.tensor
        def _(pe):
            cond = condT[:, :].rearrange("p (c k) -> p k c", c=2)

            def modulation(js):
                for j in js:
                    w = ada_view(j)
                    if j == 0:
                        pe.wait_ge(ada_first_in, 16)
                    else:
                        pe.wait_ge(ada_in[j % ADA_RING], 16 * (j // ADA_RING + 1))
                    s = take(pe, "S", "mrow", j)
                    for k in range(KD):
                        if j == 0 and k == KD // 2:
                            pe.wait_ge(ada_in[0], 16)
                        m = pe.matmul(slot(s)[0:2, 0:512], cond[:, k, :], w[:, k, :], start=k == 0, stop=k == KD - 1)
                    Tn(m.then_inc(tensor_done, 1), "mrow", j)
                    Tn.named[("ada_used", j)] = Tn.count

            def modulation_turned(i, lo, hi):
                pe.wait_ge(scalar_done, Sc["mrow", hi // 4 - 1])
                s = take(pe, "V", "modT", i)
                for j in range(lo, hi):
                    m = pe.transpose(slot(s)[:, 2 * j:2 * j + 2], mrow[:, j * P:(j + 1) * P], K("ident", 0, 2, 2))
                Tn(m.then_inc(tensor_done, 1), "modT", i)

            modulation(range(2))
            channel_sum(pe, "n1")
            modulation(range(2, 4))
            pe.wait_ge(rows_in, 16 * 10)
            s = take(pe, "V", "pcol")
            pe.transpose(slot(s)[:, 0:N_ROWS], prow[0:N_ROWS, :], K("ident", rows=N_ROWS)[:, 0:N_ROWS])
            Tn(pe.transpose(slot(s)[:, 512:560], brow[0:48, :], K("ident", 0, 48, 48)).then_inc(tensor_done, 1), "pcol")
            modulation_turned(0, 0, 16)
            pe.wait_ge(hidden_in, 16 * 4)
            s = take(pe, "V", "bcol")
            Tn(pe.transpose(slot(s)[0:HID, 0:4], hrow, K("ident", 0, 4, 4)).then_inc(tensor_done, 1), "bcol")
            modulation(range(4, ADA_FIRST))
            modulation_turned(1, 16, 4 * ADA_FIRST)

            def hidden(n, lhs, rhs):
                s = take(pe, "V", "arg", n)
                for lo, hi in HALVES:
                    m = pe.matmul(tokens(s)[0:HID, lo:hi], lhs, rhs[:, lo:hi], start=True, stop=True)
                Tn(m.then_inc(tensor_done, 1), "arg", n)

            pe.wait_ge(filt_in, 16 * 4)
            hidden(1, w1sb, feat)

            def h1_tile(k):
                pe.wait_ge(vector_done, Vc["h_lo", "n1", k])

            for o in range(4):
                if o % QT == 0:
                    w = weight_parts(pe, "z", o // QT)
                s = take(pe, "S", "z", o)
                Tn(dense_parts(pe, s, w, o % QT, h1, after=None if o else h1_tile).then_inc(tensor_done, 1), "z", o)
                if o % QT == QT - 1:
                    w_used("z", o // QT)
                if o == 2:
                    pe.wait_ge(scalar_done, Sc["hid", 1])
                    hidden(2, w2sb, hid1)
            for o in range(6):
                if o % QT == 0:
                    w = weight_parts(pe, "xbc", o // QT)
                s = take(pe, "V", "conv", "xbc", o)
                Tn(dense_parts(pe, s, w, o % QT, h1).then_inc(tensor_done, 1), "conv", "xbc", o)
                if o % QT == QT - 1:
                    w_used("xbc", o // QT)
            w = weight_parts(pe, "dt")
            s = take(pe, "S", "dt_row")
            Tn(dense_parts(pe, s, w, 0, h1, cols=16).then_inc(tensor_done, 1), "dt_row")
            w_used("dt")
            s = take(pe, "V", "dt_tok")
            pe.wait_ge(scalar_done, Sc["dt_row"])
            for c in range(NT):
                m = pe.transpose(slot(s)[:, 16 * c:16 * c + 16], dt_row[:, c * P:(c + 1) * P], K("ident", 0, 16, 16))
            Tn(m.then_inc(tensor_done, 1), "dt_tok")
            pe.wait_ge(state_in, 64)
            s = take(pe, "V", "H0")
            for i in range(8):
                m = pe.transpose(slot(s)[:, 64 * i:64 * i + 64], init_rows[:, 128 * i:128 * (i + 1)], K("ident", 0, 64, 64))
            Tn(m.then_inc(tensor_done, 1), "H0")
            pe.wait_ge(scalar_done, Sc["xbc", 5])
            for c in range(NT):
                s = take(pe, "V", "x_tok", c)
                for o in range(5):
                    m = pe.transpose(slot(s)[:, 128 * o:128 * (o + 1)], xbc[:, o, c * P:(c + 1) * P], K("ident"))
                Tn(m.then_inc(tensor_done, 1), "x_tok", c)
            pe.wait_ge(vector_done, Vc["dA"])
            s = take(pe, "S", "decays")
            for r, tri in enumerate(("t_gt_j", "t_lt_j")):
                pe.matmul(slot(s)[:, 40 * r:40 * r + 40].rearrange("p (c h) -> p c h", c=NT), K(tri),
                          dA[:, :, 8 * r:8 * r + 8], start=True, stop=True)
            dAg = dA.rearrange("p c (r g h) -> p c r g h", r=2, g=2)
            for g in range(2):
                for r in range(2):
                    m = pe.matmul(slot(s)[64 * g:64 * g + 64, 512 + 20 * r:532 + 20 * r].rearrange("p (c h) -> p c h", c=NT),
                                  K("ones", 0, 64), dAg[:, :, r, g, :], start=True, stop=True)
            Tn(m.then_inc(tensor_done, 1), "decays")
            def decay_sums(c, r):
                pe.wait_ge(pool_done, Gp["dA_tri", c, r])
                s = take(pe, "S", "seg", c, r)
                for half in range(2):
                    m = pe.matmul(slot(s)[:, 512 * half:512 * half + 512], K(("t_gt_j", "t_lt_j")[r]),
                                  dA_tri[:, r, 512 * half:512 * half + 512], start=True, stop=True)
                Tn(m.then_inc(tensor_done, 1), "seg", c, r)
                if c >= 1:
                    s = take(pe, "S", "acc", c, r)
                    for g in range(2):
                        m = pe.matmul(slot(s)[64 * g:64 * g + 64, 0:512], K("ones", 0, 64),
                                      dA_tri[:, r, 512 * g:512 * g + 512], start=True, stop=True)
                    Tn(m.then_inc(tensor_done, 1), "acc", c, r)

            def scores_of(c):
                s = take(pe, "V", "G", c)
                for g in range(2):
                    m = pe.matmul(slot(s)[:, 512 * g:512 * g + 128], BT[64 * g:64 * g + 64, c * P:(c + 1) * P],
                                  CT[64 * g:64 * g + 64, c * P:(c + 1) * P], start=True, stop=True)
                Tn(m.then_inc(tensor_done, 1), "G", c)

            scores_of(0)
            for r in range(2):
                decay_sums(0, r)
            for i, (c, r) in enumerate(CHAIN):
                pe.wait_ge(vector_done, Vc["xw", c, r])
                s = take(pe, "V", "state", c, r)
                for g in range(2):
                    m = pe.matmul(slot(s)[64 * g:64 * g + 64, 0:256], B_tok[:, c, 64 * g:64 * g + 64],
                                  xw[i % 2][:, 256 * g:256 * g + 256], start=True, stop=True)
                Tn(m.then_inc(tensor_done, 1), "state", c, r)
            s = take(pe, "V", "end_rows")
            for r in range(2):
                for hh in range(4):
                    m = pe.transpose(slot(s)[0:64, 512 * r + 128 * hh:512 * r + 128 * hh + 128],
                                     H_end[:, r, 64 * hh:64 * hh + 64], K("ident"))
            Tn(m.then_inc(tensor_done, 1), "end_rows")

            def outputs(c):
                pe.wait_ge(vector_done, Vc["S", c, 1])
                s = take(pe, "V", "y", c)
                for h in range(HEADS):
                    g, hh, e = h // 4, h % 4, 64 * (h % 2)
                    at = 512 * g + 128 * (hh // 2)
                    dst = slot(s)[e:e + 64, at:at + 128]
                    last = 2 if c == 0 else 4
                    i = 0
                    for r in range(2):
                        i += 1
                        m = pe.matmul(dst, xdt[c % 2][r][:, 64 * h:64 * h + 64], E_seg[c % 2][:, r, 128 * h:128 * h + 128],
                                      start=i == 1, stop=i == last)
                    if c >= 1:
                        for r in range(2):
                            i += 1
                            m = pe.matmul(dst, H[64 * g:64 * g + 64, r, c - 1, 64 * hh:64 * hh + 64],
                                          C_dec[c % 2][64 * g:64 * g + 64, r, 128 * hh:128 * hh + 128], start=False, stop=i == last)
                Tn(m.then_inc(tensor_done, 1), "y", c)

            for c in range(1, NT + 1):
                if c < NT:
                    scores_of(c)
                    for r in range(2):
                        decay_sums(c, r)
                outputs(c - 1)

            def modulation_ffn(j):
                w = weights(pe, "ada", j)
                s = take(pe, "S", "mrow_ffn", j)
                for k in range(KD):
                    m = pe.matmul(slot(s)[0:2, 0:QT * P], cond[:, k, :], w[:, k, :], start=k == 0, stop=k == KD - 1)
                Tn(m.then_inc(tensor_done, 1), "mrow_ffn", j)
                w_used("ada", j)

            def modulation_ffn_turned(i):
                lo, hi, _ = apart[i]
                pe.wait_ge(scalar_done, Sc["mrow_ffn", hi // QT - 1])
                s = take(pe, "V", "modT", i)
                for j in range(lo, hi):
                    m = pe.transpose(slot(s)[:, 2 * j:2 * j + 2], ffn_row(i, j), K("ident", 0, 2, 2))
                Tn(m.then_inc(tensor_done, 1), "modT", i)

            def filter_tile(i, c):
                pe.wait_ge(w3_in, 16 * 2)
                pe.wait_ge(scalar_done, Sc["hid", 2])
                s = take(pe, "V", "filt", i, c)
                for r in range(2):
                    m = pe.matmul(slot(s)[:, 512 * r:512 * r + 512], hid2[:, c * P:(c + 1) * P],
                                  w3[i][:, 512 * r:512 * r + 512], start=True, stop=True)
                Tn(m.then_inc(tensor_done, 1), "filt", i, c)

            def transform(name, i, cos_rhs, sin_rhs, engine, nyquist):
                s = take(pe, engine, name, i, "p")
                pe.matmul(slot(s)[:, 0:512], K("dft_c_p"), cos_rhs[:, 0, :], start=True, stop=True)
                Tn(pe.matmul(slot(s)[:, 512:1024], K("dft_s_p"), sin_rhs[:, 0, :], start=True, stop=True)
                   .then_inc(tensor_done, 1), name, i, "p")
                if nyquist:
                    s = take(pe, engine, name + "n", i, "p")
                    Tn(pe.matmul(slot(s)[0:1, 0:512], K("dft_s_p", 0, 1), cos_rhs[:, 0, :], start=True, stop=True)
                       .then_inc(tensor_done, 1), name + "n", i, "p")
                for a in range(2):
                    for kind, rhs in (("cos", cos_rhs), ("sin", sin_rhs)):
                        s = take(pe, engine, name, i, a, kind)
                        for parity in range(2):
                            for j in range(2):
                                at = LH * j + P * a
                                m = pe.matmul(slot(s)[:, 512 * parity:512 * parity + 512],
                                              K(kind + ("_even", "_odd")[parity], at, at + P),
                                              rhs[:, 1 + 2 * parity + j, :], start=j == 0, stop=j == 1)
                        Tn(m.then_inc(tensor_done, 1), name, i, a, kind)
                    if nyquist and a == 0:
                        s = take(pe, engine, name + "n", i, "mid")
                        for j in range(2):
                            m = pe.matmul(slot(s)[0:1, 0:512], K("sin_even", LH * j, LH * j + 1), cos_rhs[:, 1 + j, :],
                                          start=j == 0, stop=j == 1)
                        Tn(m.then_inc(tensor_done, 1), name + "n", i, "mid")

            INVERSE = (("cos_even", "sin_even_t"), ("cos_odd_t", "sin_odd_t"))

            def product_ready(i):
                pe.wait_ge(pool_done, Gp["Y", i, 1])

            def hy_project(o):
                w = weights(pe, "hy", o // QT)
                s = take(pe, "V", "conv", "hy", o)
                Tn(dense(pe, s, w, o % QT, hk).then_inc(tensor_done, 1), "conv", "hy", o)
                if o % QT == QT - 1:
                    w_used("hy", o // QT)

            def turn(b, o):
                pe.wait_ge(vector_done, Vc["conv4", "hy", 4 * b + o])
                s = take(pe, "S", "turn", b, o)
                raw = conv_raw[o % 2]
                by_parity = raw[:, LP:T].rearrange("p (n two) -> p two n", two=2)
                for c in range(NT):
                    src = raw[:, 0:LP] if c == 0 else by_parity[:, (c - 1) // 2, P * ((c - 1) % 2):P * ((c - 1) % 2) + P]
                    m = pe.transpose(token_tiles(s)[:, c * P:(c + 1) * P], src, K("ident"))
                Tn(m.then_inc(tensor_done, 1), "turn", b, o)

            for n in range(8):
                hy_project(n)
                if n == 0:
                    channel_sum(pe, "ssm")
                else:
                    turn((n - 1) // 4, (n - 1) % 4)
                if 1 <= n <= NT:
                    filter_tile(0, n - 1)
            pe.wait_ge(vector_done, Vc["fsum", 0, 4])
            pe.wait_ge(dft_in, 16)
            transform("K", 0, fsum, fdif, "S", True)
            pe.wait_ge(scalar_done, Sc["turn", 0, 3])
            turn(1, 3)
            transform("U", 0, v_tok, v_tok, "V", False)
            for o in (8, 9):
                hy_project(o)
            for c in range(NT):
                if c == 0:
                    pe.wait_ge(vector_done, Vc["Y", 0, "p"])
                elif c == 1:
                    product_ready(0)
                s = take(pe, "V", "z1", c)
                if c == 0:
                    pe.matmul(slot(s)[:, 0:512], K("dft_c_p"), Yr[:, 0, :], start=True, stop=False)
                    m = pe.matmul(slot(s)[:, 0:512], K("idft_s_p"), Ys[:, 0, :], start=False, stop=True)
                else:
                    parity, j = (c - 1) // 2, (c - 1) % 2
                    for a in range(2):
                        at = LH * a + P * j
                        pe.matmul(slot(s)[:, 0:512], K(INVERSE[parity][0], at, at + P), Yr[:, 1 + 2 * parity + a, :],
                                  start=a == 0, stop=False)
                        m = pe.matmul(slot(s)[:, 0:512], K(INVERSE[parity][1], at, at + P), Ys[:, 1 + 2 * parity + a, :],
                                      start=False, stop=a == 1)
                Tn(m.then_inc(tensor_done, 1), "z1", c)
            hy_project(10)
            for c in range(NT):
                filter_tile(1, c)
            hy_project(11)
            pe.wait_ge(vector_done, Vc["fsum", 1, 4])
            transform("K", 1, fsum, fdif, "S", True)
            transform("U", 1, x1_tok, x1_tok, "V", False)
            for j in range(2 * ADA_FIRST, 2 * ADA_FIRST + ADA_HY):
                modulation_ffn(j)
            product_ready(1)
            for o in range(4):
                s = take(pe, "V", "hyY", o)
                oc = slice(o * P, (o + 1) * P)
                pe.matmul(token_tiles(s)[:, 0:LP], Yr[:, 0, oc], K("dft_c_p"), start=True, stop=False)
                pe.matmul(token_tiles(s)[:, 0:LP], Ys[:, 0, oc], K("idft_s_p"), start=False, stop=True)
                for parity in range(2):
                    dst = token_tiles(s)[:, LP + LH * parity:LP + LH * (parity + 1)]
                    for a in range(2):
                        q = 1 + 2 * parity + a
                        pe.matmul(dst, Yr[:, q, oc], K(INVERSE[parity][0], LH * a, LH * (a + 1)), start=a == 0, stop=False)
                        m = pe.matmul(dst, Ys[:, q, oc], K(INVERSE[parity][1], LH * a, LH * (a + 1)), start=False, stop=a == 1)
                Tn(m.then_inc(tensor_done, 1), "hyY", o)
            modulation_ffn_turned(2)

            def h2_tile(name):
                return lambda k: pe.wait_ge(vector_done, Vc["h_lo", name, k])

            for o in range(4):
                if o % QT == 0:
                    w = weight_parts(pe, "q", o // QT)
                s = take(pe, "S", "q", o)
                Tn(dense_parts(pe, s, w, o % QT, h2, after=None if o else h2_tile("att")).then_inc(tensor_done, 1), "q", o)
                if o % QT == QT - 1:
                    w_used("q", o // QT)
            w = weight_parts(pe, "kv")
            for o, name in enumerate((("q", 4), ("vT",))):
                s = take(pe, "S", *name)
                Tn(dense_parts(pe, s, w, o, h2).then_inc(tensor_done, 1), *name)
            w_used("kv")
            s = take(pe, "S", "v")
            pe.wait_ge(scalar_done, Sc["vT"])
            for c in range(NT):
                m = pe.transpose(token_tiles(s)[:, c * P:(c + 1) * P], vT[:, c * P:(c + 1) * P], K("ident"))
            Tn(m.then_inc(tensor_done, 1), "v")
            for o in range(5):
                s = take(pe, "V", "rot", o)
                pe.wait_ge(scalar_done, Sc["q", o])
                src = (qT[:, o, :] if o < 4 else kT)
                Tn(pe.matmul(slot(s)[:, 0:512], K("rotate"), src[:, LP:T], start=True, stop=True)
                   .then_inc(tensor_done, 1), "rot", o)
            pe.wait_ge(cache_in, 32)
            s = take(pe, "S", "kcT")
            pe.transpose(slot(s)[:, 0:P], kc_rows, K("ident"))
            Tn(pe.transpose(slot(s)[:, 512:640], kT[:, 0:P], K("ident")).then_inc(tensor_done, 1), "kcT")

            def scores(n):
                b, t = UNITS[n]
                s = take(pe, "V", "max", n)
                for g in range(2):
                    q = qT[64 * g:64 * g + 64, t, b * P:(b + 1) * P]
                    if b == 0:
                        m = pe.matmul(slot(s)[:, 512 * g:512 * g + 128], q, kT[64 * g:64 * g + 64, 0:P], start=True, stop=True)
                    else:
                        lo, hi = max(1, b - 1), min(NT, b + 2)
                        pe.matmul(slot(s)[:, 512 * g:512 * g + 128], q, kcT[64 * g:64 * g + 64, :], start=True, stop=True)
                        m = pe.matmul(slot(s)[:, 512 * g + 128:512 * g + 128 + (hi - lo) * P], q,
                                      kT[64 * g:64 * g + 64, lo * P:hi * P], start=True, stop=True)
                Tn(m.then_inc(tensor_done, 1), "scores", n)

            def turn_probs(n):
                b, t = UNITS[n]
                pe.wait_ge(vector_done, Vc["probs", n])
                s = take(pe, "S", "PT", n)
                for g in range(2):
                    for j in range(n_keys(b)):
                        m = pe.transpose(slot(s)[:, 512 * g + 128 * j:512 * g + 128 * (j + 1)],
                                         S_sb[n % 3][:, g, 128 * j:128 * (j + 1)], K("ident"))
                Tn(m.then_inc(tensor_done, 1), "PT", n)

            def values(n):
                b, t = UNITS[n]
                pe.wait_ge(scalar_done, Sc["PT", n])
                s = take(pe, "V", "att", n)
                kt = key_tiles(b)
                for g in range(2):
                    for j, c in enumerate(kt):
                        v = v_ctx if c < 0 else v_att[:, c, :]
                        m = pe.matmul(slot(s)[64 * g:64 * g + 64, 0:128], v[:, 64 * g:64 * g + 64],
                                      PT_sb[n % 3][:, g, 128 * j:128 * (j + 1)], start=j == 0, stop=j == len(kt) - 1)
                Tn(m.then_inc(tensor_done, 1), "att", n)

            if -1 in ADA_AT:
                modulation_ffn(2 * ADA_FIRST + ADA_HY)
            pe.wait_ge(vector_done, Vc["rope", 4])
            pe.wait_ge(scalar_done, Sc["kcT"])
            for n in range(len(UNITS) + 3):
                if n < len(UNITS):
                    scores(n)
                if 2 <= n < len(UNITS) + 2:
                    turn_probs(n - 2)
                if n >= 3:
                    values(n - 3)
                if n in ADA_AT:
                    modulation_ffn(2 * ADA_FIRST + ADA_HY + ADA_AT.index(n))
            modulation_ffn_turned(3)

            for b in range(3):
                for oq in range(4):
                    w = weight_parts(pe, "gate", oq, b)
                    for o in range(QT):
                        s = take(pe, "S", "gate", oq, b, o)
                        Tn(dense_parts(pe, s, w, o, h2).then_inc(tensor_done, 1), "gate", oq, b, o)
                    w_used("gate", oq, b)
                    w = weight_parts(pe, "proj", oq, b)
                    for o in range(QT):
                        s = take(pe, "V", "proj", oq, b, o)
                        Tn(dense_parts(pe, s, w, o, (y_hi[b], tile_list(y_lo[b], 4)),
                                       after=None if oq or o else lambda k: pe.wait_ge(vector_done, Vc["y_lo", b, k]))
                           .then_inc(tensor_done, 1), "proj", oq, b, o)
                    w_used("proj", oq, b)
            for o in range(KD):
                if o % QT == 0:
                    w = weight_parts(pe, "out", o // QT)
                s = take(pe, "S", "mix", 0, o)
                Tn(dense_parts(pe, s, w, o % QT, (m_hi, tile_list(m_lo)),
                               after=None if o else lambda k: pe.wait_ge(vector_done, Vc["m_lo", k]))
                   .then_inc(tensor_done, 1), "mix", 0, o)
                if o % QT == QT - 1:
                    w_used("out", o // QT)
            channel_sum(pe, "p1")
            for j in range(24 - ADA_LAST, 24):
                modulation_ffn(j)
            modulation_ffn_turned(4)
            channel_sum(pe, "n2")

            for i, (f0, nf) in enumerate(FPARTS):
                for j in range(f0 // QT, (f0 + nf) // QT):
                    for u, name in enumerate(("fgate", "fup")):
                        w = weight_parts(pe, "up", u, j)
                        for o in range(QT):
                            s = take(pe, "SV"[u], name, QT * j + o)
                            Tn(dense_parts(pe, s, w, o, h2, after=h2_tile("n2") if u == j == o == 0 else None)
                               .then_inc(tensor_done, 1), name, QT * j + o)
                        w_used("up", u, j)
                for o in range(KD):
                    if o % QT == 0:
                        w = weight_parts(pe, "down", i, o // QT)
                    s = take(pe, "V" if i else "S", "down", i, o)
                    Tn(dense_parts(pe, s, w, o % QT, (tile_list(a_hi, nf), tile_list(a_lo, nf)),
                                   after=None if o else lambda k: pe.wait_ge(vector_done, Vc["a_lo", f0 + k]))
                       .then_inc(tensor_done, 1), "down", i, o)
                    if o % QT == QT - 1:
                        w_used("down", i, o // QT)
            channel_sum(pe, "p2")

        @block.vector
        def _(dve):
            for k in range(KD):
                add_to_residual(dve, Vc, 1, mix2, k)
            norm_apply(dve, "n1")
            dve.wait_ge(tensor_done, Tn["pcol"])
            s = used("pcol")
            Vc(dve.tensor_copy(pcol[:, :], slot(s)[:, 0:N_ROWS]).then_inc(vector_done, 1))
            Vc(dve.tensor_copy(bcol[:, 0:48], slot(s)[:, 512:560]).then_inc(vector_done, 1), "pcol")

            def modulation(i, lo, hi):
                dve.wait_ge(tensor_done, Tn["modT", i])
                dve.wait_ge(vector_done, Vc["pcol"])
                b = bcol[:, lo:hi].unsqueeze(2).broadcast_to([P, hi - lo, 2])
                got = slot(used("modT", i))[:, 2 * lo:2 * hi].rearrange("p (n c) -> p n c", c=2)
                Vc(dve.tensor_tensor(modT[:, lo:hi, :], got, b, ALU.add).then_inc(vector_done, 1), "modT", i)
                dve.wait_ge(vector_done, Vc["modT", i])

            def pre_gain(i):
                pre = row(("mix_pre", "ffn_pre")[i], 0, 8).unsqueeze(2).broadcast_to([P, 8, 2])
                Vc(dve.scalar_tensor_tensor(out=scale_pre[:, i], in0=modT[:, 24 * i + 8:24 * i + 16, :], scalar=1.0, in1=pre,
                                            op0=ALU.add, op1=ALU.mult).then_inc(vector_done, 1), "gains", i)

            modulation(0, 0, 16)
            pre_gain(0)
            dve.wait_ge(tensor_done, Tn["bcol"])
            Vc(dve.tensor_copy(bcol[0:HID, 48:52], slot(used("bcol"))[0:HID, 0:4]).then_inc(vector_done, 1), "bcol")
            normed_low(dve, "n1")
            dve.wait_ge(rowvec_in, 16 * 4)
            for e in range(2):
                half = slice(64 * e, 64 * e + 64)
                Vc(dve.tensor_tensor(dskip[half, :], dskip2[half, e:8:2], dskip2[half, 8 + e:16:2], ALU.add)
                   .then_inc(vector_done, 1), "dskip")
            dve.wait_ge(scalar_done, Sc["exp_a"])
            Vc(dve.tensor_scalar(neg_a[:, :], neg_a[:, :], -1.0, None, ALU.mult).then_inc(vector_done, 1), "neg_a")

            def post_gain(i):
                post = row(("mix_post", "ffn_post")[i], 0, 8).unsqueeze(2).broadcast_to([P, 8, 2])
                Vc(dve.tensor_tensor(gain_post[:, i], modT[:, 24 * i + 16:24 * i + 24, :], post, ALU.mult)
                   .then_inc(vector_done, 1), "gain_post", i)

            modulation(1, 16, 4 * ADA_FIRST)
            post_gain(0)

            def arg(n):
                dve.wait_ge(tensor_done, Tn["arg", n])
                h = (hid1, arg_2)[n - 1]
                b, fr = bcol[0:HID, 48 + 2 * (n - 1):49 + 2 * (n - 1)], bcol[0:HID, 49 + 2 * (n - 1):50 + 2 * (n - 1)]
                Vc(dve.tensor_scalar(h, tokens(used("arg", n))[0:HID, :], b, fr, ALU.add, ALU.mult)
                   .then_inc(vector_done, 1))
                big = 1.5 * 2.0 ** 23
                hi = float(np.float32(6.28125))
                lo = float(np.float32(TWO_PI - hi))
                pi = float(np.nextafter(np.float32(np.pi), np.float32(0)))
                dve.wait_ge(vector_done, Vc.count)
                Vc(dve.tensor_scalar(arg_k, h, float(np.float32(1 / TWO_PI)), big, ALU.mult, ALU.add).then_inc(vector_done, 1))
                dve.wait_ge(vector_done, Vc.count)
                Vc(dve.tensor_scalar(arg_k, arg_k, -big, None, ALU.add).then_inc(vector_done, 1))
                for part_ in (hi, lo):
                    dve.wait_ge(vector_done, Vc.count)
                    Vc(dve.scalar_tensor_tensor(out=h, in0=arg_k, scalar=-part_, in1=h, op0=ALU.mult, op1=ALU.add)
                       .then_inc(vector_done, 1))
                dve.wait_ge(vector_done, Vc.count)
                Vc(dve.tensor_scalar(h, h, pi, -pi, ALU.min, ALU.max).then_inc(vector_done, 1), "arg_in", n)

            split_lo(dve, 0)
            arg(1)
            split_lo(dve, split_index["z", 1])
            split_lo(dve, split_index["xbc", 0])
            arg(2)

            def conv(kind, o, dst, name):
                dve.wait_ge(tensor_done, Tn["conv", kind, o])
                src = tokens(used("conv", kind, o))
                n = {"xbc": 6, "hy": 12}[kind]
                tag = {"xbc": "ssm", "hy": "hy"}[kind]
                w = [row(tag + "_w", n * j + o) for j in range(3)]
                Vc(dve.tensor_scalar(dst, src, w[1], row(tag + "_b", o), ALU.mult, ALU.add).then_inc(vector_done, 1))
                for lo, hi in ((0, LP), (LP, T)):
                    dve.wait_ge(vector_done, Vc.count)
                    Vc(dve.scalar_tensor_tensor(out=dst[:, lo + 1:hi], in0=src[:, lo:hi - 1], scalar=w[0],
                                                in1=dst[:, lo + 1:hi], op0=ALU.mult, op1=ALU.add).then_inc(vector_done, 1))
                    dve.wait_ge(vector_done, Vc.count)
                    Vc(dve.scalar_tensor_tensor(out=dst[:, lo:hi - 1], in0=src[:, lo + 1:hi], scalar=w[2],
                                                in1=dst[:, lo:hi - 1], op0=ALU.mult, op1=ALU.add).then_inc(vector_done, 1))
                Vc.named[("conv", kind, o)] = Vc.named[name] = Vc.count

            for o in range(6):
                if o % QT == 0:
                    split_lo(dve, split_index["xbc", o // QT] + 1)
                conv("xbc", o, xbc[:, o, :], ("conv4", "xbc", o))
            dve.wait_ge(tensor_done, Tn["dt_tok"])
            raw = slot(used("dt_tok"))[:, 0:80].rearrange("p (c m) -> p c m", c=NT)
            v, e, u = sp_a, sp_b, sp_c
            v3 = v.rearrange("p (c m) -> p c m", c=NT)
            Vc(dve.tensor_tensor(v3, raw, dt_bias[:, :].unsqueeze(1).broadcast_to([P, NT, 16]), ALU.add)
               .then_inc(vector_done, 1), "dt_tok")
            dve.wait_ge(vector_done, Vc.count)
            Vc(dve.scalar_tensor_tensor(out=e, in0=v, scalar=-1.0, in1=v, op0=ALU.mult, op1=ALU.min)
               .then_inc(vector_done, 1), "dt_abs")
            dve.wait_ge(scalar_done, Sc["dt_exp"])
            Vc(dve.tensor_scalar(u, e, 1.0, None, ALU.add).then_inc(vector_done, 1), "dt_u")
            dve.wait_ge(vector_done, Vc.count)
            flat = dts.rearrange("p c m -> p (c m)")
            dAf = dA.rearrange("p c m -> p (c m)")
            Vc(dve.scalar_tensor_tensor(out=e, in0=u, scalar=-1.0, in1=e, op0=ALU.add, op1=ALU.subtract)
               .then_inc(vector_done, 1))
            Vc(dve.reciprocal(dAf, u).then_inc(vector_done, 1), "u_inverse")
            dve.wait_ge(vector_done, Vc.count)
            Vc(dve.tensor_tensor(e, e, dAf, ALU.mult).then_inc(vector_done, 1))
            dve.wait_ge(vector_done, Vc.count)
            Vc(dve.scalar_tensor_tensor(out=flat, in0=v, scalar=0.0, in1=e, op0=ALU.max, op1=ALU.subtract)
               .then_inc(vector_done, 1))
            dve.wait_ge(vector_done, Vc.count)
            dve.wait_ge(scalar_done, Sc["dt_ln"])
            Vc(dve.tensor_tensor(flat, flat, u, ALU.add).then_inc(vector_done, 1))
            dve.wait_ge(vector_done, Vc.count)
            Vc(dve.tensor_tensor(dA, dts, neg_a[:, :].unsqueeze(1).broadcast_to([P, NT, 16]), ALU.mult)
               .then_inc(vector_done, 1), "dA")
            dve.wait_ge(tensor_done, Tn["H0"])
            h0 = slot(used("H0"))[:, 0:512].rearrange("p (r n) -> p r n", r=2)
            Vc(dve.tensor_copy(H[:, 0, 0, :], h0[:, 0, :]).then_inc(vector_done, 1))
            Vc(dve.tensor_copy(H[:, 1, 3, :], h0[:, 1, :]).then_inc(vector_done, 1), "H0")
            for c in range(NT):
                dve.wait_ge(tensor_done, Tn["x_tok", c])
                s = used("x_tok", c)
                Vc(dve.tensor_copy(x_tok[:, c, :], slot(s)[:, 0:512]).then_inc(vector_done, 1))
                Vc(dve.tensor_copy(B_tok[:, c, :], slot(s)[:, 512:640]).then_inc(vector_done, 1), "x_tok", c)
            for o in range(4):
                Vc(dve.tensor_scalar(xskip[:, o, :], xskip[:, o, :], dskip[:, o:o + 1], None, ALU.mult)
                   .then_inc(vector_done, 1), "xskip", o)

            def heads(x):
                return x.rearrange("p (h n) -> p h n", h=HEADS)

            def dt_of(c, r):
                return dts[:, c, 8 * r:8 * r + 8].unsqueeze(2).broadcast_to([P, HEADS, HD])

            def masked_scores(c):
                dve.wait_ge(tensor_done, Tn["G", c])
                s = used("G", c)
                for r, tri in enumerate(("t_le_i", "t_ge_i")):
                    for g in range(2):
                        Vc(dve.tensor_tensor(G_tri[c % 2][:, r, g, :], slot(s)[:, 512 * g:512 * g + 128], K(tri), ALU.mult)
                           .then_inc(vector_done, 1), "G", c)
                for r in range(2):
                    if c >= 2:
                        dve.wait_ge(tensor_done, Tn["y", c - 2])
                    Vc(dve.tensor_tensor(heads(xdt[c % 2][r]), heads(x_tok[:, c, :]), dt_of(c, r), ALU.mult)
                       .then_inc(vector_done, 1))

            def decayed_scores(c):
                for r in range(2):
                    dve.wait_ge(scalar_done, Sc["acc" if c else "seg", c, r])
                    if c:
                        cb = CT[:, c * P:(c + 1) * P].unsqueeze(1).broadcast_to([P, 4, P])
                        d = C_dec[c % 2][:, r, :].rearrange("p (h n) -> p h n", h=4)
                        Vc(dve.tensor_tensor(d, d, cb, ALU.mult).then_inc(vector_done, 1))
                    dve.wait_ge(vector_done, Vc["G", c])
                    for g in range(2):
                        ev = E_seg[c % 2][:, r, 512 * g:512 * g + 512].rearrange("p (h n) -> p h n", h=4)
                        Vc(dve.tensor_tensor(ev, ev, G_tri[c % 2][:, r, g, :].unsqueeze(1).broadcast_to([P, 4, P]), ALU.mult)
                           .then_inc(vector_done, 1), "S", c, r)

            dve.wait_ge(scalar_done, Sc["decays"])

            def weighted(i):
                c, r = CHAIN[i]
                xwi = heads(xw[i % 2])
                Vc(dve.tensor_tensor(xwi, heads(x_tok[:, c, :]), dt_of(c, r), ALU.mult).then_inc(vector_done, 1))
                dve.wait_ge(vector_done, Vc.count)
                Vc(dve.tensor_tensor(xwi, xwi, w_end[:, r, c, :].unsqueeze(2).broadcast_to([P, HEADS, HD]), ALU.mult)
                   .then_inc(vector_done, 1), "xw", c, r)

            weighted(0)
            masked_scores(0)
            for i, (c, r) in enumerate(CHAIN):
                if i + 1 < len(CHAIN):
                    weighted(i + 1)
                dve.wait_ge(tensor_done, Tn["state", c, r])
                got = slot(used("state", c, r))[:, 0:256]
                if c == 0:
                    Vc(dve.tensor_copy(H_end[:, r, :], got).then_inc(vector_done, 1), "state", c, r)
                    continue
                to = c + 1 if r == 0 else c - 1
                dec = chunk_decay[:, c, r, :].unsqueeze(2).broadcast_to([P, 4, 64])
                Vc(dve.tensor_tensor(H[:, r, to - 1, :].rearrange("p (h n) -> p h n", h=4),
                                     H[:, r, c - 1, :].rearrange("p (h n) -> p h n", h=4), dec, ALU.mult)
                   .then_inc(vector_done, 1))
                dve.wait_ge(vector_done, Vc.count)
                Vc(dve.tensor_tensor(H[:, r, to - 1, :], H[:, r, to - 1, :], got, ALU.add)
                   .then_inc(vector_done, 1), "state", c, r)
            dve.wait_ge(tensor_done, Tn["end_rows"])
            Vc(dve.tensor_copy(end_rows, slot(used("end_rows"))[0:64, 0:1024]).then_inc(vector_done, 1), "end_rows")
            def outputs(c):
                dve.wait_ge(tensor_done, Tn["y", c])
                yv = xskip.rearrange("p (g o) n -> p g o n", g=2)[:, :, :, c * P:(c + 1) * P]
                got = slot(used("y", c)).rearrange("p (g o n) -> p g o n", g=2, o=4)[:, :, 0:2, :]
                Vc(dve.tensor_tensor(yv, yv, got, ALU.add)
                   .then_inc(vector_done, 1), "y", c)

            decayed_scores(0)
            for c in range(1, NT):
                masked_scores(c)
                decayed_scores(c)
                outputs(c - 1)
            outputs(NT - 1)
            dve.wait_ge(vector_done, Vc.count)
            for o in range(4):
                Vc(dve.tensor_tensor(zg[:, o, :], zg[:, o, :], xskip[:, o, :], ALU.mult).then_inc(vector_done, 1), "yz", o)
            dve.wait_ge(scalar_done, Sc["rstd", "ssm"])
            for o in range(4):
                Vc(dve.scalar_tensor_tensor(out=zg[:, o, :], in0=zg[:, o, :], scalar=row("ssm_norm", o), in1=rstd,
                                            op0=ALU.mult, op1=ALU.mult).then_inc(vector_done, 1), "ssmY", o)

            def filter_tile(i, c):
                dve.wait_ge(tensor_done, Tn["filt", i, c])
                dve.wait_ge(scalar_done, Sc["decay", i, c])
                s = used("filt", i, c)
                hb = hb_tmp[c % 2]
                Vc(dve.tensor_tensor(fsum[:, c, :], fsum[:, c, :], slot(s)[:, 0:512], ALU.mult).then_inc(vector_done, 1))
                Vc(dve.tensor_tensor(hb, hb, slot(s)[:, 512:1024], ALU.mult).then_inc(vector_done, 1), "filt", i, c)
                dve.wait_ge(vector_done, Vc.count)
                if c <= 1:
                    if c == 0:
                        dve.wait_ge(filt_in, 16 * (4 + i))
                    Vc(dve.tensor_tensor(fsum[0:1, c, :], fsum[0:1, c, :], bias_row, ALU.add).then_inc(vector_done, 1))
                    Vc(dve.memset(hb[0:1, :], 0.0).then_inc(vector_done, 1), "bias", i, c)
                    dve.wait_ge(vector_done, Vc.count)
                Vc(dve.tensor_tensor(fdif[:, c, :], fsum[:, c, :], hb, ALU.subtract).then_inc(vector_done, 1))
                dve.wait_ge(vector_done, Vc.count)
                Vc(dve.tensor_tensor(fsum[:, c, :], fsum[:, c, :], hb, ALU.add).then_inc(vector_done, 1), "fsum", i, c)

            def spectrum(i):
                def op(out, a, b, how, *name):
                    Vc(dve.tensor_tensor(out, a, b, how).then_inc(vector_done, 1), *name)

                def complex_product(yr, ys, ur, us, kr, ks, *name):
                    op(yr, ur, kr, ALU.mult)
                    op(prod_a, us, ks, ALU.mult)
                    op(ys, ur, ks, ALU.mult)
                    op(prod_b, us, kr, ALU.mult)
                    dve.wait_ge(vector_done, Vc.count)
                    op(yr, yr, prod_a, ALU.subtract)
                    op(ys, ys, prod_b, ALU.add, *name)
                    dve.wait_ge(vector_done, Vc.count)

                dve.wait_ge(tensor_done, Tn["U", i, "p"])
                dve.wait_ge(scalar_done, Sc["Kn", i, "p"])
                s = used("U", i, "p")
                ur, us = slot(s)[:, 0:512], slot(s)[:, 512:1024]
                complex_product(Yr[:, 0, :], Ys[:, 0, :], ur, us, Kr[:, 0, :], Ks[:, 0, :])
                op(Yr[0:1, 0, :], ur[0:1, :], Kr[0:1, 0, :], ALU.mult)
                op(Ys[0:1, 0, :], us[0:1, :], Ks[0:1, 0, :], ALU.mult, "Y", i, "p")
                Vc.named[("U", i, "p")] = Vc.count
                for a in range(2):
                    dve.wait_ge(tensor_done, Tn["U", i, a, "sin"])
                    dve.wait_ge(scalar_done, Sc["U_odd", i, a])
                    dve.wait_ge(pool_done, Gp["K", i, a])
                    c, sn = slot(used("U", i, a, "cos")), slot(used("U", i, a, "sin"))
                    odd_c, odd_s = U_odd[a]
                    op(U_c, c[:, 0:512], odd_c, ALU.add)
                    op(U_s, sn[:, 0:512], odd_s, ALU.add)
                    dve.wait_ge(vector_done, Vc.count)
                    complex_product(Yr[:, 1 + a, :], Ys[:, 1 + a, :], U_c, U_s, Kr[:, 1 + a, :], Ks[:, 1 + a, :])
                    op(U_c, c[:, 0:512], odd_c, ALU.subtract, "U", i, a, "cos")
                    op(U_s, odd_s, sn[:, 0:512], ALU.subtract, "U", i, a, "sin")
                    dve.wait_ge(vector_done, Vc.count)
                    if a == 0:
                        dve.wait_ge(pool_done, Gp["K", i, 1])
                    else:
                        dve.wait_ge(pool_done, Gp["Y", i, 0])
                    complex_product(T_c, T_s, U_c, U_s, Kr[:, 3 + a, :], Ks[:, 3 + a, :], "Y", i, a)

            for n in range(8):
                if n >= 2:
                    dve.wait_ge(tensor_done, Tn["turn", (n - 2) // 4, (n - 2) % 4])
                conv("hy", n, conv_raw[n % 2], ("conv4", "hy", n))
                if 1 <= n <= NT:
                    filter_tile(0, n - 1)
            spectrum(0)
            for o in range(2):
                conv("hy", 8 + o, x2T[:, o, :], ("conv4", "hy", 8 + o))
            for c in range(NT):
                dve.wait_ge(tensor_done, Tn["z1", c])
                if c == 0:
                    dve.wait_ge(scalar_done, Sc["turn", 1, 3])
                Vc(dve.tensor_tensor(x1_tok[:, c, :], x1_tok[:, c, :], slot(used("z1", c))[:, 0:512], ALU.mult)
                   .then_inc(vector_done, 1), "z1", c)
            conv("hy", 10, x2T[:, 2, :], ("conv4", "hy", 10))
            for c in range(NT):
                filter_tile(1, c)
            conv("hy", 11, x2T[:, 3, :], ("conv4", "hy", 11))
            spectrum(1)
            split_lo(dve, split_index["q", 0])
            dve.wait_ge(vector_done, Vc.count)
            for o in range(4):
                dve.wait_ge(tensor_done, Tn["hyY", o])
                got = token_tiles(used("hyY", o))
                Vc(dve.tensor_tensor(hyY[:, o, 0:LP], x2T[:, o, 0:LP], got[:, 0:LP], ALU.mult).then_inc(vector_done, 1))
                pairs = lambda t: t[:, o, LP:T].rearrange("p (n two) -> p two n", two=2)
                Vc(dve.tensor_tensor(pairs(hyY), pairs(x2T), got[:, LP:T].rearrange("p (two n) -> p two n", two=2), ALU.mult)
                   .then_inc(vector_done, 1), "hyY", o)

            normed_low(dve, "att")
            modulation(2, *apart[2][0:2])
            for m in range(split_index["q", 1], split_index["kv",] + 1):
                split_lo(dve, m)
            for o in range(5):
                x = (qT[:, o, :] if o < 4 else kT)[:, LP:T]
                dve.wait_ge(tensor_done, Tn["rot", o])
                if o >= 2:
                    dve.wait_ge(vector_done, Vc["rope", o - 2])
                Vc(dve.tensor_tensor(rot_tmp[o % 2], slot(used("rot", o))[:, 0:512], K("sin"), ALU.mult)
                   .then_inc(vector_done, 1), "rot", o)
                Vc(dve.tensor_tensor(x, x, K("cos"), ALU.mult).then_inc(vector_done, 1))
                dve.wait_ge(vector_done, Vc.count)
                Vc(dve.tensor_tensor(x, x, rot_tmp[o % 2], ALU.add).then_inc(vector_done, 1), "rope", o)

            def sink_of(n, g):
                return sinks[:, 4 * g + UNITS[n][1]:4 * g + UNITS[n][1] + 1]

            def softmax_max(n):
                b, _ = UNITS[n]
                w = n_keys(b) * P
                mask = K("mask_first") if b == 1 else K("mask")
                dve.wait_ge(tensor_done, Tn["scores", n])
                if n >= 3:
                    dve.wait_ge(tensor_done, Tn["PT", n - 3])
                for g in range(2):
                    Vc(dve.tensor_tensor_reduce(out=S_sb[n % 3][:, g, 0:w], in0=slot(used("max", n))[:, 512 * g:512 * g + w],
                                                in1=mask[:, 0:w], scale=HD ** -0.5, scalar=sink_of(n, g), op0=ALU.add,
                                                op1=ALU.max, accum_out=stat[:, n, g:g + 1]).then_inc(vector_done, 1), "max", n)
                dve.wait_ge(vector_done, Vc.count)
                Vc(dve.tensor_scalar(stat[:, n, 2:4], stat[:, n, 0:2], -1.0, None, ALU.mult).then_inc(vector_done, 1))
                sk = sinks[:, UNITS[n][1]:UNITS[n][1] + 5:4]
                dve.wait_ge(vector_done, Vc.count)
                Vc(dve.tensor_tensor(stat[:, n, 4:6], sk, stat[:, n, 2:4], ALU.add).then_inc(vector_done, 1), "negmax", n)

            def softmax_scale(n):
                b, _ = UNITS[n]
                w = n_keys(b) * P
                dve.wait_ge(scalar_done, Sc["exp", n])
                Vc(dve.tensor_tensor(stat[:, n, 6:8], stat[:, n, 6:8], stat[:, n, 4:6], ALU.add).then_inc(vector_done, 1))
                dve.wait_ge(vector_done, Vc.count)
                Vc(dve.reciprocal(stat[:, n, 8:10], stat[:, n, 6:8]).then_inc(vector_done, 1))
                dve.wait_ge(vector_done, Vc.count)
                for g in range(2):
                    Vc(dve.tensor_scalar(S_sb[n % 3][:, g, 0:w], S_sb[n % 3][:, g, 0:w], stat[:, n, 8 + g:9 + g], None, ALU.mult)
                       .then_inc(vector_done, 1), "probs", n)

            def attended(n):
                b, t = UNITS[n]
                dve.wait_ge(tensor_done, Tn["att", n])
                Vc(dve.tensor_copy(attY[:, t, b * P:(b + 1) * P], slot(used("att", n))[:, 0:P]).then_inc(vector_done, 1), "att", n)

            for n in range(len(UNITS) + 3):
                if n < len(UNITS):
                    softmax_max(n)
                if 1 <= n <= len(UNITS):
                    softmax_scale(n - 1)
                if n >= 3:
                    attended(n - 3)
                if n == SPLIT_AT:
                    split_lo(dve, split_index["gate", 0, 0])
            modulation(3, *apart[3][0:2])

            i = 0
            def merged_low(oq):
                for m in range(QT * oq, QT * (oq + 1)):
                    dve.wait_ge(scalar_done, Sc["m_hi", m])
                    Vc(dve.tensor_tensor(m_lo[:, m, :], merged[:, m, :], m_hi[m].bitcast(F32), ALU.subtract)
                       .then_inc(vector_done, 1), "m_lo", m)

            def branch_low(b):
                for k in range(4):
                    y = (hyY, ssmY, attY)[b][:, k, :]
                    dve.wait_ge(scalar_done, Sc["y_hi", b, k])
                    Vc(dve.tensor_tensor(y_lo[b][:, k, :], y, y_hi[b][k].bitcast(F32), ALU.subtract)
                       .then_inc(vector_done, 1), "y_lo", b, k)

            branch_low(0)
            g = 0
            for b in range(3):
                for oq in range(4):
                    split_lo(dve, split_index["gate", oq, b] + 1)
                    split_lo(dve, split_index["proj", oq, b] + 1)
                    for o in range(QT):
                        m = QT * oq + o
                        dve.wait_ge(tensor_done, Tn["proj", oq, b, o])
                        dve.wait_ge(scalar_done, Sc["gate", oq, b, o])
                        if b == 0:
                            dst = merged[:, m, :]
                        else:
                            dst = part[i % 2]
                            if i >= 2:
                                dve.wait_ge(pool_done, Gp["part", i - 2])
                            i += 1
                        if g == 0:
                            dve.wait_ge(scalar_done, Sc["PT", len(UNITS) - 1])
                            dve.wait_ge(kv_out, 32)
                        Vc(dve.tensor_tensor(dst, sig[g % 3], tokens(used("proj", oq, b, o)), ALU.mult)
                           .then_inc(vector_done, 1), "proj", oq, b, o)
                        g += 1
                    if oq == 0 and b < 2:
                        branch_low(b + 1)
                    if b == 2 and oq:
                        merged_low(oq - 1)
            merged_low(3)
            for oq in range(3):
                split_lo(dve, split_index["out", oq] + 1)
            dve.wait_ge(scalar_done, Sc["rstd", "p1"])
            for k in range(KD):
                if k % 2:
                    dve.wait_ge(pool_done, Gp["normed", k])
                add_to_residual(dve, Vc, 0, mix, k, k % 2 == 1)
            split_lo(dve, split_index["up", 0, 0])
            modulation(4, *apart[4][0:2])
            pre_gain(1)
            post_gain(1)
            norm_apply(dve, "n2")
            normed_low(dve, "n2")

            def act_low(f):
                f0 = max(f0 for f0, _ in FPARTS if f0 <= f)
                dve.wait_ge(scalar_done, Sc["a_hi", f])
                Vc(dve.tensor_tensor(a_lo[:, f - f0, :], act[f % 2], a_hi[:, f - f0, :].bitcast(F32), ALU.subtract)
                   .then_inc(vector_done, 1), "a_lo", f)

            for i, (f0, nf) in enumerate(FPARTS):
                for j in range(f0 // QT, (f0 + nf) // QT):
                    split_lo(dve, split_index["up", 0, j] + 1)
                    split_lo(dve, split_index["up", 1, j] + 1)
                    for f in range(QT * j, QT * (j + 1)):
                        dve.wait_ge(tensor_done, Tn["fup", f])
                        dve.wait_ge(scalar_done, Sc["fgate", f])
                        Vc(dve.tensor_tensor(act[f % 2], ffn_gate[f % 4], tokens(used("fup", f)), ALU.mult)
                           .then_inc(vector_done, 1), "fup", f)
                    for f in range(QT * j, QT * (j + 1)):
                        act_low(f)
                for o in range(KD):
                    if o % QT == 0:
                        split_lo(dve, split_index["down", i, o // QT] + 1)
                    if i:
                        dve.wait_ge(tensor_done, Tn["down", i, o])
                        dve.wait_ge(vector_done, Vc["down", i - 1, o]) if i > 1 else dve.wait_ge(scalar_done, Sc["down", 0, o])
                        Vc(dve.tensor_tensor(mix2[:, o, :], mix2[:, o, :], tokens(used("down", i, o)), ALU.add)
                           .then_inc(vector_done, 1), "down", i, o)

        @block.scalar
        def _(sc):
            def mrows(js):
                for j in js:
                    sc.wait_ge(tensor_done, Tn["mrow", j])
                    Sc(sc.copy(mrow[:, 512 * j:512 * (j + 1)], slot(used("mrow", j))[0:2, 0:512]).then_inc(scalar_done, 1), "mrow", j)

            pre_squares(sc, 0, "n1")
            mrows(range(2))
            rstd_of(sc, "n1", D)
            mrows(range(2, 4))
            pre_norm(sc, 0, "n1")
            mrows(range(4, ADA_FIRST))
            sc.wait_ge(rowvec_in, 16 * 4)
            Sc(sc.activation(neg_a[:, :], neg_a[:, :], ACT.Exp).then_inc(scalar_done, 1), "exp_a")
            split_hi(sc, 0)
            for o in range(4):
                if o % QT == 0:
                    split_hi(sc, split_index["z", o // QT] + 1)
                sc.wait_ge(tensor_done, Tn["z", o])
                Sc(sc.activation(zg[:, o, :], tokens(used("z", o)), ACT.Silu).then_inc(scalar_done, 1), "z", o)
                if o == 0:
                    sc.wait_ge(vector_done, Vc["arg_in", 1])
                    Sc(sc.activation(hid1, hid1, ACT.Sin).then_inc(scalar_done, 1), "hid", 1)
            for o in range(6):
                if o % QT == 0:
                    split_hi(sc, split_index["xbc", o // QT] + 1)
                sc.wait_ge(vector_done, Vc["conv4", "xbc", o])
                Sc(sc.activation(xbc[:, o, :], xbc[:, o, :], ACT.Silu).then_inc(scalar_done, 1), "xbc", o)
            sc.wait_ge(tensor_done, Tn["dt_row"])
            Sc(sc.copy(dt_row, tokens(used("dt_row"))[0:16, :]).then_inc(scalar_done, 1), "dt_row")
            sc.wait_ge(vector_done, Vc["arg_in", 2])
            Sc(sc.activation(hid2, arg_2, ACT.Sin).then_inc(scalar_done, 1), "hid", 2)
            sc.wait_ge(vector_done, Vc["dt_abs"])
            Sc(sc.activation(sp_b, sp_b, ACT.Exp).then_inc(scalar_done, 1), "dt_exp")
            sc.wait_ge(vector_done, Vc["u_inverse"])
            Sc(sc.activation(sp_c, sp_c, ACT.Ln).then_inc(scalar_done, 1), "dt_ln")
            sc.wait_ge(tensor_done, Tn["decays"])
            s = used("decays")
            Sc(sc.activation(w_end.rearrange("p r c h -> p (r c h)"), slot(s)[:, 0:80], ACT.Exp).then_inc(scalar_done, 1))
            Sc(sc.activation(chunk_decay.rearrange("p c r h -> p r c h"),
                             slot(s)[:, 512:552].rearrange("p (r c h) -> p r c h", r=2, c=NT), ACT.Exp)
               .then_inc(scalar_done, 1), "decays")
            for c in range(NT):
                for r in range(2):
                    sc.wait_ge(tensor_done, Tn["seg", c, r])
                    if c >= 2:
                        sc.wait_ge(tensor_done, Tn["y", c - 2])
                    Sc(sc.activation(E_seg[c % 2][:, r, :], slot(used("seg", c, r)), ACT.Exp).then_inc(scalar_done, 1), "seg", c, r)
                    if c == 2 and r == 0:
                        sc.wait_ge(state_out, 64)
                    if c:
                        sc.wait_ge(tensor_done, Tn["acc", c, r])
                        Sc(sc.activation(E_acc[c % 2][:, r, :], slot(used("acc", c, r))[:, 0:512], ACT.Exp)
                           .then_inc(scalar_done, 1), "acc", c, r)
            for o in range(4):
                sc.wait_ge(vector_done, Vc["yz", o])
                if o == 3:
                    sc.wait_ge(pool_done, Gp["sq", "ssm", 1])
                Sc(sc.activation(sq_of("ssm", o), zg[:, o, :], ACT.Square).then_inc(scalar_done, 1), "sq", "ssm", o)
            rstd_of(sc, "ssm", 512)

            def decays(i, c):
                if c == 0:
                    sc.wait_ge(decay_in, 16 * 4)
                if c >= 2:
                    sc.wait_ge(vector_done, Vc["fsum", i, c - 2])
                Sc(sc.activation(fsum[:, c, :], decay[i][:, 0, :], ACT.Exp, scale=K("neg_t", c, c + 1)).then_inc(scalar_done, 1))
                Sc(sc.activation(hb_tmp[c % 2], decay[i][:, 1, :], ACT.Exp, scale=K("neg_t", c, c + 1))
                   .then_inc(scalar_done, 1), "decay", i, c)

            def filter_spectrum(i):
                def weigh(dst, src, w, *name):
                    Sc(sc.activation(dst, src, ACT.Identity, scale=w).then_inc(scalar_done, 1), *name)

                sc.wait_ge(tensor_done, Tn["K", i, "p"])
                s = used("K", i, "p")
                weigh(Kr[:, 0, :], slot(s)[:, 0:512], K("spec_w", 0, 1))
                weigh(Ks[:, 0, :], slot(s)[:, 512:1024], K("spec_w", 0, 1), "K", i, "p")
                sc.wait_ge(tensor_done, Tn["Kn", i, "p"])
                sc.wait_ge(scalar_done, Sc["K", i, "p"])
                weigh(Ks[0:1, 0, :], slot(used("Kn", i, "p"))[0:1, 0:512], 0.5 / LP, "Kn", i, "p")
                for a in range(2):
                    if a:
                        sc.wait_ge(pool_done, Gp["K", i, 0])
                    for dst, odd, kind, col in ((Kr, T_c, "cos", 1), (Ks, T_s, "sin", 2)):
                        w = K("spec_w", col, col + 1) if a == 0 else 1.0 / LS
                        sc.wait_ge(tensor_done, Tn["K", i, a, kind])
                        s = used("K", i, a, kind)
                        if a == 0 and kind == "sin":
                            weigh(K_mid[1], slot(s)[0:1, 512:1024], 1.0 / LS)
                        weigh(dst[:, 1 + a, :], slot(s)[:, 0:512], w)
                        weigh(odd, slot(s)[:, 512:1024], w, "K", i, a, kind)
                    if a == 0:
                        sc.wait_ge(tensor_done, Tn["Kn", i, "mid"])
                        weigh(K_mid[0], slot(used("Kn", i, "mid"))[0:1, 0:512], 1.0 / LS, "Kn", i, "mid")

            def odd_sums(i):
                for a in range(2):
                    for kind, dst in zip(("cos", "sin"), U_odd[a]):
                        sc.wait_ge(tensor_done, Tn["U", i, a, kind])
                        if a == 0 and kind == "sin":
                            Sc(sc.copy(U_mid, slot(used("U", i, a, kind))[0:1, 0:512]).then_inc(scalar_done, 1))
                        Sc(sc.copy(dst, slot(used("U", i, a, kind))[:, 512:1024]).then_inc(scalar_done, 1), "U_odd", i, a)

            sc.wait_ge(vector_done, Vc["ssmY", 3])
            for b in range(2):
                for o in range(4):
                    if 4 * b + o < NT:
                        decays(0, 4 * b + o)
                    if (b, o) == (1, 3):
                        filter_spectrum(0)
                    sc.wait_ge(tensor_done, Tn["turn", b, o])
                    dst = (v_tok, x1_tok)[b][:, :, o * P:(o + 1) * P]
                    Sc(sc.copy(dst, token_tiles(used("turn", b, o)).rearrange("p (c n) -> p c n", c=NT)).then_inc(scalar_done, 1), "turn", b, o)
            odd_sums(0)
            sc.wait_ge(tensor_done, Tn["z1", NT - 1])
            for c in range(NT):
                decays(1, c)
            sc.wait_ge(tensor_done, Tn["filt", 1, NT - 1])
            filter_spectrum(1)
            odd_sums(1)
            def mrow_of_ffn(i, j):
                sc.wait_ge(tensor_done, Tn["mrow_ffn", j])
                Sc(sc.copy(ffn_row(i, QT * j, QT), slot(used("mrow_ffn", j))[0:2, 0:QT * P])
                   .then_inc(scalar_done, 1), "mrow_ffn", j)

            for j in range(2 * ADA_FIRST, 2 * ADA_FIRST + ADA_HY):
                mrow_of_ffn(2, j)
            sc.wait_ge(pool_done, Gp["Y_mid", 1])
            split_hi(sc, split_index["q", 0])

            sc.wait_ge(tensor_done, Tn["hyY", 3])
            for k in range(KD):
                Sc(sc.copy(h_hi[:, k, :], hT[:, k, :]).then_inc(scalar_done, 1), "h_hi", "att", k)
            for o in range(5):
                if o in (0, QT):
                    split_hi(sc, split_index["q", o // QT] + 1)
                sc.wait_ge(tensor_done, Tn["q", o])
                Sc(sc.copy(qT[:, o, :] if o < 4 else kT, tokens(used("q", o))).then_inc(scalar_done, 1), "q", o)
            sc.wait_ge(tensor_done, Tn["vT"])
            Sc(sc.copy(vT, tokens(used("vT"))).then_inc(scalar_done, 1), "vT")
            sc.wait_ge(tensor_done, Tn["v"])
            Sc(sc.copy(v_att.rearrange("p c n -> p (c n)"), token_tiles(used("v"))).then_inc(scalar_done, 1), "v")
            sc.wait_ge(tensor_done, Tn["kcT"])
            s = used("kcT")
            Sc(sc.copy(k_rows, slot(s)[:, 512:640]).then_inc(scalar_done, 1), "k_rows")
            Sc(sc.copy(kcT, slot(s)[:, 0:P]).then_inc(scalar_done, 1), "kcT")

            def exps(n):
                b, _ = UNITS[n]
                w = n_keys(b) * P
                sc.wait_ge(vector_done, Vc["negmax", n])
                for g in range(2):
                    Sc(sc.activation(S_sb[n % 3][:, g, 0:w], S_sb[n % 3][:, g, 0:w], ACT.Exp, bias=stat[:, n, 2 + g:3 + g],
                                     accum_out=stat[:, n, 6 + g:7 + g]).then_inc(scalar_done, 1))
                Sc(sc.activation(stat[:, n, 4:6], stat[:, n, 4:6], ACT.Exp).then_inc(scalar_done, 1), "exp", n)

            def probs_turned(n):
                b, _ = UNITS[n]
                w = n_keys(b) * P
                sc.wait_ge(tensor_done, Tn["PT", n])
                if n >= 3:
                    sc.wait_ge(tensor_done, Tn["att", n - 3])
                src = slot(used("PT", n)).rearrange("p (g n) -> p g n", g=2)
                Sc(sc.copy(PT_sb[n % 3][:, :, 0:w], src[:, :, 0:w]).then_inc(scalar_done, 1), "PT", n)

            if -1 in ADA_AT:
                mrow_of_ffn(3, 2 * ADA_FIRST + ADA_HY)
            for n in range(len(UNITS) + 2):
                if n < len(UNITS):
                    exps(n)
                if n >= 2:
                    probs_turned(n - 2)
                if n in ADA_AT:
                    mrow_of_ffn(3, 2 * ADA_FIRST + ADA_HY + ADA_AT.index(n))
                if n == SPLIT_AT:
                    split_hi(sc, split_index["gate", 0, 0])

            def merged_high(oq):
                for m in range(QT * oq, QT * (oq + 1)):
                    sc.wait_ge(pool_done, Gp["merged", m, 2])
                    Sc(sc.copy(m_hi[m], merged[:, m, :]).then_inc(scalar_done, 1), "m_hi", m)

            def branch_high(b):
                if b == 0:
                    sc.wait_ge(vector_done, Vc["probs", len(UNITS) - 1])
                    sc.wait_ge(tensor_done, Tn["att", len(UNITS) - 1])
                if b == 2:
                    sc.wait_ge(tensor_done, Tn["proj", 3, 0, 1])
                    sc.wait_ge(vector_done, Vc["att", len(UNITS) - 1])
                for k in range(4):
                    Sc(sc.copy(y_hi[b][k], (hyY, ssmY, attY)[b][:, k, :]).then_inc(scalar_done, 1), "y_hi", b, k)

            branch_high(0)
            order = [(oq, b, o) for b in range(3) for oq in range(4) for o in range(QT)]
            for g, (oq, b, o) in enumerate(order):
                if o == 0:
                    split_hi(sc, split_index["gate", oq, b] + 1)
                sc.wait_ge(tensor_done, Tn["gate", oq, b, o])
                if g >= 3:
                    sc.wait_ge(vector_done, Vc[("proj",) + order[g - 3]])
                Sc(sc.activation(sig[g % 3], tokens(used("gate", oq, b, o)), ACT.Sigmoid)
                   .then_inc(scalar_done, 1), "gate", oq, b, o)
                if o == QT - 1:
                    split_hi(sc, split_index["proj", oq, b] + 1)
                    if oq == 0 and b < 2:
                        branch_high(b + 1)
                    if b == 2 and oq:
                        merged_high(oq - 1)
            merged_high(3)
            mixed(sc, 0, mix, "p1")

            def last_mrows(k):
                for j in range(ADA_LAST):
                    if k == min(KD - 1, 2 * j + 1):
                        mrow_of_ffn(4, 24 - ADA_LAST + j)

            pre_squares(sc, 1, "n2", last_mrows)
            split_hi(sc, split_index["up", 0, 0])
            rstd_of(sc, "n2", D)
            pre_norm(sc, 1, "n2")
            for i, (f0, nf) in enumerate(FPARTS):
                for j in range(f0 // QT, (f0 + nf) // QT):
                    split_hi(sc, split_index["up", 0, j] + 1)
                    for f in range(QT * j, QT * (j + 1)):
                        sc.wait_ge(tensor_done, Tn["fgate", f])
                        if f >= 4:
                            sc.wait_ge(vector_done, Vc["fup", f - 4])
                        Sc(sc.activation(ffn_gate[f % 4], tokens(used("fgate", f)), ACT.Silu)
                           .then_inc(scalar_done, 1), "fgate", f)
                    split_hi(sc, split_index["up", 1, j] + 1)
                    for f in range(QT * j, QT * (j + 1)):
                        sc.wait_ge(vector_done, Vc["fup", f])
                        Sc(sc.copy(a_hi[:, f - f0, :], act[f % 2]).then_inc(scalar_done, 1), "a_hi", f)
                for o in range(KD):
                    if o % QT == 0:
                        split_hi(sc, split_index["down", i, o // QT] + 1)
                    if i == 0:
                        sc.wait_ge(tensor_done, Tn["down", i, o])
                        Sc(sc.copy(mix2[:, o, :], tokens(used("down", i, o))).then_inc(scalar_done, 1), "down", i, o)
                    elif i == len(FPARTS) - 1:
                        sc.wait_ge(vector_done, Vc["down", i, o])
                        Sc(sc.activation(hT[:, o, :], mix2[:, o, :], ACT.Square).then_inc(scalar_done, 1), "sq", "p2", o)
            rstd_of(sc, "p2", D)

        @block.gpsimd
        def _(pool):
            add_squares(pool, "n1", KD)
            pool.wait_ge(vector_done, Vc["dA"])
            for c in range(NT):
                for r in range(2):
                    if c >= 1:
                        pool.wait_ge(tensor_done, Tn["acc", c - 1, r] if c > 1 else Tn["seg", 0, r])
                    tri = K(("t_le_i", "t_ge_i")[r]).unsqueeze(1).broadcast_to([P, HEADS, P])
                    d = dA[:, c, 8 * r:8 * r + 8].unsqueeze(2).broadcast_to([P, HEADS, P])
                    Gp(pool.tensor_tensor(dA_tri[:, r, :].rearrange("p (h n) -> p h n", h=HEADS), tri, d, ALU.mult)
                       .then_inc(pool_done, 1), "dA_tri", c, r)
            add_squares(pool, "ssm", 4)

            def mirrored(even, odd, mirror, sign):
                a, b = (even, odd) if sign > 0 else (odd, even)
                Gp(pool.tensor_tensor(mirror, a, b, ALU.subtract).then_inc(pool_done, 1))
                pool.wait_ge(pool_done, Gp.count)
                Gp(pool.tensor_tensor(even, even, odd, ALU.add).then_inc(pool_done, 1))

            for i in range(2):
                for a in range(2):
                    pool.wait_ge(scalar_done, Sc["K", i, a, "sin"])
                    mirrored(Kr[:, 1 + a, :], T_c, Kr[:, 3 + a, :], 1)
                    mirrored(Ks[:, 1 + a, :], T_s, Ks[:, 3 + a, :], -1)
                    Gp.named[("K", i, a)] = Gp.count
                def op(out, a, b, how):
                    Gp(pool.tensor_tensor(out, a, b, how).then_inc(pool_done, 1), "Y_mid", i)

                for a in range(2):
                    pool.wait_ge(vector_done, Vc["Y", i, a])
                    mirrored(Yr[:, 1 + a, :], T_c, Yr[:, 3 + a, :], 1)
                    Gp(pool.tensor_tensor(Ys[:, 3 + a, :], Ys[:, 1 + a, :], T_s, ALU.add).then_inc(pool_done, 1))
                    pool.wait_ge(pool_done, Gp.count)
                    Gp(pool.tensor_tensor(Ys[:, 1 + a, :], Ys[:, 1 + a, :], T_s, ALU.subtract).then_inc(pool_done, 1), "Y", i, a)
                    if a == 0:
                        pool.wait_ge(scalar_done, Sc["Kn", i, "mid"])
                        pool.wait_ge(scalar_done, Sc["U_odd", i, 0])
                        mid = U_mid, U_odd[0][1][0:1, :]
                        op(mid_a, mid[0], K_mid[0], ALU.mult)
                        op(mid_b, mid[1], K_mid[1], ALU.mult)
                        pool.wait_ge(pool_done, Gp.count)
                        op(Ys[0:1, 1, :], mid_a, mid_b, ALU.subtract)
                        pool.wait_ge(pool_done, Gp.count)
                        op(mid_a, mid[0], K_mid[1], ALU.mult)
                        op(mid_b, mid[1], K_mid[0], ALU.mult)
                        pool.wait_ge(pool_done, Gp.count)
                        op(Ys[0:1, 3, :], mid_a, mid_b, ALU.add)
            i = 0
            for b in (1, 2):
                for oq in range(4):
                    for o in range(QT):
                        m = QT * oq + o
                        pool.wait_ge(vector_done, Vc["proj", oq, b, o])
                        if b == 2:
                            pool.wait_ge(pool_done, Gp["merged", m, 1])
                        Gp(pool.tensor_tensor(merged[:, m, :], merged[:, m, :], part[i % 2], ALU.add).then_inc(pool_done, 1), "part", i)
                        Gp.named[("merged", m, b)] = Gp.count
                        i += 1
            add_squares(pool, "p1", KD)
            pool.wait_ge(scalar_done, Sc["rstd", "p1"])
            for k in range(1, KD, 2):
                Gp(pool.tensor_tensor(mix[:, k, :], mix[:, k, :], rstd, ALU.mult).then_inc(pool_done, 1), "normed", k)
            for name in ("n2", "p2"):
                add_squares(pool, name, KD)

        @block.sync
        def _(sp):
            l = layer

            def ada_load(j):
                if j >= ADA_RING:
                    sp.wait_ge(tensor_done, Tn["ada_used", j - ADA_RING])
                view, src = ada_view(j), k_major(ada, 512 * j, 512)
                if j == 0:
                    sp.dma_start(view[:, 0:KD // 2, :], src[:, 0:KD // 2, :]).then_inc(ada_first_in, 16)
                    view, src = view[:, KD // 2:, :], src[:, KD // 2:, :]
                sp.dma_start(view, src).then_inc(ada_in[j % ADA_RING], 16)

            for j in range(2):
                ada_load(j)
            for name, src in (("mix_pre", "norm_mix_pre"), ("mix_post", "norm_mix_post"), ("ffn_pre", "norm_ffn_pre"),
                              ("ffn_post", "norm_ffn_post"), ("hy_b", "hy_conv_b"), ("ssm_b", "ssm_conv_b"), ("ssm_norm", "ssm_norm")):
                at, w = ROWS[name]
                sp.dma_start(prow[at:at + w, :], A[src][l].rearrange("(k p) -> k p", p=P)).then_inc(rows_in, 16)
            for name, src in (("hy_w", "hy_conv_w"), ("ssm_w", "ssm_conv_w")):
                at, w = ROWS[name]
                sp.dma_start(prow[at:at + w, :], A[src][l].rearrange("j (k p) -> (j k) p", p=P)).then_inc(rows_in, 16)
            sp.dma_start(brow[0:48, :], A["ada_b"][l].rearrange("(k p) -> k p", p=P)).then_inc(rows_in, 16)
            for j, src in enumerate(("hy_b1", "hy_freq1", "hy_b2", "hy_freq2")):
                sp.dma_start(hrow[j:j + 1, :], A[src][l].unsqueeze(0)).then_inc(hidden_in, 16)
            sp.dma_start(dt_bias[:, :], A["ssm_dt_bias"][l].rearrange("r h -> (r h)").partition_broadcast(P)).then_inc(rowvec_in, 16)
            sp.dma_start(neg_a[:, :], A["ssm_a_log"][l].rearrange("r h -> (r h)").partition_broadcast(P)).then_inc(rowvec_in, 16)
            sp.dma_start(sinks[:, :], A["attn_sink"][l].partition_broadcast(P)).then_inc(rowvec_in, 16)
            sp.dma_start(dskip2[:, :], A["ssm_d"][l].rearrange("r h -> (r h)").partition_broadcast(P)).then_inc(rowvec_in, 16)
            for r in range(2):
                for g in range(2):
                    sp.dma_start(init_rows[:, 512 * r:512 * r + 512].rearrange("p (h g n) -> p h g n", h=4, g=2)[:, :, g, :],
                                   A["state_ssm"][0, l, r, 4 * g:4 * g + 4].rearrange("h p n -> p h n")).then_inc(state_in, 16)
            sp.dma_start(w1sb, A["hy_w1"][l]).then_inc(filt_in, 16)
            sp.dma_start(w2sb, A["hy_w2"][l]).then_inc(filt_in, 16)
            sp.dma_start(feat, A["feat"]).then_inc(filt_in, 16)
            sp.dma_start(bias_row, A["hy_bias"][l][0:1, :]).then_inc(filt_in, 16)

            def filter_loads(i):
                sp.dma_start(w3[i], A["hy_w3"][l][:, 1024 * i:1024 * (i + 1)]).then_inc(w3_in, 16)
                for r in range(2):
                    src = A["hy_decay"][l][1024 * i + 512 * r:1024 * i + 512 * r + 512]
                    sp.dma_start(decay[i][:, r, :], src.partition_broadcast(P)).then_inc(decay_in, 16)

            def beside(name):
                if name == ("hy", 0):
                    sp.wait_ge(tensor_done, Tn["dt_row"])
                    filter_loads(0)
                    filter_loads(1)
                    sp.dma_start(arena[:, DFT_AT:DFT_AT + N_DFT], A["consts"][:, N_CONST:N_CONST + N_DFT]).then_inc(dft_in, 16)
                elif name == ("hy", 2):
                    sp.wait_ge(vector_done, Vc["end_rows"])
                    for r in range(2):
                        for g in range(2):
                            sp.dma_start(O["new_ssm"][0, l, r, 4 * g:4 * g + 4].rearrange("h p n -> p h n"),
                                         end_rows[:, 512 * r:512 * r + 512].rearrange("p (h g n) -> p h g n", h=4, g=2)[:, :, g, :]
                                         ).then_inc(state_out, 16)
                elif name == ("hy", 4):
                    sp.wait_ge(vector_done, Vc["bias", 0, 1])
                    sp.dma_start(bias_row, A["hy_bias"][l][1:2, :]).then_inc(filt_in, 16)
                elif name == ("kv",):
                    sp.wait_ge(tensor_done, Tn["hyY", 3])
                    sp.dma_start(kc_rows, A["cache_k"][0, l].rearrange("s g n -> s (g n)")).then_inc(cache_in, 16)
                    sp.dma_start(v_ctx, A["cache_v"][0, l].rearrange("s g n -> s (g n)")).then_inc(cache_in, 16)
                elif name == ("proj", 0, 0):
                    sp.wait_ge(scalar_done, Sc["k_rows"])
                    sp.dma_start(O["new_k"][0, l].rearrange("s g n -> s (g n)"), k_rows).then_inc(kv_out, 16)
                    sp.dma_start(O["new_v"][0, l].rearrange("s g n -> s (g n)"), v_att[:, 0, :]).then_inc(kv_out, 16)

            for j in range(2, ADA_FIRST):
                ada_load(j)
            for n, (name, kind, k, cols, src) in enumerate(blocks):
                beside(name)
                if n < RAW:
                    sp.wait_ge(tensor_done, Tn["ada_used", (ADA_FIRST - 1) // ADA_RING * ADA_RING])
                elif n - RAW in split_blocks:
                    sp.wait_ge(vector_done, Vc["part", split_blocks.index(n - RAW)])
                else:
                    sp.wait_ge(tensor_done, Tn["used", n - RAW])
                view, arrived = raw_view(n), weights_in[n % RAW]
                if kind == "q":
                    for g in range(KV):
                        for kk in range(KD):
                            at = IN_Q + 256 * g + P * src
                            sp.dma_start(view[:, kk, :].rearrange("p (t g n) -> p t g n", t=QT, g=KV)[:, :, g, :],
                                         w_in[kk * P:(kk + 1) * P, at:at + P].rearrange("p (t n) -> p t n", t=QT)
                                         ).then_inc(arrived, 16)
                elif kind == "att":
                    for g in range(KV):
                        sp.dma_start(view[64 * g:64 * g + 64, :, :],
                                     A["attn_proj"][l][256 * g:256 * g + 256, QT * P * src:QT * P * (src + 1)]
                                     .rearrange("(t p) n -> p t n", p=HD)).then_inc(arrived, 16)
                else:
                    sp.dma_start(view, src).then_inc(arrived, 16)
            sp.wait_ge(state_out, 64)
            sp.wait_ge(kv_out, 32)

    return {"T": Tn.named, "V": Vc.named, "S": Sc.named, "G": Gp.named}


INPUTS = ["x_prompt", "x_sample", "c", "cache_k", "cache_v", "state_ssm", "c_ctx", "ada_w", "ada_b", "norm_mix_pre",
          "norm_mix_post", "norm_ffn_pre", "norm_ffn_post", "w_in", "hy_conv_w", "hy_conv_b", "hy_w1", "hy_b1", "hy_freq1",
          "hy_w2", "hy_b2", "hy_freq2", "hy_w3", "hy_decay", "hy_bias", "ssm_conv_w", "ssm_conv_b", "ssm_a_log",
          "ssm_dt_bias", "ssm_d", "ssm_norm", "attn_sink", "hy_proj", "ssm_proj", "attn_proj", "w_out", "ffn_w_gate",
          "ffn_w_up", "ffn_w_down"]
OUTPUTS = [("y_prompt", (1, LP, D)), ("y_sample", (1, LS, D)), ("new_k", (1, DEPTH, LP, KV, HD)),
           ("new_v", (1, DEPTH, LP, KV, HD)), ("new_ssm", (1, DEPTH, 2, HEADS, HD, 64))]


def kernel(**inputs):
    import concourse.bacc as bacc
    from concourse.bass_utils import run_bass_kernel_spmd as run

    arrays = {f"in_{n}_dram": np.ascontiguousarray(inputs[n]) for n in INPUTS}
    arrays["in_consts_dram"] = constant_tables()
    arrays["in_feat_dram"] = filter_features()

    def program(known):
        nc = bacc.Bacc("TRN2", target_bir_lowering=False, num_devices=1)
        A = {n: nc.dram_tensor(f"in_{n}_dram", arrays[f"in_{n}_dram"].shape, F32, kind="ExternalInput").ap()
             for n in INPUTS + ["consts", "feat"]}
        O = {n: nc.dram_tensor(f"out_{n}_dram", shape, F32, kind="ExternalOutput").ap() for n, shape in OUTPUTS}
        return nc, build(nc, A, O, known)

    _, steps = program({})
    nc, _ = program(steps)
    r = run(nc, [arrays], core_ids=[0])
    return tuple(r.results[0][f"out_{n}_dram"] for n, _ in OUTPUTS)
```
